# Optimizing a Trainium2 kernel written in Bass

```python
import math
import jax, jax.numpy as jnp
from jax import lax
import numpy as np

D_MODEL = 1024
BATCH = 1
SEQ = 512
DEPTH = 1
DEC_BATCH = 1
DEC_SEQ = 256
PAST_LEN = 128

MLA_HEADS = 8
MLA_NOPE_DIM = 64
MLA_ROPE_DIM = 32
MLA_V_DIM = 64
Q_LORA_RANK = 256
KV_LORA_RANK = 128
ROPE_THETA = 10000.0
DIFF_HEADS = 4
DIFF_HEAD_DIM = 64
MLA_WIDTH = MLA_HEADS * MLA_V_DIM
DIFF_WIDTH = DIFF_HEADS * 2 * DIFF_HEAD_DIM
MIX_WIDTH = MLA_WIDTH + DIFF_WIDTH
IN_SIZES = (Q_LORA_RANK, KV_LORA_RANK, MLA_ROPE_DIM, DIFF_WIDTH, DIFF_WIDTH, DIFF_WIDTH)
IN_WIDTH = Q_LORA_RANK + KV_LORA_RANK + MLA_ROPE_DIM + 3 * DIFF_WIDTH
N_EXPERTS = 16
N_GROUPS = 4
EXPERTS_PER_GROUP = N_EXPERTS // N_GROUPS
TOP_K = 2
D_FF_EXPERT = 512
Q_BLOCK = 128
LN_EPS = 1e-5
RMS_EPS = 1e-6
ALPHA = (2 * DEPTH) ** 0.25
BETA = (8 * DEPTH) ** -0.25

kernel_name = "hybrid_mla_diffattn_grouped_moe_encoder"

def layer_norm(x, g, b):
    xf = x.astype(jnp.float32)
    mu = jnp.mean(xf, axis=-1, keepdims=True)
    var = jnp.mean(jnp.square(xf - mu), axis=-1, keepdims=True)
    return ((xf - mu) * lax.rsqrt(var + LN_EPS) * g + b).astype(x.dtype)

def rms_norm(x, g, eps):
    xf = x.astype(jnp.float32)
    return (xf * lax.rsqrt(jnp.mean(jnp.square(xf), axis=-1, keepdims=True) + eps) * g).astype(x.dtype)

def rope_tables(seq):
    inv = 1.0 / (ROPE_THETA ** (jnp.arange(0, MLA_ROPE_DIM, 2, dtype=jnp.float32) / MLA_ROPE_DIM))
    ang = jnp.arange(seq, dtype=jnp.float32)[:, None] * inv[None, :]
    return jnp.cos(ang), jnp.sin(ang)

def apply_rope(x, cos, sin):
    x1, x2 = jnp.split(x.astype(jnp.float32), 2, axis=-1)
    return jnp.concatenate([x1 * cos - x2 * sin, x2 * cos + x1 * sin], axis=-1).astype(x.dtype)

def to_blocks(x):
    b, s = x.shape[0], x.shape[1]
    x = x.reshape((b, s // Q_BLOCK, Q_BLOCK) + x.shape[2:])
    return jnp.moveaxis(x, 1, 0)

def from_blocks(o):
    o = jnp.moveaxis(o, 0, 1)
    return o.reshape((o.shape[0], -1) + o.shape[3:])

def mla_attention(q_nope, q_rope, k_nope, k_rope, v):
    scale = (MLA_NOPE_DIM + MLA_ROPE_DIM) ** -0.5

    def block(args):
        qn, qr = args
        s = (jnp.einsum('bqhd,bkhd->bhqk', qn, k_nope).astype(jnp.float32)
             + jnp.einsum('bqhr,bkr->bhqk', qr, k_rope).astype(jnp.float32))
        p = jax.nn.softmax(s * scale, axis=-1).astype(v.dtype)
        return jnp.einsum('bhqk,bkhd->bqhd', p, v)

    return from_blocks(lax.map(block, (to_blocks(q_nope), to_blocks(q_rope))))

def diff_attention(q1, q2, k1, k2, v, lam):
    s_len = k1.shape[1]
    scale = DIFF_HEAD_DIM ** -0.5
    slopes = 2.0 ** (-8.0 * jnp.arange(1, DIFF_HEADS + 1, dtype=jnp.float32) / DIFF_HEADS)
    kpos = jnp.arange(s_len, dtype=jnp.float32)
    starts = jnp.arange(s_len // Q_BLOCK, dtype=jnp.float32) * Q_BLOCK

    def block(args):
        q1b, q2b, start = args
        qpos = start + jnp.arange(Q_BLOCK, dtype=jnp.float32)
        bias = -slopes[:, None, None] * jnp.abs(qpos[:, None] - kpos[None, :])[None]
        p1 = jax.nn.softmax(jnp.einsum('bqhd,bkhd->bhqk', q1b, k1).astype(jnp.float32) * scale + bias, axis=-1)
        p2 = jax.nn.softmax(jnp.einsum('bqhd,bkhd->bhqk', q2b, k2).astype(jnp.float32) * scale + bias, axis=-1)
        p = (p1 - lam * p2).astype(v.dtype)
        return jnp.einsum('bhqk,bkhd->bqhd', p, v)

    return from_blocks(lax.map(block, (to_blocks(q1), to_blocks(q2), starts)))

def token_mixer(x, layer_idx, w_in, g_q, g_kv, w_uq, w_ukv, lam_q1, lam_k1, lam_q2, lam_k2, g_sub, w_o):
    b, s, _ = x.shape
    h = x @ w_in
    offs = np.cumsum(IN_SIZES)[:-1].tolist()
    c_q, c_kv, k_rope, dq, dk, dv = jnp.split(h, offs, axis=-1)
    q = (rms_norm(c_q, g_q, RMS_EPS) @ w_uq).reshape(b, s, MLA_HEADS, MLA_NOPE_DIM + MLA_ROPE_DIM)
    q_nope, q_rope = q[..., :MLA_NOPE_DIM], q[..., MLA_NOPE_DIM:]
    kv = (rms_norm(c_kv, g_kv, RMS_EPS) @ w_ukv).reshape(b, s, MLA_HEADS, MLA_NOPE_DIM + MLA_V_DIM)
    k_nope, v_mla = kv[..., :MLA_NOPE_DIM], kv[..., MLA_NOPE_DIM:]
    cos, sin = rope_tables(s)
    q_rope = apply_rope(q_rope, cos[None, :, None, :], sin[None, :, None, :])
    k_rope = apply_rope(k_rope, cos[None], sin[None])
    o_mla = mla_attention(q_nope, q_rope, k_nope, k_rope, v_mla).reshape(b, s, MLA_WIDTH)
    dq = dq.reshape(b, s, DIFF_HEADS, 2, DIFF_HEAD_DIM)
    dk = dk.reshape(b, s, DIFF_HEADS, 2, DIFF_HEAD_DIM)
    dv = dv.reshape(b, s, DIFF_HEADS, 2 * DIFF_HEAD_DIM)
    lam_init = 0.8 - 0.6 * math.exp(-0.3 * layer_idx)
    lam = (jnp.exp(jnp.sum(lam_q1.astype(jnp.float32) * lam_k1.astype(jnp.float32)))
           - jnp.exp(jnp.sum(lam_q2.astype(jnp.float32) * lam_k2.astype(jnp.float32))) + lam_init)
    o_d = diff_attention(dq[..., 0, :], dq[..., 1, :], dk[..., 0, :], dk[..., 1, :], dv, lam)
    o_d = (rms_norm(o_d, g_sub, LN_EPS) * (1.0 - lam_init)).reshape(b, s, DIFF_WIDTH)
    return jnp.concatenate([o_mla, o_d], axis=-1) @ w_o

def grouped_moe(x, w_router, b_router, w_gate, w_up, w_down):
    b, s, d = x.shape
    xt = x.reshape(-1, d)
    scores = jax.nn.sigmoid((xt @ w_router).astype(jnp.float32))
    biased = scores + b_router.astype(jnp.float32)
    grp = biased.reshape(-1, N_GROUPS, EXPERTS_PER_GROUP)
    grp_score = jnp.sum(lax.top_k(grp, TOP_K)[0], axis=-1)
    g_idx = jnp.argmax(grp_score, axis=-1)
    in_group = (jnp.arange(N_EXPERTS) // EXPERTS_PER_GROUP)[None, :] == g_idx[:, None]
    _, e_idx = lax.top_k(jnp.where(in_group, biased, -jnp.inf), TOP_K)
    w_sel = jnp.take_along_axis(scores, e_idx, axis=-1)
    w_sel = w_sel / jnp.sum(w_sel, axis=-1, keepdims=True)
    gates = jnp.sum(jax.nn.one_hot(e_idx, N_EXPERTS, dtype=jnp.float32) * w_sel[..., None], axis=1)
    gates = gates.astype(x.dtype)
    y = jnp.zeros_like(xt)
    for e in range(N_EXPERTS):
        h = jax.nn.silu(xt @ w_gate[e]) * (xt @ w_up[e])
        y = y + gates[:, e:e + 1] * (h @ w_down[e])
    return y.reshape(b, s, d)

def trunk(x, ln0_g, ln0_b, w_in, g_q, g_kv, w_uq, w_ukv, lam_q1, lam_k1, lam_q2, lam_k2,
          g_sub, w_o, ln1_g, ln1_b, w_router, b_router, w_gate, w_up, w_down, ln2_g, ln2_b):
    x = layer_norm(x, ln0_g, ln0_b)
    for l in range(DEPTH):
        mix = token_mixer(x, l, w_in[l], g_q[l], g_kv[l], w_uq[l], w_ukv[l], lam_q1[l], lam_k1[l],
                          lam_q2[l], lam_k2[l], g_sub[l], w_o[l])
        x = layer_norm(ALPHA * x + mix, ln1_g[l], ln1_b[l])
        ffn = grouped_moe(x, w_router, b_router, w_gate[l], w_up[l], w_down[l])
        x = layer_norm(ALPHA * x + ffn, ln2_g[l], ln2_b[l])
    return x

def setup_inputs(seed: int = 0) -> dict:
    key = jax.random.key(seed)
    ks = jax.random.split(key, 26)

    def nrm(k, shape, scale):
        return jax.random.normal(k, shape, jnp.float32) * scale

    return {
        'x_prompt': nrm(ks[0], (BATCH, SEQ, D_MODEL), 1.0),
        'x_sample': nrm(ks[1], (DEC_BATCH, DEC_SEQ, D_MODEL), 1.0),
        'ln0_g': 1.0 + nrm(ks[2], (D_MODEL,), 0.01),
        'ln0_b': nrm(ks[3], (D_MODEL,), 0.01),
        'w_in': nrm(ks[4], (DEPTH, D_MODEL, IN_WIDTH), D_MODEL ** -0.5),
        'g_q': 1.0 + nrm(ks[5], (DEPTH, Q_LORA_RANK), 0.01),
        'g_kv': 1.0 + nrm(ks[6], (DEPTH, KV_LORA_RANK), 0.01),
        'w_uq': nrm(ks[7], (DEPTH, Q_LORA_RANK, MLA_HEADS * (MLA_NOPE_DIM + MLA_ROPE_DIM)), Q_LORA_RANK ** -0.5),
        'w_ukv': nrm(ks[8], (DEPTH, KV_LORA_RANK, MLA_HEADS * (MLA_NOPE_DIM + MLA_V_DIM)), KV_LORA_RANK ** -0.5),
        'lam_q1': nrm(ks[9], (DEPTH, DIFF_HEAD_DIM), 0.1),
        'lam_k1': nrm(ks[10], (DEPTH, DIFF_HEAD_DIM), 0.1),
        'lam_q2': nrm(ks[11], (DEPTH, DIFF_HEAD_DIM), 0.1),
        'lam_k2': nrm(ks[12], (DEPTH, DIFF_HEAD_DIM), 0.1),
        'g_sub': 1.0 + nrm(ks[13], (DEPTH, 2 * DIFF_HEAD_DIM), 0.01),
        'w_o': nrm(ks[14], (DEPTH, MIX_WIDTH, D_MODEL), BETA * MIX_WIDTH ** -0.5),
        'ln1_g': 1.0 + nrm(ks[15], (DEPTH, D_MODEL), 0.01),
        'ln1_b': nrm(ks[16], (DEPTH, D_MODEL), 0.01),
        'w_router': nrm(ks[17], (D_MODEL, N_EXPERTS), D_MODEL ** -0.5),
        'b_router': nrm(ks[18], (N_EXPERTS,), 0.01),
        'w_gate': nrm(ks[19], (DEPTH, N_EXPERTS, D_MODEL, D_FF_EXPERT), D_MODEL ** -0.5),
        'w_up': nrm(ks[20], (DEPTH, N_EXPERTS, D_MODEL, D_FF_EXPERT), D_MODEL ** -0.5),
        'w_down': nrm(ks[21], (DEPTH, N_EXPERTS, D_FF_EXPERT, D_MODEL), BETA * D_FF_EXPERT ** -0.5),
        'ln2_g': 1.0 + nrm(ks[22], (DEPTH, D_MODEL), 0.01),
        'ln2_b': nrm(ks[23], (DEPTH, D_MODEL), 0.01),
    }

def reference(x_prompt, x_sample, ln0_g, ln0_b, w_in, g_q, g_kv, w_uq, w_ukv, lam_q1, lam_k1,
              lam_q2, lam_k2, g_sub, w_o, ln1_g, ln1_b, w_router, b_router, w_gate, w_up, w_down,
              ln2_g, ln2_b):
    y_prompt = trunk(x_prompt, ln0_g, ln0_b, w_in, g_q, g_kv, w_uq, w_ukv, lam_q1, lam_k1, lam_q2, lam_k2,
                     g_sub, w_o, ln1_g, ln1_b, w_router, b_router, w_gate, w_up, w_down, ln2_g, ln2_b)
    y_sample = trunk(x_sample, ln0_g, ln0_b, w_in, g_q, g_kv, w_uq, w_ukv, lam_q1, lam_k1, lam_q2, lam_k2,
                     g_sub, w_o, ln1_g, ln1_b, w_router, b_router, w_gate, w_up, w_down, ln2_g, ln2_b)
    return (y_prompt, y_sample)


_drawn_inputs = setup_inputs


def setup_inputs(seed=0):
    import zlib

    import numpy as np

    out = dict(_drawn_inputs(seed))
    spreads = {}
    factors = {'g_q': 8.0,
     'g_kv': 8.0,
     'lam_q1': 3.614,
     'lam_k1': 8.0,
     'g_sub': 19.67,
     'ln1_b': 2.783,
     'ln2_g': 31.836,
     'ln2_b': 32.84,
     'lam_q2': 3.068,
     'lam_k2': 4.484}
    for name, (base, spread) in spreads.items():
        noise = np.random.default_rng([zlib.crc32(name.encode()), seed]).standard_normal(out[name].shape)
        drawn = base * np.exp(spread * noise) if base else spread * noise
        out[name] = __import__('jax').numpy.asarray(drawn.astype(out[name].dtype))
    for name, factor in factors.items():
        out[name] = (out[name] * factor).astype(out[name].dtype)
    return out
```

```python
import math

import concourse.bass as bass
from concourse import mybir

F = mybir.dt.float32
FR = mybir.dt.float32r
I32 = mybir.dt.int32
ALU = mybir.AluOpType
ACT = mybir.ActivationFunctionType
AX = mybir.AxisListType.X

P = 128
D = 1024
KD = D // P
SEQ_P, SEQ_S = 512, 256
NT_P, NT_S = SEQ_P // P, SEQ_S // P
NT = NT_P + NT_S
TOK = NT * P
HEADS = 8
NOPE, ROPE, VDIM = 64, 32, 64
HALF = ROPE // 2
QK = NOPE + ROPE
QR, KVR = 256, 128
CW = QR + KVR + ROPE
DH = 4
DHD = 64
DW = DH * 2 * DHD
IN_W = CW + 3 * DW
NE, NG, EPG = 16, 4, 4
FF = 512
LN_EPS, RMS_EPS = 1e-5, 1e-6
ALPHA = 2.0 ** 0.25
LAM_INIT = 0.2
MLA_SCALE = QK ** -0.5
DIFF_SCALE = DHD ** -0.5
ALIBI_W = 2 * SEQ_P - P
SEQS = ((0, SEQ_P, NT_P), (SEQ_P, SEQ_S, NT_S))
MAX_MORE = (2 * TOK - 1) // P
MAX_TILES = NE + MAX_MORE + 1
KB = 1024


def encoder_trunk(nc, x_prompt, x_sample, ln0_g, ln0_b, w_in, g_q, g_kv, w_uq, w_ukv, lam_q1, lam_k1,
                  lam_q2, lam_k2, g_sub, w_o, ln1_g, ln1_b, w_router, b_router, w_gate, w_up, w_down,
                  ln2_g, ln2_b, rope_cos, rope_sin, alibi, y_prompt, y_sample):
    base = 16640
    used = [0]

    def at(name, kb, shape, dt=F):
        n = 1
        for s in shape[1:]:
            n *= s
        assert base + kb * KB + 4 * n <= nc.sbuf_usable_end, name
        return nc.alloc_sbuf_tensor_at(name, list(shape), dt, offset=base + int(kb * KB))

    def small(name, shape, dt=F):
        n = 4
        for s in shape[1:]:
            n *= s
        off = used[0]
        used[0] += (n + 31) // 32 * 32
        assert used[0] <= 6 * KB, name
        return nc.alloc_sbuf_tensor_at(name, list(shape), dt, offset=base + off)

    def sem(name):
        return nc.alloc_semaphore(name)

    def f32(ap):
        return ap.bitcast(F)

    def bcast(vec, n):
        return vec.rearrange("(a n) -> a n", a=1).to_broadcast([P, n])

    ident = small("ident", [P, P])
    cos = small("cos", [P, NT, HALF])
    sin = small("sin", [P, NT, HALF])
    minus_half = small("minus_half", [P, 2 * NT])
    gq_col = small("gq_col", [P, 3])
    gsub_col = small("gsub_col", [P, 1])
    lam_col = small("lam_col", [P, 1])
    res = at("res", 6, [P, NT, D])
    psum = [nc.alloc_psum_tensor(f"bank{i}", [P, 512], F) for i in range(8)]

    xT_h = at("xT_h", 30, [P, KD, TOK], FR)
    xT_l = at("xT_l", 54, [P, KD, TOK], FR)
    WB = 256
    w_raw = [at(f"w_raw{i}", 78 + 8 * i, [P, KD * WB]) for i in range(2)]
    w_h = [at(f"w_h{i}", 94 + 8 * i, [P, KD * WB], FR) for i in range(2)]
    w_l = [at(f"w_l{i}", 110 + 8 * i, [P, KD * WB], FR) for i in range(2)]
    dqT = at("dqT", 126, [P, DH, TOK])
    dkT = at("dkT", 138, [P, DH, TOK])
    dv = at("dv", 150, [P, NT, DW])
    cT_h = at("cT_h", 162, [P, 3, TOK], FR)
    cT_l = at("cT_l", 171, [P, 3, TOK], FR)
    craw = at("craw", 180, [P, NT, CW])
    ln_g = at("ln_g", 190, [P, D])
    ln_b = at("ln_b", 194, [P, D])
    junk = at("junk", 198, [P, QR])
    kr = at("kr", 199, [P, NT, ROPE])
    ropetmp = at("ropetmp", 200, [P, 4, HEADS, HALF])
    lam_in = at("lam_in", 202, [P, 4, DHD])
    lam_prod = at("lam_prod", 203, [P, 2, DHD])
    q_tok = at("q_tok", 30, [P, NT, HEADS, QK])
    k_tok = at("k_tok", 48, [P, NT, HEADS, QK])
    v_tok = at("v_tok", 66, [P, NT, HEADS, VDIM])
    stats = small("stats", [P, 2, 2, 6])
    mv = small("mv", [P, NT, 2])
    rstd = small("rstd", [P, NT])
    ssq = small("ssq", [P, 2, NT])
    rms = small("rms", [P, 2, NT])
    lam_e = small("lam_e", [P, 2])
    lam_s = small("lam_s", [P, 2])

    s_const = sem("const_landed")
    s_lam_in = sem("lam_landed")
    s_lnw = sem("ln_weights_landed")
    s_x = [sem(f"x_landed{t}") for t in range(NT)]
    s_w = [sem(f"w_landed{i}") for i in range(2)]
    s_ident = sem("ident_ready")
    s_var = sem("variance_ready")
    s_rstd = sem("rstd_ready")
    s_dve = sem("dve_step")
    s_pool = sem("pool_step")
    s_act = sem("act_step")
    s_xln = sem("xln_ready")
    s_tp = sem("transposed")
    s_th = sem("transposed_high")
    s_tl = sem("transposed_low")
    s_wh = sem("w_high")
    s_wl = sem("w_low")
    s_proj = sem("projected")
    s_pev = sem("projection_out")
    s_ssq = sem("square_sums_ready")
    s_rms = sem("rms_ready")
    s_kr = sem("k_rope_ready")
    s_lam = sem("lambda_parts")
    s_kfill = sem("k_rope_filled")

    dve_steps = [0]

    def then(ins):
        dve_steps[0] += 1
        ins.then_inc(s_dve, 1)
        nc.vector.wait_ge(s_dve, dve_steps[0])

    w_in_v = w_in[0].rearrange("(c p) n -> p c n", p=P)
    blocks = [(w_in_v[:, :, 0:QR], KD, QR), (w_in_v[:, :, QR:CW], KD, CW - QR)]
    for i in range(3 * DW // WB):
        blocks.append((w_in_v[:, :, CW + i * WB:CW + (i + 1) * WB], KD, WB))
    blocks.append((w_uq[0].rearrange("(c p) n -> p c n", p=P), QR // P, HEADS * QK))
    blocks.append((w_ukv[0].rearrange("(c p) n -> p c n", p=P), 1, HEADS * (NOPE + VDIM)))
    NB = len(blocks)
    UQ, UKV = NB - 2, NB - 1
    BANKS = 6

    def wview(t, b):
        _, c, n = blocks[b]
        return t[b % 2][:, 0:c * n].rearrange("p (c n) -> p c n", c=c)

    def groups(b):
        if b < 2:
            return [("c", b, t) for t in range(NT)]
        if b < 6:
            return [("qk", b, f, s) for f in range(2) for s in range(2)]
        if b < 8:
            return [("v", b, t) for t in range(NT)]
        return [("uq" if b == UQ else "ukv", b, t, hf) for t in range(NT) for hf in range(2)]

    order = [g for t in range(NT) for g in (("c", 0, t), ("c", 1, t))]
    for b in range(2, NB):
        order += groups(b)
    first_of = {b: next(i for i, g in enumerate(order) if g[1] == b) for b in range(NB)}
    last_of = {b: max(i for i, g in enumerate(order) if g[1] == b) for b in range(NB)}
    NX = 2 * NT

    def xhalf(t, hf, hi_lo):
        return hi_lo[:, 4 * hf:4 * hf + 4, t * P:(t + 1) * P]

    with nc.Block() as block:

        @block.sync
        def _(sp):
            def load_w(b):
                if b >= 2:
                    sp.wait_ge(s_wl, 2 * (b - 2) + 2)
                sp.dma_start(wview(w_raw, b), blocks[b][0]).then_inc(s_w[b % 2], 16)

            def load_x(t):
                src = x_prompt[0, t * P:(t + 1) * P, :] if t < NT_P else x_sample[0, (t - NT_P) * P:(t - NT_P + 1) * P, :]
                sp.dma_start(res[:, t, :], src).then_inc(s_x[t], 16)

            load_x(0)
            sp.dma_start(ln_g[:], bcast(ln0_g, D)).then_inc(s_lnw, 16)
            sp.dma_start(ln_b[:], bcast(ln0_b, D)).then_inc(s_lnw, 16)
            load_w(0)
            load_x(1)
            load_w(1)
            for t in range(2, NT):
                load_x(t)
            sp.dma_start(cos[:], rope_cos).then_inc(s_const, 16)
            sp.dma_start(sin[:], rope_sin).then_inc(s_const, 16)
            with nc.allow_non_contiguous_dma("a column of gains"):
                sp.dma_start(gq_col[:, 0:2], g_q[0].rearrange("(c p) -> p c", p=P)).then_inc(s_const, 16)
                sp.dma_start(gq_col[:, 2:3], g_kv[0].rearrange("(c p) -> p c", p=P)).then_inc(s_const, 16)
                sp.dma_start(gsub_col[:], g_sub[0].rearrange("(c p) -> p c", p=P)).then_inc(s_const, 16)
            for i, v in enumerate((lam_q1, lam_k1, lam_q2, lam_k2)):
                sp.dma_start(lam_in[:, i, :], bcast(v[0], DHD)).then_inc(s_lam_in, 16)
            for b in range(2, NB):
                load_w(b)

        @block.gpsimd
        def _(pool):
            nc.gpsimd.memset(ident[:], 0.0).then_inc(s_pool, 1)
            nc.gpsimd.memset(minus_half[:], -0.5).then_inc(s_pool, 1)
            pool.wait_ge(s_pool, 2)
            nc.gpsimd.affine_select(out=ident[:], in_=ident[:], compare_op=ALU.not_equal, fill=1.0, base=0,
                                    pattern=[[-1, P]], channel_multiplier=1).then_inc(s_ident, 1)
            for t in range(NT):
                pool.wait_ge(s_var, t + 1)
                nc.gpsimd.tensor_tensor(rstd[:, t:t + 1], mv[:, t, 1:2], minus_half[:, 0:1], ALU.pow).then_inc(s_rstd, 1)
            pool.wait_ge(s_ssq, 1)
            nc.gpsimd.tensor_tensor(rms[:].rearrange("p a t -> p (a t)"), ssq[:].rearrange("p a t -> p (a t)"),
                                    minus_half[:], ALU.pow).then_inc(s_rms, 1)
            pool.wait_ge(s_kr, 1)
            for t in range(NT):
                pool.wait_ge(s_pev, last_of[7] + 1)
                nc.gpsimd.tensor_copy(k_tok[:, t, :, NOPE:QK],
                                      kr[:, t, :].unsqueeze(1).to_broadcast([P, HEADS, ROPE])).then_inc(s_kfill, 1)

        @block.tensor
        def _(pe):
            def transpose_x(t):
                pe.wait_ge(s_xln, t + 1)
                for hf in range(2):
                    q = 2 * t + hf
                    if q >= 2:
                        pe.wait_ge(s_tl, q - 1)
                    for j in range(4):
                        c = 4 * hf + j
                        last = nc.tensor.transpose(psum[q % 2][:, j * P:(j + 1) * P], res[:, t, c * P:(c + 1) * P], ident[:])
                    last.then_inc(s_tp, 1)

            def transpose_c():
                pe.wait_ge(s_pev, last_of[1] + 1)
                q = NX
                for j in range(3):
                    for t0, _, nt in SEQS:
                        pe.wait_ge(s_tl, q - 1)
                        for i in range(nt):
                            last = nc.tensor.transpose(psum[q % 2][:, i * P:(i + 1) * P],
                                                       craw[:, t0 // P + i, j * P:(j + 1) * P], ident[:])
                        last.then_inc(s_tp, 1)
                        q += 1

            def product(o, out, pairs):
                if o >= BANKS:
                    pe.wait_ge(s_pev, o - BANKS + 1)
                n = 3 * len(pairs)
                i = 0
                for ah, al, bh, bl in pairs:
                    for a, b in ((ah, bh), (al, bh), (ah, bl)):
                        last = nc.tensor.matmul(out, a, b, start=(i == 0), stop=(i == n - 1))
                        i += 1
                return last

            pe.wait_ge(s_ident, 1)
            transpose_x(0)
            for o, g in enumerate(order):
                kind, b = g[0], g[1]
                _, kc, n = blocks[b]
                wh, wl = wview(w_h, b), wview(w_l, b)
                bank = psum[2 + o % BANKS]
                if kind == "c" and b == 0:
                    if g[2] + 1 < NT:
                        transpose_x(g[2] + 1)
                    pe.wait_ge(s_tl, 2 * g[2] + 2)
                if o == first_of[b]:
                    pe.wait_ge(s_wl, 2 * b + 2)
                if o == first_of[3]:
                    transpose_c()
                if o == first_of[UQ]:
                    pe.wait_ge(s_tl, NX + 6)
                if kind in ("c", "v"):
                    t = g[2]
                    ts = slice(t * P, (t + 1) * P)
                    last = product(o, bank[:, 0:n], [(xT_h[:, c, ts], xT_l[:, c, ts], wh[:, c, :], wl[:, c, :])
                                                     for c in range(kc)])
                elif kind == "qk":
                    t0, nn, _ = SEQS[g[3]]
                    fs, ts = slice(g[2] * P, (g[2] + 1) * P), slice(t0, t0 + nn)
                    last = product(o, bank[:, 0:nn], [(wh[:, c, fs], wl[:, c, fs], xT_h[:, c, ts], xT_l[:, c, ts])
                                                      for c in range(kc)])
                else:
                    t, hf = g[2], g[3]
                    ts, c0 = slice(t * P, (t + 1) * P), (0 if kind == "uq" else 2)
                    w = n // 2
                    last = product(o, bank[:, 0:w], [(cT_h[:, c0 + c, ts], cT_l[:, c0 + c, ts],
                                                      wh[:, c, hf * w:(hf + 1) * w], wl[:, c, hf * w:(hf + 1) * w])
                                                     for c in range(kc)])
                last.then_inc(s_proj, 1)

        @block.scalar
        def _(act):
            def x_high(t):
                for hf in range(2):
                    q = 2 * t + hf
                    act.wait_ge(s_tp, q + 1)
                    nc.scalar.activation(xhalf(t, hf, xT_h), psum[q % 2][:].rearrange("p (c n) -> p c n", c=4),
                                         ACT.Copy).then_inc(s_th, 1)

            def c_high():
                act.wait_ge(s_const, 5 * 16)
                q = NX
                for j in range(3):
                    for t0, nn, _ in SEQS:
                        act.wait_ge(s_tp, q + 1)
                        nc.scalar.activation(cT_h[:, j, t0:t0 + nn], psum[q % 2][:, 0:nn], ACT.Copy,
                                             scale=gq_col[:, j:j + 1]).then_inc(s_th, 1)
                        q += 1

            def w_high(b):
                act.wait_ge(s_w[b % 2], 16 * (b // 2 + 1))
                if b >= 2:
                    act.wait_ge(s_proj, last_of[b - 2] + 1)
                w = blocks[b][1] * blocks[b][2] // 2
                for hf in range(2):
                    nc.scalar.activation(w_h[b % 2][:, hf * w:(hf + 1) * w], w_raw[b % 2][:, hf * w:(hf + 1) * w],
                                         ACT.Copy).then_inc(s_wh, 1)

            def c_squares():
                act.wait_ge(s_pev, last_of[1] + 1)
                k = 0
                for t in range(NT):
                    for i, (lo, n) in enumerate(((0, QR), (QR, KVR))):
                        if k:
                            act.wait_ge(s_act, k)
                        nc.scalar.activation(junk[:, 0:n], craw[:, t, lo:lo + n], ACT.Square,
                                             accum_out=ssq[:, i, t:t + 1]).then_inc(s_act, 1)
                        k += 1

            def out(o):
                g = order[o]
                kind, b = g[0], g[1]
                bank = psum[2 + o % BANKS]
                act.wait_ge(s_proj, o + 1)
                if kind == "c":
                    t = g[2]
                    lo, n = (0, QR) if b == 0 else (QR, CW - QR)
                    nc.scalar.activation(craw[:, t, lo:lo + n], bank[:, 0:n], ACT.Copy).then_inc(s_pev, 1)
                elif kind == "qk":
                    h = 2 * (b - 2) + g[2]
                    t0, nn, _ = SEQS[g[3]]
                    dst = dqT[:, h, t0:t0 + nn] if h < DH else dkT[:, h - DH, t0:t0 + nn]
                    nc.scalar.activation(dst, bank[:, 0:nn], ACT.Copy,
                                         scale=DIFF_SCALE if h < DH else 1.0).then_inc(s_pev, 1)
                elif kind == "v":
                    nc.scalar.activation(dv[:, g[2], (b - 6) * WB:(b - 5) * WB], bank[:, 0:WB], ACT.Copy).then_inc(s_pev, 1)
                elif kind == "uq":
                    t, hf = g[2], g[3]
                    nc.scalar.activation(q_tok[:, t, 4 * hf:4 * hf + 4, :],
                                         bank[:, 0:4 * QK].rearrange("p (h n) -> p h n", h=4),
                                         ACT.Copy, scale=rms[:, 0, t:t + 1]).then_inc(s_pev, 1)
                else:
                    t, hf = g[2], g[3]
                    kv = bank[:].rearrange("p (h n) -> p h n", h=4)
                    nc.scalar.activation(k_tok[:, t, 4 * hf:4 * hf + 4, 0:NOPE], kv[:, :, 0:NOPE], ACT.Copy,
                                         scale=rms[:, 1, t:t + 1])
                    nc.scalar.activation(v_tok[:, t, 4 * hf:4 * hf + 4, :], kv[:, :, NOPE:NOPE + VDIM], ACT.Copy,
                                         scale=rms[:, 1, t:t + 1]).then_inc(s_pev, 1)

            w_high(0)
            x_high(0)
            w_high(1)
            for o, g in enumerate(order):
                b = g[1]
                if g[0] == "c" and b == 0 and g[2] + 1 < NT:
                    x_high(g[2] + 1)
                out(o)
                if o == last_of[1]:
                    w_high(2)
                    c_squares()
                    act.wait_ge(s_lam, 1)
                    nc.scalar.activation(lam_e[:], lam_s[:], ACT.Exp).then_inc(s_lam, 1)
                    w_high(3)
                elif o == last_of[b] and b + 2 < NB and b >= 2:
                    w_high(b + 2)
                if o == last_of[2]:
                    c_high()
                    act.wait_ge(s_rms, 2)

        @block.vector
        def _(dve):
            def ln_stats(t):
                dve.wait_ge(s_x[t], 16)
                for i in range(2):
                    last = nc.vector.bn_stats(stats[:, t % 2, i, :], res[:, t, i * 512:(i + 1) * 512])
                    then(last)
                then(nc.vector.bn_aggr(mv[:, t, :], stats[:, t % 2, :, :].rearrange("p a b -> p (a b)")))
                nc.vector.tensor_scalar_add(mv[:, t, 1:2], mv[:, t, 1:2], LN_EPS).then_inc(s_var, 1)

            def ln_apply(t):
                if t == 0:
                    dve.wait_ge(s_lnw, 32)
                then(nc.vector.scalar_tensor_tensor(out=res[:, t, :], in0=res[:, t, :], scalar=mv[:, t, 0:1], in1=ln_g[:],
                                                    op0=ALU.subtract, op1=ALU.mult))
                dve.wait_ge(s_rstd, t + 1)
                nc.vector.scalar_tensor_tensor(out=res[:, t, :], in0=res[:, t, :], scalar=rstd[:, t:t + 1], in1=ln_b[:],
                                               op0=ALU.mult, op1=ALU.add).then_inc(s_xln, 1)

            def x_low(t):
                for hf in range(2):
                    q = 2 * t + hf
                    dve.wait_ge(s_th, q + 1)
                    nc.vector.tensor_tensor(xhalf(t, hf, xT_l), psum[q % 2][:].rearrange("p (c n) -> p c n", c=4),
                                            f32(xhalf(t, hf, xT_h)), ALU.subtract).then_inc(s_tl, 1)

            def w_low(b):
                w = blocks[b][1] * blocks[b][2] // 2
                for hf in range(2):
                    dve.wait_ge(s_wh, 2 * b + hf + 1)
                    nc.vector.tensor_tensor(w_l[b % 2][:, hf * w:(hf + 1) * w], w_raw[b % 2][:, hf * w:(hf + 1) * w],
                                            f32(w_h[b % 2][:, hf * w:(hf + 1) * w]), ALU.subtract).then_inc(s_wl, 1)

            def rotate(x1, x2, c, s, shape):
                a = [ropetmp[:, i] for i in range(4)] if shape == "heads" else [
                    ropetmp[:, i].rearrange("p h n -> p (h n)")[:, 0:NT * HALF].rearrange("p (t n) -> p t n", n=HALF)
                    for i in range(4)]
                nc.vector.tensor_tensor(a[0], x1, c, ALU.mult)
                nc.vector.tensor_tensor(a[1], x2, s, ALU.mult)
                nc.vector.tensor_tensor(a[2], x2, c, ALU.mult)
                then(nc.vector.tensor_tensor(a[3], x1, s, ALU.mult))
                nc.vector.tensor_tensor(x1 if shape == "heads" else kr[:, :, 0:HALF], a[0], a[1], ALU.subtract)
                return nc.vector.tensor_tensor(x2 if shape == "heads" else kr[:, :, HALF:ROPE], a[2], a[3], ALU.add)

            ln_stats(0)
            ln_apply(0)
            w_low(0)
            w_low(1)
            for t in range(NT):
                if t + 1 < NT:
                    ln_stats(t + 1)
                x_low(t)
                if t + 1 < NT:
                    ln_apply(t + 1)
            dve.wait_ge(s_lam_in, 64)
            lv = lam_in[:].rearrange("p (a b) n -> p a b n", b=2)
            then(nc.vector.tensor_tensor(lam_prod[:], lv[:, :, 0, :], lv[:, :, 1, :], ALU.mult))
            nc.vector.reduce_sum(lam_s[:], lam_prod[:], axis=AX).then_inc(s_lam, 1)
            w_low(2)
            dve.wait_ge(s_act, 2 * NT)
            nc.vector.tensor_scalar(ssq[:, 0, :], ssq[:, 0, :], 1.0 / QR, RMS_EPS, ALU.mult, ALU.add)
            nc.vector.tensor_scalar(ssq[:, 1, :], ssq[:, 1, :], 1.0 / KVR, RMS_EPS, ALU.mult, ALU.add).then_inc(s_ssq, 1)
            dve.wait_ge(s_lam, 2)
            then(nc.vector.tensor_tensor(lam_col[:], lam_e[:, 0:1], lam_e[:, 1:2], ALU.subtract))
            then(nc.vector.tensor_scalar_add(lam_col[:], lam_col[:], LAM_INIT))
            w_low(3)
            dve.wait_ge(s_rms, 1)
            nc.vector.tensor_scalar_mul(rms[:, 0, :], rms[:, 0, :], MLA_SCALE).then_inc(s_rms, 1)
            dve.wait_ge(s_const, 5 * 16)
            nc.vector.tensor_scalar_mul(gsub_col[:], gsub_col[:], 1.0 - LAM_INIT)
            rotate(craw[:, :, QR + KVR:QR + KVR + HALF], craw[:, :, QR + KVR + HALF:CW], cos[:], sin[:], "kr").then_inc(s_kr, 1)
            q = NX
            for j in range(3):
                for t0, nn, _ in SEQS:
                    dve.wait_ge(s_th, q + 1)
                    nc.vector.scalar_tensor_tensor(out=cT_l[:, j, t0:t0 + nn], in0=psum[q % 2][:, 0:nn],
                                                   scalar=gq_col[:, j:j + 1], in1=f32(cT_h[:, j, t0:t0 + nn]),
                                                   op0=ALU.mult, op1=ALU.subtract).then_inc(s_tl, 1)
                    q += 1
            for b in range(4, NB):
                w_low(b)
            for t in range(NT):
                dve.wait_ge(s_pev, first_of[UQ] + 2 * t + 2)
                then(rotate(q_tok[:, t, :, NOPE:NOPE + HALF], q_tok[:, t, :, NOPE + HALF:QK],
                            cos[:, t, :].unsqueeze(1).to_broadcast([P, HEADS, HALF]),
                            sin[:, t, :].unsqueeze(1).to_broadcast([P, HEADS, HALF]), "heads"))

    def wait(eng, semaphore, value):
        if not isinstance(value, int) or value > 0:
            eng.wait_ge(semaphore, value)
            if eng is nc.gpsimd and not isinstance(value, int):
                eng.sem_inc(s_passed, 1)

    s_passed = sem("passed_wait")

    def over(eng, n, body):
        body(0, True, False)
        with eng.Fori(1, n - 1) as i:
            body(i, False, False)
        body(n - 1, False, True)

    mixD_h = at("mixD_h", 162, [P, DH, TOK], FR)
    mixD_l = at("mixD_l", 174, [P, DH, TOK], FR)
    q_h = [[at(f"q_h{x}{m}", 78 + 6 * m + 4 * x, [P, SEQS[x][1]], FR) for m in range(2)] for x in range(2)]
    q_l = [[at(f"q_l{x}{m}", 80 + 6 * m + 3 * x, [P, SEQS[x][1]], FR) for m in range(2)] for x in range(2)]
    kk_h = [at(f"kk_h{x}", 90 + 4 * x, [P, SEQS[x][1]], FR) for x in range(2)]
    kk_l = [at(f"kk_l{x}", 92 + 3 * x, [P, SEQS[x][1]], FR) for x in range(2)]
    vv_h = [at(f"vv_h{x}", 96 + 4 * x, [P, SEQS[x][2], P], FR) for x in range(2)]
    vv_l = [at(f"vv_l{x}", 98 + 3 * x, [P, SEQS[x][2], P], FR) for x in range(2)]
    dpT_h = [at(f"dpT_h{i}", 102 + 4 * i, [P, 512], FR) for i in range(2)]
    dpT_l = [at(f"dpT_l{i}", 104 + 4 * i, [P, 512], FR) for i in range(2)]
    o_sb = [at(f"o_sb{i}", 110 + 0.5 * i, [P, P]) for i in range(2)]
    o_junk = at("o_junk", 111, [P, P])
    bias_t = at("bias_t", 112, [P, ALIBI_W])
    ee = [[at(f"ee{i}{m}", 186 + 4 * i + 2 * m, [P, 512]) for m in range(2)] for i in range(2)]
    pp = [at(f"pp{i}", 194 + 2 * i, [P, 512]) for i in range(2)]
    negmax = small("negmax", [P, 2, 2])
    esum = small("esum", [P, 2, 2])
    erec = small("erec", [P, 2, 2])
    osq = small("osq", [P, 2])
    orstd = small("orstd", [P, 2])

    s_alibi = sem("alibi_landed")
    s_zero = sem("zero_rows_ready")
    s_dh, s_dl = sem("diff_operands_high"), sem("diff_operands_low")
    s_sc, s_bias, s_exp = sem("diff_scores"), sem("diff_biased"), sem("diff_exp")
    s_rec, s_e2, s_p = sem("diff_reciprocals"), sem("diff_second_scaled"), sem("diff_probs")
    s_pt, s_pth, s_ptl = sem("diff_probs_T"), sem("diff_probs_T_high"), sem("diff_probs_T_low")
    s_pv, s_sq, s_or = sem("diff_out"), sem("diff_out_squares"), sem("diff_out_rstd")
    s_osb, s_ot, s_oth, s_otl = sem("diff_out_normed"), sem("diff_out_T"), sem("mixD_high"), sem("mixD_low")

    def dtile(i):
        x = int(i >= NT_P)
        return x, SEQS[x][1], SEQS[x][2], i - NT_P * x

    def shift(h, i):
        return h + i // NT, i % NT

    def reached(first, last, i):
        return not (first and i < 0) and not (last and i >= NT)

    def g_of(h, i):
        return h * NT + i

    QK_CUT = {3: (1, 0), 1: (0, 1)}
    V_CUT = {4: (1, 0), 2: (0, 1)}
    LAST_I = (NT_P - 1, NT - 1)

    with nc.Block() as block:

        @block.sync
        def _(sp):
            sp.dma_start(bias_t[:], alibi).then_inc(s_alibi, 16)

        @block.tensor
        def _(pe):
            def scores(h, i):
                h, i = shift(h, i)
                x, n, _, qt = dtile(i)
                g = g_of(h, i)
                if qt == 0:
                    wait(pe, s_dl, 8 * h + 4 * x + 3)
                for m in range(2):
                    wait(pe, s_bias, 2 * g - 4 + m + 1)
                    qs = slice(qt * P, (qt + 1) * P)
                    out = psum[2 * (i % 2) + m][:, 0:n]
                    nc.tensor.matmul(out, q_h[x][m][:, qs], kk_h[x][:], start=True, stop=False)
                    nc.tensor.matmul(out, q_l[x][m][:, qs], kk_h[x][:], start=False, stop=False)
                    nc.tensor.matmul(out, q_h[x][m][:, qs], kk_l[x][:], start=False, stop=True).then_inc(s_sc, 1)

            def out_T(h, i):
                h, i = shift(h, i)
                g = g_of(h, i)
                wait(pe, s_osb, g + 1)
                wait(pe, s_otl, g)
                nc.tensor.transpose(psum[7][:, 0:P], o_sb[i % 2][:], ident[:]).then_inc(s_ot, 1)

            def head(h, first, last):
                for i in range(NT):
                    x, n, nk, qt = dtile(i)
                    g = g_of(h, i)
                    wait(pe, s_p, g + 1)
                    wait(pe, s_ptl, g - 1)
                    for j in range(nk):
                        t = nc.tensor.transpose(psum[4 + i % 2][:, j * P:(j + 1) * P], pp[i % 2][:, j * P:(j + 1) * P], ident[:])
                    t.then_inc(s_pt, 1)
                    if reached(first, last, i + 2):
                        scores(h, i + 2)
                    wait(pe, s_ptl, g + 1)
                    wait(pe, s_osb, g)
                    if qt == 0:
                        wait(pe, s_dl, 8 * h + 4 * x + 4)
                    k = 0
                    for j in range(nk):
                        js = slice(j * P, (j + 1) * P)
                        for a, b in ((dpT_h, vv_h), (dpT_l, vv_h), (dpT_h, vv_l)):
                            t = nc.tensor.matmul(psum[6][:, 0:P], a[i % 2][:, js], b[x][:, j, :],
                                                 start=(k == 0), stop=(k == 3 * nk - 1))
                            k += 1
                    t.then_inc(s_pv, 1)
                    if reached(first, last, i - 1):
                        out_T(h, i - 1)
                if last:
                    out_T(h, NT - 1)

            pe.wait_ge(s_zero, 4)
            scores(0, 0)
            scores(0, 1)
            over(pe, DH, head)

        @block.scalar
        def _(act):
            def cut_qk(h, x):
                t0, n, _ = SEQS[x]
                wait(act, s_sc, 2 * (g_of(h, LAST_I[x]) - NT) + 2)
                for m in range(2):
                    r = slice(64 * m, 64 * m + 64)
                    nc.scalar.activation(q_h[x][m][r, :], dqT[r, h, t0:t0 + n], ACT.Copy).then_inc(s_dh, 1)
                nc.scalar.activation(kk_h[x][:], dkT[:, h, t0:t0 + n], ACT.Copy).then_inc(s_dh, 1)

            def cut_v(h, x):
                t0, _, nt = SEQS[x]
                wait(act, s_pv, g_of(h, LAST_I[x]) - NT + 1)
                nc.scalar.activation(vv_h[x][:], dv[:, t0 // P:t0 // P + nt, bass.ds(h * P, P)], ACT.Copy).then_inc(s_dh, 1)

            def exp(h, i, m):
                h, i = shift(h, i)
                n = dtile(i)[1]
                wait(act, s_bias, 2 * g_of(h, i) + m + 1)
                e = ee[i % 2][m][:, 0:n]
                nc.scalar.activation(e, e, ACT.Exp, scale=-1.0, bias=negmax[:, i % 2, m:m + 1],
                                     accum_out=esum[:, i % 2, m:m + 1]).then_inc(s_exp, 1)

            def squares(h, i):
                h, i = shift(h, i)
                wait(act, s_pv, g_of(h, i) + 1)
                nc.scalar.activation(o_junk[:], psum[6][:, 0:P], ACT.Square, scale=P ** -0.5,
                                     accum_out=osq[:, i % 2:i % 2 + 1]).then_inc(s_sq, 1)

            def normed(h, i):
                h, i = shift(h, i)
                g = g_of(h, i)
                wait(act, s_or, 2 * g + 2)
                wait(act, s_ot, g - 1)
                nc.scalar.activation(o_sb[i % 2][:], psum[6][:, 0:P], ACT.Copy, scale=orstd[:, i % 2:i % 2 + 1]).then_inc(s_osb, 1)

            def mix_high(h, i):
                h, i = shift(h, i)
                wait(act, s_ot, g_of(h, i) + 1)
                nc.scalar.activation(mixD_h[:, h, i * P:(i + 1) * P], psum[7][:, 0:P], ACT.Copy, scale=gsub_col[:]).then_inc(s_oth, 1)

            def head(h, first, last):
                for i in range(NT):
                    g = g_of(h, i)
                    if reached(first, last, i - 1):
                        squares(h, i - 1)
                    if reached(first, last, i + 1):
                        exp(h, i + 1, 0)
                    if reached(first, last, i - 1):
                        normed(h, i - 1)
                    if reached(first, last, i + 1):
                        exp(h, i + 1, 1)
                    wait(act, s_pt, g + 1)
                    wait(act, s_pv, g - 1)
                    n = dtile(i)[1]
                    nc.scalar.activation(dpT_h[i % 2][:, 0:n], psum[4 + i % 2][:, 0:n], ACT.Copy).then_inc(s_pth, 1)
                    if reached(first, last, i - 2):
                        mix_high(h, i - 2)
                    for cut, slots in ((cut_qk, QK_CUT), (cut_v, V_CUT)):
                        if i in slots:
                            dh, x = slots[i]
                            if not (last and dh):
                                cut(h + dh, x)
                if last:
                    squares(h, NT - 1)
                    normed(h, NT - 1)
                    mix_high(h, NT - 2)
                    mix_high(h, NT - 1)

            cut_qk(0, 0)
            cut_v(0, 0)
            exp(0, 0, 0)
            exp(0, 0, 1)
            over(act, DH, head)

        @block.gpsimd
        def _(pool):
            for x in range(2):
                for m in range(2):
                    r = slice(64 - 64 * m, 128 - 64 * m)
                    nc.gpsimd.memset(f32(q_h[x][m][r, :]), 0.0)
                    nc.gpsimd.memset(f32(q_l[x][m][r, :]), 0.0).then_inc(s_zero, 1)

            def second(h, i):
                h, i = shift(h, i)
                n = dtile(i)[1]
                wait(pool, s_rec, g_of(h, i) + 1)
                e = ee[i % 2][1][:, 0:n]
                nc.gpsimd.tensor_scalar(e, e, erec[:, i % 2, 1:2], None, ALU.mult).then_inc(s_e2, 1)

            def rstd_of(h, i):
                h, i = shift(h, i)
                g = g_of(h, i)
                wait(pool, s_sq, g + 1)
                o = orstd[:, i % 2:i % 2 + 1]
                nc.gpsimd.tensor_scalar_add(o, osq[:, i % 2:i % 2 + 1], LN_EPS).then_inc(s_or, 1)
                wait(pool, s_or, 2 * g + 1)
                nc.gpsimd.tensor_tensor(o, o, minus_half[:, 0:1], ALU.pow).then_inc(s_or, 1)

            def head(h, first, last):
                for i in range(NT):
                    if reached(first, last, i - 1):
                        rstd_of(h, i - 1)
                    if reached(first, last, i + 1):
                        second(h, i + 1)
                if last:
                    rstd_of(h, NT - 1)

            second(0, 0)
            over(pool, DH, head)

        @block.vector
        def _(dve):
            s_in = sem("bias_table_ready")

            def cut_qk(h, x):
                t0, n, _ = SEQS[x]
                for m in range(2):
                    r = slice(64 * m, 64 * m + 64)
                    wait(dve, s_dh, 8 * h + 4 * x + m + 1)
                    nc.vector.tensor_tensor(q_l[x][m][r, :], dqT[r, h, t0:t0 + n], f32(q_h[x][m][r, :]), ALU.subtract).then_inc(s_dl, 1)
                wait(dve, s_dh, 8 * h + 4 * x + 3)
                nc.vector.tensor_tensor(kk_l[x][:], dkT[:, h, t0:t0 + n], f32(kk_h[x][:]), ALU.subtract).then_inc(s_dl, 1)

            def cut_v(h, x):
                t0, _, nt = SEQS[x]
                wait(dve, s_dh, 8 * h + 4 * x + 4)
                nc.vector.tensor_tensor(vv_l[x][:], dv[:, t0 // P:t0 // P + nt, bass.ds(h * P, P)],
                                        f32(vv_h[x][:]), ALU.subtract).then_inc(s_dl, 1)

            def biased(h, i):
                h, i = shift(h, i)
                x, n, _, qt = dtile(i)
                for m in range(2):
                    wait(dve, s_sc, 2 * g_of(h, i) + m + 1)
                    dve.sem_inc(s_passed, 1)
                    lo = SEQ_P - P - qt * P
                    nc.vector.tensor_tensor_reduce(out=ee[i % 2][m][:, 0:n], in0=psum[2 * (i % 2) + m][:, 0:n],
                                                   in1=bias_t[:, lo:lo + n], scale=-1.0, scalar=3.0e38, op0=ALU.add,
                                                   op1=ALU.min, accum_out=negmax[:, i % 2, m:m + 1]).then_inc(s_bias, 1)

            def reciprocals(h, i):
                h, i = shift(h, i)
                g = g_of(h, i)
                wait(dve, s_exp, 2 * g + 2)
                nc.vector.reciprocal(erec[:, i % 2, :], esum[:, i % 2, :]).then_inc(s_rc, 1)
                wait(dve, s_rc, g + 1)
                nc.vector.tensor_tensor(erec[:, i % 2, 1:2], erec[:, i % 2, 1:2], lam_col[:], ALU.mult).then_inc(s_rec, 1)

            def probs(h, i):
                h, i = shift(h, i)
                n = dtile(i)[1]
                g = g_of(h, i)
                wait(dve, s_e2, g + 1)
                wait(dve, s_pt, g - 1)
                nc.vector.scalar_tensor_tensor(out=pp[i % 2][:, 0:n], in0=ee[i % 2][0][:, 0:n], scalar=erec[:, i % 2, 0:1],
                                               in1=ee[i % 2][1][:, 0:n], op0=ALU.mult, op1=ALU.subtract).then_inc(s_p, 1)

            def mix_low(h, i):
                h, i = shift(h, i)
                wait(dve, s_oth, g_of(h, i) + 1)
                ts = slice(i * P, (i + 1) * P)
                nc.vector.scalar_tensor_tensor(out=mixD_l[:, h, ts], in0=psum[7][:, 0:P], scalar=gsub_col[:],
                                               in1=f32(mixD_h[:, h, ts]), op0=ALU.mult, op1=ALU.subtract).then_inc(s_otl, 1)

            def head(h, first, last):
                for i in range(NT):
                    g = g_of(h, i)
                    n = dtile(i)[1]
                    if reached(first, last, i + 1):
                        reciprocals(h, i + 1)
                    wait(dve, s_pth, g + 1)
                    nc.vector.tensor_tensor(dpT_l[i % 2][:, 0:n], psum[4 + i % 2][:, 0:n], f32(dpT_h[i % 2][:, 0:n]),
                                            ALU.subtract).then_inc(s_ptl, 1)
                    if reached(first, last, i + 1):
                        probs(h, i + 1)
                    if reached(first, last, i - 2):
                        mix_low(h, i - 2)
                    for cut, slots in ((cut_qk, QK_CUT), (cut_v, V_CUT)):
                        if i in slots:
                            dh, x = slots[i]
                            if not (last and dh):
                                cut(h + dh, x)
                    if reached(first, last, i + 2):
                        if i + 2 == NT:
                            nc.vector.tensor_scalar_mul(bias_t[:], bias_t[:], 0.25).then_inc(s_in, 1)
                            wait(dve, s_in, h + 2)
                        biased(h, i + 2)
                if last:
                    mix_low(h, NT - 2)
                    mix_low(h, NT - 1)

            s_rc = sem("diff_sum_reciprocals")
            cut_qk(0, 0)
            cut_v(0, 0)
            dve.wait_ge(s_alibi, 16)
            nc.vector.tensor_scalar_mul(bias_t[:], bias_t[:], 0.25).then_inc(s_in, 1)
            dve.wait_ge(s_in, 1)
            biased(0, 0)
            biased(0, 1)
            reciprocals(0, 0)
            probs(0, 0)
            over(dve, DH, head)

    TP = 2 * NT
    START = (0, NT_P, NT, NT + NT_P)
    mixM_h = at("mixM_h", 126, [P, HEADS // 2, TOK], FR)
    mixM_l = at("mixM_l", 138, [P, HEADS // 2, TOK], FR)
    stage_q = [at(f"stage_q{x}", 78 + 3 * x, [P, SEQS[x][2], QK]) for x in range(2)]
    stage_k = [at(f"stage_k{x}", 79.5 + 2.25 * x, [P, SEQS[x][2], QK]) for x in range(2)]
    mq_h = [at(f"mq_h{x}", 83 + 8 * x, [P, SEQS[x][1]], FR) for x in range(2)]
    mq_l = [at(f"mq_l{x}", 85 + 7 * x, [P, SEQS[x][1]], FR) for x in range(2)]
    mk_h = [at(f"mk_h{x}", 87 + 6 * x, [P, SEQS[x][1]], FR) for x in range(2)]
    mk_l = [at(f"mk_l{x}", 89 + 5 * x, [P, SEQS[x][1]], FR) for x in range(2)]
    mv_h = [at(f"mv_h{x}", 95 + 4 * x, [P, SEQS[x][2], P], FR) for x in range(2)]
    mv_l = [at(f"mv_l{x}", 97 + 3 * x, [P, SEQS[x][2], P], FR) for x in range(2)]
    pT_h = [at(f"pT_h{x}", 102 + 16 * x, [P, SEQS[x][2], SEQS[x][1]], FR) for x in range(2)]
    pT_l = [at(f"pT_l{x}", 110 + 10 * x, [P, SEQS[x][2], SEQS[x][1]], FR) for x in range(2)]
    NE3 = 3
    me = [at(f"me{i}", 186 + 2 * i, [P, 512]) for i in range(NE3)]
    mmax = small("mmax", [P, 2])
    msum = small("msum", [P, 2])
    mrec = small("mrec", [P, 2])

    m_stage, m_tq = sem("mla_staged"), sem("mla_qk_T")
    m_qh, m_ql = sem("mla_qk_high"), sem("mla_qk_low")
    m_vh, m_vl = sem("mla_v_high"), sem("mla_v_low")
    m_sc, m_max, m_exp, m_rec, m_p = (sem("mla_scores"), sem("mla_max"), sem("mla_exp"), sem("mla_reciprocal"), sem("mla_probs"))
    m_pt, m_pth, m_ptl = sem("mla_probs_T"), sem("mla_probs_T_high"), sem("mla_probs_T_low")
    m_pv, m_mh, m_ml = sem("mla_out"), sem("mixM_high"), sem("mixM_low")

    def mtile(i):
        k = max(j for j in range(4) if START[j] <= i)
        x = k % 2
        return k, x, SEQS[x][1], SEQS[x][2], i - START[k]

    def mshift(hp, i):
        return hp + i // TP, i % TP

    def mreached(first, last, i):
        return not (first and i < 0) and not (last and i >= TP)

    STAGE_SLOTS = {7: (1, 0), 11: (1, 1), 1: (0, 2), 5: (0, 3)}
    TURN_SLOTS = {8: (1, 0), 0: (0, 1), 2: (0, 2), 6: (0, 3)}
    V_SLOTS = {0: 0, 2: 1}
    PV_SLOTS = {4: (0, 0), 6: (0, 1), 10: (0, 2), 0: (-1, 3)}
    MIX_SLOTS = {5: (0, 0), 7: (0, 1), 11: (0, 2), 1: (-1, 3)}

    def unit_last(w_pair, k):
        return w_pair * TP + (START[k + 1] if k < 3 else TP) - 1

    with nc.Block() as block:

        @block.tensor
        def _(pe):
            def turn(hp, k):
                x = k % 2
                w = 4 * hp + k
                wait(pe, m_stage, w + 1)
                wait(pe, m_ql, 2 * w)
                for bank, src in ((4, stage_q), (5, stage_k)):
                    for t in range(SEQS[x][2]):
                        last = nc.tensor.transpose(psum[bank][0:QK, t * P:(t + 1) * P], src[x][:, t, :], ident[:])
                    last.then_inc(m_tq, 1)

            def scores(hp, i):
                hp, i = mshift(hp, i)
                k, x, n, _, qt = mtile(i)
                g = hp * TP + i
                if qt == 0:
                    wait(pe, m_ql, 8 * hp + 2 * k + 2)
                wait(pe, m_exp, g - 1)
                qs = slice(qt * P, (qt + 1) * P)
                out = psum[i % 2][:, 0:n]
                nc.tensor.matmul(out, mq_h[x][0:QK, qs], mk_h[x][0:QK, :], start=True, stop=False)
                nc.tensor.matmul(out, mq_l[x][0:QK, qs], mk_h[x][0:QK, :], start=False, stop=False)
                nc.tensor.matmul(out, mq_h[x][0:QK, qs], mk_l[x][0:QK, :], start=False, stop=True).then_inc(m_sc, 1)

            def product(hp, k):
                x = k % 2
                _, n, nk = SEQS[x]
                wait(pe, m_ptl, unit_last(hp, k) + 1)
                wait(pe, m_vl, 2 * hp + x + 1)
                wait(pe, m_ml, 4 * hp + k - 1)
                i = 0
                for j in range(nk):
                    for a, b in ((mv_h, pT_h), (mv_l, pT_h), (mv_h, pT_l)):
                        last = nc.tensor.matmul(psum[6 + k % 2][:, 0:n], a[x][:, j, :], b[x][:, j, :],
                                                start=(i == 0), stop=(i == 3 * nk - 1))
                        i += 1
                last.then_inc(m_pv, 1)

            def pair(hp, first, last):
                for i in range(TP):
                    k, x, n, nk, qt = mtile(i)
                    g = hp * TP + i
                    wait(pe, m_p, g + 1)
                    wait(pe, m_ptl, g - 1)
                    for j in range(nk):
                        t = nc.tensor.transpose(psum[2 + i % 2][:, j * P:(j + 1) * P], me[i % NE3][:, j * P:(j + 1) * P], ident[:])
                    t.then_inc(m_pt, 1)
                    if i in TURN_SLOTS and not (last and TURN_SLOTS[i][0]):
                        turn(hp + TURN_SLOTS[i][0], TURN_SLOTS[i][1])
                    if mreached(first, last, i + 2):
                        scores(hp, i + 2)
                    if i in PV_SLOTS and not (first and PV_SLOTS[i][0]):
                        product(hp + PV_SLOTS[i][0], PV_SLOTS[i][1])
                if last:
                    product(hp, 3)

            turn(0, 0)
            scores(0, 0)
            scores(0, 1)
            over(pe, HEADS // 2, pair)

        @block.scalar
        def _(act):
            def cut_qk(hp, k):
                x = k % 2
                n = SEQS[x][1]
                w = 4 * hp + k
                wait(act, m_sc, unit_last(hp, k) - NT + 1)
                for j, dst in enumerate((mq_h, mk_h)):
                    wait(act, m_tq, 2 * w + j + 1)
                    nc.scalar.activation(dst[x][0:QK, :], psum[4 + j][0:QK, 0:n], ACT.Copy).then_inc(m_qh, 1)

            def exp(hp, i):
                hp, i = mshift(hp, i)
                n = mtile(i)[2]
                g = hp * TP + i
                wait(act, m_max, g + 1)
                wait(act, m_pt, g - NE3 + 1)
                nc.scalar.activation(me[i % NE3][:, 0:n], psum[i % 2][:, 0:n], ACT.Exp, bias=mmax[:, i % 2:i % 2 + 1],
                                     accum_out=msum[:, i % 2:i % 2 + 1]).then_inc(m_exp, 1)

            def mix_high(hp, k):
                t0, n, _ = SEQS[k % 2]
                r = slice(VDIM * (k // 2), VDIM * (k // 2) + VDIM)
                wait(act, m_pv, 4 * hp + k + 1)
                nc.scalar.activation(mixM_h[r, hp, t0:t0 + n], psum[6 + k % 2][r, 0:n], ACT.Copy).then_inc(m_mh, 1)

            def pair(hp, first, last):
                for i in range(TP):
                    k, x, n, nk, qt = mtile(i)
                    g = hp * TP + i
                    if mreached(first, last, i + 1):
                        exp(hp, i + 1)
                    wait(act, m_pt, g + 1)
                    if qt == 0:
                        wait(act, m_pv, 4 * hp + k - 1)
                    nc.scalar.activation(pT_h[x][:, :, qt * P:(qt + 1) * P], psum[2 + i % 2][:, 0:n].rearrange("p (j q) -> p j q", q=P),
                                         ACT.Copy).then_inc(m_pth, 1)
                    if i in TURN_SLOTS and not (last and TURN_SLOTS[i][0]):
                        cut_qk(hp + TURN_SLOTS[i][0], TURN_SLOTS[i][1])
                    if i in V_SLOTS:
                        vx = V_SLOTS[i]
                        t0, _, nt = SEQS[vx]
                        wait(act, m_pv, 4 * hp + vx - 1)
                        nc.scalar.activation(mv_h[vx][:].rearrange("p t (h n) -> p t h n", h=2),
                                             v_tok[:, t0 // P:t0 // P + nt, bass.ds(2 * hp, 2), :], ACT.Copy).then_inc(m_vh, 1)
                    if i in MIX_SLOTS and not (first and MIX_SLOTS[i][0]):
                        mix_high(hp + MIX_SLOTS[i][0], MIX_SLOTS[i][1])
                if last:
                    mix_high(hp, 3)

            cut_qk(0, 0)
            exp(0, 0)
            over(act, HEADS // 2, pair)

        @block.gpsimd
        def _(pool):
            def stage(hp, k):
                x = k % 2
                t0, _, nt = SEQS[x]
                wait(pool, m_tq, 2 * (4 * hp + k) - 2)
                for dst, src in ((stage_q, q_tok), (stage_k, k_tok)):
                    last = nc.gpsimd.tensor_copy(dst[x][:].unsqueeze(2), src[:, t0 // P:t0 // P + nt, bass.ds(2 * hp + k // 2, 1), :])
                last.then_inc(m_stage, 1)

            def normalise(hp, i):
                hp, i = mshift(hp, i)
                n = mtile(i)[2]
                wait(pool, m_rec, hp * TP + i + 1)
                e = me[i % NE3][:, 0:n]
                nc.gpsimd.tensor_scalar(e, e, mrec[:, i % 2:i % 2 + 1], None, ALU.mult).then_inc(m_p, 1)

            def pair(hp, first, last):
                for i in range(TP):
                    if mreached(first, last, i + 1):
                        normalise(hp, i + 1)
                    if i in STAGE_SLOTS and not (last and STAGE_SLOTS[i][0]):
                        stage(hp + STAGE_SLOTS[i][0], STAGE_SLOTS[i][1])

            stage(0, 0)
            stage(0, 1)
            normalise(0, 0)
            over(pool, HEADS // 2, pair)

        @block.vector
        def _(dve):
            def cut_qk(hp, k):
                x = k % 2
                n = SEQS[x][1]
                for j, (hi, lo) in enumerate(((mq_h, mq_l), (mk_h, mk_l))):
                    wait(dve, m_qh, 2 * (4 * hp + k) + j + 1)
                    nc.vector.tensor_tensor(lo[x][0:QK, :], psum[4 + j][0:QK, 0:n], f32(hi[x][0:QK, :]), ALU.subtract).then_inc(m_ql, 1)

            def maximum(hp, i):
                hp, i = mshift(hp, i)
                n = mtile(i)[2]
                wait(dve, m_sc, hp * TP + i + 1)
                nc.vector.tensor_reduce(mmax[:, i % 2:i % 2 + 1], psum[i % 2][:, 0:n], axis=AX, op=ALU.max,
                                        negate=True).then_inc(m_max, 1)

            def reciprocal(hp, i):
                hp, i = mshift(hp, i)
                wait(dve, m_exp, hp * TP + i + 1)
                nc.vector.reciprocal(mrec[:, i % 2:i % 2 + 1], msum[:, i % 2:i % 2 + 1]).then_inc(m_rec, 1)

            def mix_low(hp, k):
                t0, n, _ = SEQS[k % 2]
                r = slice(VDIM * (k // 2), VDIM * (k // 2) + VDIM)
                wait(dve, m_mh, 4 * hp + k + 1)
                nc.vector.tensor_tensor(mixM_l[r, hp, t0:t0 + n], psum[6 + k % 2][r, 0:n], f32(mixM_h[r, hp, t0:t0 + n]),
                                        ALU.subtract).then_inc(m_ml, 1)

            def pair(hp, first, last):
                for i in range(TP):
                    k, x, n, nk, qt = mtile(i)
                    g = hp * TP + i
                    if mreached(first, last, i + 1):
                        reciprocal(hp, i + 1)
                    wait(dve, m_pth, g + 1)
                    qs = slice(qt * P, (qt + 1) * P)
                    nc.vector.tensor_tensor(pT_l[x][:, :, qs], psum[2 + i % 2][:, 0:n].rearrange("p (j q) -> p j q", q=P),
                                            f32(pT_h[x][:, :, qs]), ALU.subtract).then_inc(m_ptl, 1)
                    if i in TURN_SLOTS and not (last and TURN_SLOTS[i][0]):
                        cut_qk(hp + TURN_SLOTS[i][0], TURN_SLOTS[i][1])
                    if i in V_SLOTS:
                        vx = V_SLOTS[i]
                        t0, _, nt = SEQS[vx]
                        wait(dve, m_vh, 2 * hp + vx + 1)
                        nc.vector.tensor_tensor(mv_l[vx][:].rearrange("p t (h n) -> p t h n", h=2),
                                                v_tok[:, t0 // P:t0 // P + nt, bass.ds(2 * hp, 2), :],
                                                f32(mv_h[vx][:]).rearrange("p t (h n) -> p t h n", h=2),
                                                ALU.subtract).then_inc(m_vl, 1)
                    if i in MIX_SLOTS and not (first and MIX_SLOTS[i][0]):
                        mix_low(hp + MIX_SLOTS[i][0], MIX_SLOTS[i][1])
                    if mreached(first, last, i + 2):
                        maximum(hp, i + 2)
                if last:
                    mix_low(hp, 3)

            cut_qk(0, 0)
            maximum(0, 0)
            maximum(0, 1)
            reciprocal(0, 0)
            over(dve, HEADS // 2, pair)


    HW = D // 2
    wo_raw = [at(f"wo_raw{c}", 30 + 2 * c, [P, HW]) for c in range(KD)]
    wo_h = [at(f"wo_h{c}", 46 + 2 * c, [P, HW], FR) for c in range(KD)]
    wo_l = [at(f"wo_l{c}", 62 + 2 * c, [P, HW], FR) for c in range(KD)]
    ln1g_sb = at("ln1g_sb", 186, [P, D])
    ln1b_sb = at("ln1b_sb", 190, [P, D])
    ax = [at(f"ax{i}", 194 + 4 * i, [P, D]) for i in range(2)]
    x1T = at("x1T", 202, [P, KD, P])
    raw = {X: [at(f"raw{X}{i}", 78 + 16 * n + 4 * i, [P, 2 * FF]) for i in range(4)] for n, X in enumerate("GUD")}
    x1_rows = nc.dram_tensor("x1_rows", (TOK + P, D), F).ap()
    acc_rows = nc.dram_tensor("acc_rows", (TOK + P, D), F).ap()

    cursor = [150 * KB]

    def tmp(name, shape, dt=F):
        n = 4
        for v in shape[1:]:
            n *= v
        off = cursor[0]
        cursor[0] += (n + 31) // 32 * 32
        assert cursor[0] <= 162 * KB, name
        return nc.alloc_sbuf_tensor_at(name, list(shape), dt, offset=base + off)

    wr_sb = tmp("wr_sb", [P, KD, NE])
    br_sb = tmp("br_sb", [P, NE])
    before = tmp("before", [P, P])
    ones = tmp("ones", [P, P])
    i128 = tmp("i128", [P, P])
    i32a = tmp("i32a", [P, P], I32)
    itile = tmp("itile", [P, MAX_TILES])
    irank = tmp("irank", [P, NE])
    grank = tmp("grank", [P, NG])
    iexp = tmp("iexp", [P, NE])
    tok1 = tmp("tok1", [P, NT])
    padrow = tmp("padrow", [P, 1])
    sg = tmp("sg", [P, NT, NE])
    bs = tmp("bs", [P, NT, NE])
    g6 = [tmp(f"g6_{i}", [P, NT * NG]) for i in range(6)]
    r1 = tmp("r1", [P, NT])
    r2 = tmp("r2", [P, NT])
    mb = [tmp(f"mb{i}", [P, NT, NE]) for i in range(2)]
    t16 = tmp("t16", [P, NT, NE])
    picks = tmp("picks", [P, 2, NT, NE])
    prod = tmp("prod", [P, 2, NT, NE])
    member = tmp("member", [P, NT, NE])
    pos = tmp("pos", [P, NT, NE])
    more = tmp("more", [P, NE])
    upto = tmp("upto", [P, NE])
    cnt_i = tmp("cnt_i", [P, NE], I32)
    first_more = tmp("first_more", [P, NE])
    gate = tmp("gate", [P, 2, NT])
    place = tmp("place", [P, 2, NT])
    place_i = tmp("place_i", [P, 2, NT], I32)
    blk = tmp("blk", [P, 2, NT])
    low = tmp("low", [P, 2, NT])
    exp_of = tmp("exp_of", [P, 2, NT])
    tile_of = tmp("tile_of", [P, 2, NT])
    hot = tmp("hot", [P, 2, P])
    vals = tmp("vals", [P, 2, 2, MAX_TILES])
    le = tmp("le", [1, MAX_MORE + 1, NE])
    te_f = tmp("te_f", [1, MAX_TILES])
    idx_f = tmp("idx_f", [P, MAX_TILES])
    idx_tab = small("idx_tab", [P, MAX_TILES], I32)
    gate_tab = small("gate_tab", [P, MAX_TILES])
    tile_expert = small("tile_expert", [1, MAX_TILES], I32)
    n_more_sb = small("n_more_sb", [1, 1], I32)

    s_ln1w, s_rt = sem("ln1_weights_landed"), sem("router_weights_landed")
    s_wo = [sem(f"wo_landed{c}") for c in range(KD)]
    s_woh, s_wol, s_wou = sem("wo_high"), sem("wo_low"), sem("wo_chunk_used")
    s_o0, s_o1, s_y0, s_y1 = sem("o_first_half"), sem("o_second_half"), sem("o_first_half_out"), sem("o_second_half_out")
    s_var1, s_rstd1, s_x1 = sem("ln1_variance"), sem("ln1_rstd"), sem("x1_ready")
    s_x1t, s_x1e, s_log = sem("x1_transposed"), sem("x1T_ready"), sem("logits")
    s_ax, s_x1st, s_stored = sem("scaled_x1"), sem("x1_stored"), [sem(f"scaled_x1_stored{i}") for i in range(2)]
    s_zrow, s_zst = sem("zero_rows"), sem("zero_rows_stored")
    s_consts = sem("router_constants")
    s_rexp, s_member, s_prefix = sem("router_exp"), sem("router_members"), sem("router_prefix")
    s_hot, s_hotused, s_slots = sem("one_hots"), sem("one_hots_used"), sem("slot_table")
    s_raw = {X: [sem(f"raw{X}{i}_landed") for i in range(4)] for X in "GUD"}

    def unit_src(X, e, i):
        if X == "D":
            return w_down[0, bass.ds(e, 1), i * P:(i + 1) * P, :].rearrange("a p n -> p (a n)")
        w = w_gate if X == "G" else w_up
        return w[0, bass.ds(e, 1), 2 * i * P:(2 * i + 2) * P, :].rearrange("a (c p) n -> p (a c) n", p=P)

    def unit_dst(X, i):
        return raw[X][i][:] if X == "D" else raw[X][i][:].rearrange("p (c n) -> p c n", c=2)

    def mix(c, hi):
        t = (mixM_h if hi else mixM_l) if c < KD // 2 else (mixD_h if hi else mixD_l)
        return t[:, c % (KD // 2), :]

    with nc.Block() as block:

        @block.sync
        def _(sp):
            for u in range(2 * KD):
                n, c = u // KD, u % KD
                if n:
                    sp.wait_ge(s_wol, u - KD + 1)
                sp.dma_start(wo_raw[c][:], w_o[0, c * P:(c + 1) * P, n * HW:(n + 1) * HW]).then_inc(s_wo[c], 16)
                if u == KD - 1:
                    sp.dma_start(ln1g_sb[:], bcast(ln1_g[0], D)).then_inc(s_ln1w, 16)
                    sp.dma_start(ln1b_sb[:], bcast(ln1_b[0], D)).then_inc(s_ln1w, 16)
                    sp.dma_start(wr_sb[:], w_router.rearrange("(c p) n -> p c n", p=P)).then_inc(s_rt, 16)
                    sp.dma_start(br_sb[:], bcast(b_router, NE)).then_inc(s_rt, 16)
                    for X in "GUD":
                        for i in range(4):
                            sp.dma_start(unit_dst(X, i), unit_src(X, 0, i)).then_inc(s_raw[X][i], 16)
            sp.wait_ge(s_zrow, 1)
            sp.dma_start(x1_rows[TOK:TOK + P, :], ax[1][:]).then_inc(s_zst, 16)
            sp.dma_start(acc_rows[TOK:TOK + P, :], ax[1][:]).then_inc(s_zst, 16)
            for t in range(NT):
                sp.wait_ge(s_x1, t + 1)
                sp.dma_start(x1_rows[t * P:(t + 1) * P, :], res[:, t, :]).then_inc(s_x1st, 16)
                sp.wait_ge(s_ax, t + 1)
                sp.dma_start(acc_rows[t * P:(t + 1) * P, :], ax[t % 2][:]).then_inc(s_stored[t % 2], 16)
            sp.wait_ge(s_zst, 32)
            for i in range(2):
                sp.wait_ge(s_stored[i], 16 * (NT // 2))
            sp.wait_ge(s_x1st, 16 * NT)

        @block.tensor
        def _(pe):
            def second_half(t):
                wait(pe, s_y1, t - 1)
                ts = slice(t * P, (t + 1) * P)
                out = psum[6 + t % 2][:]
                for c in range(KD):
                    if t == 0:
                        pe.wait_ge(s_wol, KD + c + 1)
                    nc.tensor.matmul(out, mix(c, True)[:, ts], wo_h[c][:], start=(c == 0), stop=False)
                    nc.tensor.matmul(out, mix(c, False)[:, ts], wo_h[c][:], start=False, stop=False)
                    last = nc.tensor.matmul(out, mix(c, True)[:, ts], wo_l[c][:], start=False, stop=(c == KD - 1))
                last.then_inc(s_o1, 1)

            def turn_x1(t):
                pe.wait_ge(s_x1, t + 1)
                pe.wait_ge(s_y0, 2)
                wait(pe, s_x1e, 2 * t)
                for hf in range(2):
                    for j in range(4):
                        c = 4 * hf + j
                        last = nc.tensor.transpose(psum[hf][:, j * P:(j + 1) * P], res[:, t, c * P:(c + 1) * P], ident[:])
                    last.then_inc(s_x1t, 1)

            def logits(t):
                pe.wait_ge(s_x1e, 2 * t + 2)
                pe.wait_ge(s_rt, 32)
                pe.wait_ge(s_y0, 3)
                for c in range(KD):
                    last = nc.tensor.matmul(psum[2][:, t * NE:(t + 1) * NE], x1T[:, c, :], wr_sb[:, c, :],
                                            start=(c == 0), stop=(c == KD - 1))
                last.then_inc(s_log, 1)

            for c in range(KD):
                pe.wait_ge(s_wol, c + 1)
                for t in range(NT):
                    ts = slice(t * P, (t + 1) * P)
                    out = psum[t][:]
                    nc.tensor.matmul(out, mix(c, True)[:, ts], wo_h[c][:], start=(c == 0), stop=False)
                    nc.tensor.matmul(out, mix(c, False)[:, ts], wo_h[c][:], start=False, stop=False)
                    last = nc.tensor.matmul(out, mix(c, True)[:, ts], wo_l[c][:], start=False, stop=(c == KD - 1))
                    if c == KD - 1:
                        last.then_inc(s_o0, 1)
                if c < KD - 1:
                    last.then_inc(s_wou, 1)
            for t in range(NT):
                second_half(t)
                if t >= 2:
                    logits(t - 2)
                if t >= 1:
                    turn_x1(t - 1)
            logits(NT - 2)
            turn_x1(NT - 1)
            logits(NT - 1)

            pe.wait_ge(s_member, 1)
            pe.wait_ge(s_consts, 1)
            pe.wait_ge(s_y0, NT)
            m = member[:].rearrange("p t e -> p (t e)")
            nc.tensor.matmul(psum[3][:, 0:NT * NE], before[:], m, start=True, stop=False)
            for d in range(1, NT):
                nc.tensor.matmul(psum[3][:, d * NE:NT * NE], ones[:], m[:, 0:(NT - d) * NE], start=False, stop=(d == NT - 1))
            for t in range(NT):
                last = nc.tensor.matmul(psum[4][:, 0:NE], ones[:], member[:, t, :], start=(t == 0), stop=(t == NT - 1))
            last.then_inc(s_prefix, 1)
            for n in range(2 * NT):
                pe.wait_ge(s_hot, n + 1)
                nc.tensor.matmul(psum[5][:, 0:2 * MAX_TILES], hot[:, n % 2, :], vals[:, n % 2].rearrange("p a b -> p (a b)"),
                                 start=(n == 0), stop=(n == 2 * NT - 1)).then_inc(s_slots, 1)

        @block.scalar
        def _(act):
            def wo_high(u):
                n, c = u // KD, u % KD
                act.wait_ge(s_wo[c], 16 * (n + 1))
                if n:
                    if c < KD - 1:
                        act.wait_ge(s_wou, c + 1)
                    else:
                        act.wait_ge(s_o0, NT)
                nc.scalar.activation(wo_h[c][:], wo_raw[c][:], ACT.Copy).then_inc(s_woh, 1)

            for u in range(2 * KD):
                wo_high(u)
            act.wait_ge(s_zst, 32)
            for t in range(NT):
                act.wait_ge(s_x1, t + 1)
                if t >= 2:
                    act.wait_ge(s_stored[t % 2], 16 * (t // 2))
                for hf in range(2):
                    act.wait_ge(s_x1t, 2 * t + hf + 1)
                    wait(act, s_log, t)
                    nc.scalar.activation(x1T[:, 4 * hf:4 * hf + 4, :], psum[hf][:].rearrange("p (c n) -> p c n", c=4),
                                         ACT.Copy).then_inc(s_x1e, 1)
                nc.scalar.activation(ax[t % 2][:], res[:, t, :], ACT.Copy, scale=ALPHA).then_inc(s_ax, 1)
            act.wait_ge(s_log, NT)
            nc.scalar.activation(sg[:], psum[2][:, 0:NT * NE].rearrange("p (t e) -> p t e", t=NT), ACT.Exp,
                                 scale=-1.0).then_inc(s_rexp, 1)

        @block.gpsimd
        def _(pool):
            n = [0]

            def done(ins):
                n[0] += 1
                ins.then_inc(s_pool2, 1)
                pool.wait_ge(s_pool2, n[0])

            s_pool2 = sem("router_pool_step")
            nc.gpsimd.memset(ax[1][:], 0.0).then_inc(s_zrow, 1)
            done(nc.gpsimd.memset(before[:], 1.0))
            nc.gpsimd.memset(ones[:], 1.0)
            done(nc.gpsimd.affine_select(out=before[:], in_=before[:], compare_op=ALU.is_gt, fill=0.0, base=0,
                                         pattern=[[1, P]], channel_multiplier=-1))

            def counted(dst, pattern, base0, mult):
                w = 1
                for _, k in pattern:
                    w *= k
                done(nc.gpsimd.iota(i32a[:, 0:w], pattern=pattern, base=base0, channel_multiplier=mult))
                done(nc.gpsimd.tensor_copy(dst, i32a[:, 0:w]))

            counted(i128[:], [[1, P]], 0, 0)
            counted(itile[:], [[1, MAX_TILES]], 0, 0)
            counted(irank[:], [[-1, NE]], NE, 0)
            counted(grank[:], [[-1, NG]], NG, 0)
            counted(iexp[:], [[1, NE]], 0, 0)
            counted(tok1[:], [[P, NT]], 1, 1)
            counted(padrow[:], [[1, 1]], TOK + 1, 1)
            nc.gpsimd.memset(te_f[:], 0.0).then_inc(s_consts, 1)
            for t in range(NT):
                pool.wait_ge(s_var1, t + 1)
                nc.gpsimd.tensor_tensor(rstd[:, t:t + 1], mv[:, t, 1:2], minus_half[:, 0:1], ALU.pow).then_inc(s_rstd1, 1)

        @block.vector
        def _(dve):
            def wo_low(u):
                c = u % KD
                dve.wait_ge(s_woh, u + 1)
                nc.vector.tensor_tensor(wo_l[c][:], wo_raw[c][:], f32(wo_h[c][:]), ALU.subtract).then_inc(s_wol, 1)

            for u in range(2 * KD):
                wo_low(u)
            for t in range(NT):
                dve.wait_ge(s_o0, t + 1)
                nc.vector.scalar_tensor_tensor(out=res[:, t, 0:HW], in0=res[:, t, 0:HW], scalar=ALPHA, in1=psum[t][:],
                                               op0=ALU.mult, op1=ALU.add).then_inc(s_y0, 1)
            dve.wait_ge(s_ln1w, 32)
            for t in range(NT):
                dve.wait_ge(s_o1, t + 1)
                nc.vector.scalar_tensor_tensor(out=res[:, t, HW:D], in0=res[:, t, HW:D], scalar=ALPHA, in1=psum[6 + t % 2][:],
                                               op0=ALU.mult, op1=ALU.add).then_inc(s_y1, 1)
                dve.wait_ge(s_y0, t + 1)
                nc.vector.bn_stats(stats[:, t % 2, 0, :], res[:, t, 0:HW])
                dve.wait_ge(s_y1, t + 1)
                then(nc.vector.bn_stats(stats[:, t % 2, 1, :], res[:, t, HW:D]))
                then(nc.vector.bn_aggr(mv[:, t, :], stats[:, t % 2, :, :].rearrange("p a b -> p (a b)")))
                nc.vector.tensor_scalar_add(mv[:, t, 1:2], mv[:, t, 1:2], LN_EPS).then_inc(s_var1, 1)
                then(nc.vector.scalar_tensor_tensor(out=res[:, t, :], in0=res[:, t, :], scalar=mv[:, t, 0:1], in1=ln1g_sb[:],
                                                    op0=ALU.subtract, op1=ALU.mult))
                dve.wait_ge(s_rstd1, t + 1)
                nc.vector.scalar_tensor_tensor(out=res[:, t, :], in0=res[:, t, :], scalar=rstd[:, t:t + 1], in1=ln1b_sb[:],
                                               op0=ALU.mult, op1=ALU.add).then_inc(s_x1, 1)

            tt, ts = nc.vector.tensor_tensor, nc.vector.tensor_scalar
            tne = [P, NT, NE]

            dve.wait_ge(s_rexp, 1)
            dve.wait_ge(s_rt, 32)
            dve.wait_ge(s_consts, 1)
            then(nc.vector.tensor_scalar_add(sg[:], sg[:], 1.0))
            then(nc.vector.reciprocal(sg[:], sg[:]))
            then(tt(bs[:], sg[:], br_sb[:].unsqueeze(1).to_broadcast(tne), ALU.add))
            four = bs[:].rearrange("p t (g k) -> p (t g) k", k=EPG)
            a, b, c, d = (four[:, :, i] for i in range(4))
            tt(g6[0][:], a, b, ALU.max)
            tt(g6[1][:], a, b, ALU.min)
            tt(g6[2][:], c, d, ALU.max)
            then(tt(g6[3][:], c, d, ALU.min))
            tt(g6[4][:], g6[0][:], g6[2][:], ALU.max)
            tt(g6[5][:], g6[0][:], g6[2][:], ALU.min)
            then(tt(g6[1][:], g6[1][:], g6[3][:], ALU.max))
            then(tt(g6[5][:], g6[5][:], g6[1][:], ALU.max))
            then(tt(g6[0][:], g6[4][:], g6[5][:], ALU.add))

            def first_best(val, rank, work, n, out, best):
                full = [P, NT, n]
                then(nc.vector.tensor_reduce(best, val, axis=AX, op=ALU.max))
                then(tt(work, val, best.unsqueeze(2).to_broadcast(full), ALU.is_equal))
                then(tt(work, work, rank[:].unsqueeze(1).to_broadcast(full), ALU.mult))
                then(nc.vector.tensor_reduce(best, work, axis=AX, op=ALU.max))
                then(tt(out, work, best.unsqueeze(2).to_broadcast(full), ALU.is_equal))

            def by_group(t):
                return t[:].rearrange("p (t g) -> p t g", g=NG)

            first_best(by_group(g6[0]), grank, by_group(g6[1]), NG, by_group(g6[2]), r1[:])
            BIG = 1.0e30
            inside = g6[2][:].unsqueeze(2).to_broadcast([P, NT * NG, EPG])
            k4 = lambda t: t[:].rearrange("p t (g k) -> p (t g) k", k=EPG)
            then(tt(k4(mb[0]), k4(bs), inside, ALU.mult))
            then(ts(g6[3][:], g6[2][:], BIG, -BIG, ALU.mult, ALU.add))
            then(tt(k4(mb[0]), k4(mb[0]), g6[3][:].unsqueeze(2).to_broadcast([P, NT * NG, EPG]), ALU.add))
            first_best(mb[0][:], irank, t16[:], NE, picks[:, 0], r1[:])
            then(nc.vector.scalar_tensor_tensor(out=mb[1][:], in0=picks[:, 0], scalar=-BIG, in1=mb[0][:], op0=ALU.mult, op1=ALU.add))
            first_best(mb[1][:], irank, t16[:], NE, picks[:, 1], r1[:])
            tt(member[:], picks[:, 0], picks[:, 1], ALU.add).then_inc(s_member, 1)

            def both(x):
                return x.unsqueeze(1).to_broadcast([P, 2, NT, NE])

            def pick(dst, table):
                for k in range(2):
                    then(tt(prod[:, k], picks[:, k], table, ALU.mult))
                then(nc.vector.tensor_reduce(dst, prod[:].rearrange("p a t e -> p (a t) e"), axis=AX, op=ALU.add))

            flat = lambda t: t[:].rearrange("p a t -> p (a t)")
            pick(flat(gate), sg[:])
            then(tt(r1[:], gate[:, 0, :], gate[:, 1, :], ALU.add))
            then(nc.vector.reciprocal(r2[:], r1[:]))
            then(tt(gate[:], gate[:], r2[:].unsqueeze(1).to_broadcast([P, 2, NT]), ALU.mult))
            pick(flat(exp_of), iexp[:].unsqueeze(1).to_broadcast(tne))
            dve.wait_ge(s_prefix, 1)
            then(nc.vector.tensor_copy(pos[:], psum[3][:, 0:NT * NE].rearrange("p (t e) -> p t e", t=NT)))
            then(ts(more[:], psum[4][:, 0:NE], 1.0, -1.0, ALU.max, ALU.add))
            then(nc.vector.tensor_copy(cnt_i[:], more[:]))
            then(nc.vector.tensor_single_scalar(cnt_i[:], cnt_i[:], 7, op=ALU.logical_shift_right))
            then(nc.vector.tensor_copy(more[:], cnt_i[:]))
            then(nc.vector.tensor_tensor_scan(out=upto[:], data0=ones[:, 0:NE], data1=more[:], initial=0.0, op0=ALU.mult, op1=ALU.add))
            then(tt(first_more[:], upto[:], more[:], ALU.subtract))
            then(tt(first_more[:], first_more[:], iexp[:], ALU.subtract))
            then(nc.vector.tensor_scalar_add(first_more[:], first_more[:], NE - 1.0))
            pick(flat(place), pos[:])
            then(nc.vector.tensor_copy(place_i[:], place[:]))
            then(nc.vector.tensor_single_scalar(place_i[:], place_i[:], 7, op=ALU.logical_shift_right))
            then(nc.vector.tensor_copy(blk[:], place_i[:]))
            then(nc.vector.scalar_tensor_tensor(out=flat(low), in0=flat(blk), scalar=-float(P), in1=flat(place), op0=ALU.mult, op1=ALU.add))
            pick(flat(tile_of), first_more[:].unsqueeze(1).to_broadcast(tne))
            then(tt(flat(tile_of), flat(tile_of), flat(blk), ALU.add))
            then(nc.vector.scalar_tensor_tensor(out=flat(tile_of), in0=flat(blk), scalar=0.5, in1=flat(tile_of), op0=ALU.is_gt, op1=ALU.mult))
            then(tt(flat(tile_of), flat(tile_of), flat(exp_of), ALU.add))
            for n in range(2 * NT):
                k, t = n // NT, n % NT
                if n >= 2:
                    dve.wait_ge(s_slots, n - 1)
                ts(hot[:, n % 2, :], i128[:], low[:, k, t:t + 1], None, ALU.is_equal)
                ts(vals[:, n % 2, 0, :], itile[:], tile_of[:, k, t:t + 1], tok1[:, t:t + 1], ALU.is_equal, ALU.mult)
                ts(vals[:, n % 2, 1, :], itile[:], tile_of[:, k, t:t + 1], gate[:, k, t:t + 1], ALU.is_equal, ALU.mult).then_inc(s_hot, 1)
            then(tt(le[:], upto[0:1, :].unsqueeze(1).to_broadcast([1, MAX_MORE + 1, NE]),
                    itile[0:1, 0:MAX_MORE + 1].unsqueeze(2).to_broadcast([1, MAX_MORE + 1, NE]), ALU.is_le))
            then(nc.vector.tensor_reduce(te_f[:, NE:MAX_TILES], le[:], axis=AX, op=ALU.add))
            then(nc.vector.tensor_copy(te_f[:, 0:NE], iexp[0:1, :]))
            then(nc.vector.tensor_scalar_min(te_f[:], te_f[:], NE - 1.0))
            then(nc.vector.tensor_copy(tile_expert[:], te_f[:]))
            then(nc.vector.tensor_copy(n_more_sb[:], upto[0:1, NE - 1:NE]))
            dve.wait_ge(s_slots, 2 * NT)
            then(nc.vector.tensor_copy(gate_tab[:], psum[5][:, MAX_TILES:2 * MAX_TILES]))
            then(ts(idx_f[:], psum[5][:, 0:MAX_TILES], 0.0, padrow[:], ALU.is_equal, ALU.mult))
            then(tt(idx_f[:], idx_f[:], psum[5][:, 0:MAX_TILES], ALU.add))
            then(nc.vector.tensor_scalar_add(idx_f[:], idx_f[:], -1.0))
            then(nc.vector.tensor_copy(idx_tab[:], idx_f[:]))

    wh_ = {X: [at(f"e{X}h{i}", kb + 4 * i, [P, 2 * FF], FR) for i in range(4)] for X, kb in (("G", 6), ("D", 38), ("U", 126))}
    wl_ = {X: [at(f"e{X}l{i}", kb + 4 * i, [P, 2 * FF], FR) for i in range(4)] for X, kb in (("G", 22), ("D", 54), ("U", 142))}
    xg = at("xg", 158, [P, D])
    xgT_h = at("xgT_h", 162, [P, KD, P], FR)
    xgT_l = at("xgT_l", 166, [P, KD, P], FR)
    gsil = at("gsil", 170, [P, FF])
    hid = at("hid", 172, [P, FF])
    hT_h = at("hT_h", 174, [P, FF], FR)
    hT_l = at("hT_l", 176, [P, FF], FR)
    yg = at("yg", 178, [P, D])
    idx_g = small("idx_g", [P, 1], I32)
    idx_s = small("idx_s", [P, 1], I32)
    gate_col = small("gate_col", [P, 1])

    s_hi = {X: sem(f"e{X}_high") for X in "GUD"}
    s_lo = {X: sem(f"e{X}_low") for X in "GUD"}
    s_used = {X: sem(f"e{X}_used") for X in "GUD"}
    used0 = {"G": 0, "U": 0, "D": 4}
    s_idxg, s_idxs, s_gcol = sem("gather_index"), sem("scatter_index"), sem("gate_column")
    s_gather, s_scatter = sem("rows_gathered"), sem("rows_added")
    s_tx, s_xh, s_xl = sem("xg_transposed"), sem("xgT_high"), sem("xgT_low")
    s_gated, s_silu, s_hid = sem("gate_product"), sem("silu"), sem("hidden")
    s_ht, s_hh, s_hl = sem("hidden_transposed"), sem("hT_high"), sem("hT_low")
    s_down, s_yg = sem("down_product"), sem("expert_rows")

    def n_tiles(eng):
        return eng.value_load(n_more_sb[0:1, 0:1], min_val=0, max_val=MAX_MORE) + NE

    with nc.Block() as block:

        @block.sync
        def _(sp):
            with sp.Fori(1, n_tiles(sp)) as t:
                e = sp.value_load(tile_expert[0:1, bass.ds(t, 1)], min_val=0, max_val=NE - 1)
                for X in "GUD":
                    for i in range(4):
                        sp.wait_ge(s_lo[X], 4 * t + i - 3)
                        sp.dma_start(unit_dst(X, i), unit_src(X, e, i)).then_inc(s_raw[X][i], 16)

        @block.tensor
        def _(pe):
            def turn_x(t):
                wait(pe, s_gather, 16 * t + 16)
                wait(pe, s_xl, 2 * t)
                for hf in range(2):
                    for j in range(4):
                        c = 4 * hf + j
                        last = nc.tensor.transpose(psum[4 + hf][:, j * P:(j + 1) * P], xg[:, c * P:(c + 1) * P], ident[:])
                    last.then_inc(s_tx, 1)

            def inner(X, t, units):
                out = psum["GU".index(X)][:]
                for i in units:
                    if i == 0:
                        wait(pe, s_silu if X == "G" else s_hid, t)
                    wait(pe, s_xl, 2 * t + 1 + i // 2)
                    wait(pe, s_lo[X], 4 * t + i + 1)
                    for j in range(2):
                        c, cs = 2 * i + j, slice(j * FF, (j + 1) * FF)
                        nc.tensor.matmul(out, xgT_h[:, c, :], wh_[X][i][:, cs], start=(c == 0), stop=False)
                        nc.tensor.matmul(out, xgT_l[:, c, :], wh_[X][i][:, cs], start=False, stop=False)
                        last = nc.tensor.matmul(out, xgT_h[:, c, :], wl_[X][i][:, cs], start=False, stop=(c == KD - 1))
                    last.then_inc(s_used[X], 1)

            def turn_h(t):
                wait(pe, s_hid, t + 1)
                wait(pe, s_hl, t)
                for j in range(4):
                    last = nc.tensor.transpose(psum[6][:, j * P:(j + 1) * P], hid[:, j * P:(j + 1) * P], ident[:])
                last.then_inc(s_ht, 1)

            def down(t):
                wait(pe, s_hl, t + 1)
                wait(pe, s_yg, t)
                for c in range(4):
                    wait(pe, s_lo["D"], 4 * t + c + 1)
                    cs = slice(c * P, (c + 1) * P)
                    for n in range(2):
                        out, ns = psum[2 + n][:], slice(n * FF, (n + 1) * FF)
                        nc.tensor.matmul(out, hT_h[:, cs], wh_["D"][c][:, ns], start=(c == 0), stop=False)
                        nc.tensor.matmul(out, hT_l[:, cs], wh_["D"][c][:, ns], start=False, stop=False)
                        last = nc.tensor.matmul(out, hT_h[:, cs], wl_["D"][c][:, ns], start=False, stop=(c == 3))
                    last.then_inc(s_used["D"], 1)

            pe.nop().then_inc(s_used["D"], used0["D"])
            turn_x(0)
            inner("G", 0, range(4))
            turn_x(1)
            inner("U", 0, range(4))
            count = n_tiles(pe)
            with pe.Fori(1, count) as t:
                inner("G", t, (0, 1))
                turn_h(t - 1)
                inner("G", t, (2, 3))
                down(t - 1)
                turn_x(t + 1)
                inner("U", t, range(4))
            turn_h(count - 1)
            down(count - 1)

        @block.scalar
        def _(act):
            def high(X, t):
                for i in range(4):
                    wait(act, s_raw[X][i], 16 * t + 16)
                    wait(act, s_used[X], used0[X] + 4 * t + i - 3)
                    nc.scalar.activation(wh_[X][i][:], raw[X][i][:], ACT.Copy).then_inc(s_hi[X], 1)

            def x_high(t):
                for hf in range(2):
                    wait(act, s_tx, 2 * t + hf + 1)
                    wait(act, s_used["U"], 4 * t - 2 + 2 * hf)
                    nc.scalar.activation(xgT_h[:, 4 * hf:4 * hf + 4, :], psum[4 + hf][:].rearrange("p (c n) -> p c n", c=4),
                                         ACT.Copy).then_inc(s_xh, 1)

            def silu(t):
                wait(act, s_used["G"], 4 * t + 4)
                wait(act, s_hid, t)
                nc.scalar.activation(gsil[:], psum[0][:], ACT.Silu).then_inc(s_silu, 1)

            def h_high(t):
                wait(act, s_ht, t + 1)
                wait(act, s_used["D"], used0["D"] + 4 * t)
                nc.scalar.activation(hT_h[:], psum[6][:], ACT.Copy).then_inc(s_hh, 1)

            def rows(t):
                wait(act, s_used["D"], used0["D"] + 4 * t + 4)
                wait(act, s_gcol, t + 1)
                wait(act, s_scatter, 16 * t)
                nc.scalar.activation(yg[:, 0:FF], psum[2][:], ACT.Copy, scale=gate_col[:])
                nc.scalar.activation(yg[:, FF:D], psum[3][:], ACT.Copy, scale=gate_col[:]).then_inc(s_yg, 1)

            high("G", 0)
            x_high(0)
            high("U", 0)
            silu(0)
            count = n_tiles(act)
            with act.Fori(1, count) as t:
                high("G", t)
                x_high(t)
                high("D", t - 1)
                h_high(t - 1)
                high("U", t)
                silu(t)
                rows(t - 1)
            high("D", count - 1)
            h_high(count - 1)
            rows(count - 1)

        @block.vector
        def _(dve):
            def low_part(X, t):
                for i in range(4):
                    wait(dve, s_hi[X], 4 * t + i + 1)
                    nc.vector.tensor_tensor(wl_[X][i][:], raw[X][i][:], f32(wh_[X][i][:]), ALU.subtract).then_inc(s_lo[X], 1)

            def x_low(t):
                for hf in range(2):
                    wait(dve, s_xh, 2 * t + hf + 1)
                    hs = slice(4 * hf, 4 * hf + 4)
                    nc.vector.tensor_tensor(xgT_l[:, hs, :], psum[4 + hf][:].rearrange("p (c n) -> p c n", c=4),
                                            f32(xgT_h[:, hs, :]), ALU.subtract).then_inc(s_xl, 1)

            def hidden(t):
                wait(dve, s_silu, t + 1)
                wait(dve, s_used["U"], 4 * t + 4)
                wait(dve, s_ht, t)
                nc.vector.tensor_tensor(hid[:], gsil[:], psum[1][:], ALU.mult).then_inc(s_hid, 1)

            def h_low(t):
                wait(dve, s_hh, t + 1)
                nc.vector.tensor_tensor(hT_l[:], psum[6][:], f32(hT_h[:]), ALU.subtract).then_inc(s_hl, 1)

            low_part("G", 0)
            x_low(0)
            low_part("U", 0)
            count = n_tiles(dve)
            with dve.Fori(1, count) as t:
                low_part("G", t)
                x_low(t)
                hidden(t - 1)
                low_part("D", t - 1)
                h_low(t - 1)
                low_part("U", t)
            hidden(count - 1)
            low_part("D", count - 1)
            h_low(count - 1)

        @block.gpsimd
        def _(pool):
            def gather(t):
                wait(pool, s_gather, 16 * t)
                nc.gpsimd.tensor_copy(idx_g[:], idx_tab[:, bass.ds(t, 1)]).then_inc(s_idxg, 1)
                wait(pool, s_idxg, t + 1)
                wait(pool, s_tx, 2 * t)
                pool.indirect_dma_start(out=xg[:], out_offset=None, in_=x1_rows,
                                        in_offset=bass.IndirectOffsetOnAxis(ap=idx_g[:, 0:1], axis=0),
                                        bounds_check=TOK + P - 1, oob_is_err=False).then_inc(s_gather, 16)

            def add_rows(t):
                wait(pool, s_yg, t)
                nc.gpsimd.tensor_copy(gate_col[:], gate_tab[:, bass.ds(t, 1)]).then_inc(s_gcol, 1)
                wait(pool, s_scatter, 16 * t)
                nc.gpsimd.tensor_copy(idx_s[:], idx_tab[:, bass.ds(t, 1)]).then_inc(s_idxs, 1)
                wait(pool, s_idxs, t + 1)
                wait(pool, s_yg, t + 1)
                pool.indirect_dma_start(out=acc_rows, out_offset=bass.IndirectOffsetOnAxis(ap=idx_s[:, 0:1], axis=0),
                                        in_=yg[:], in_offset=None, bounds_check=TOK + P - 1, oob_is_err=True,
                                        compute_op=ALU.add).then_inc(s_scatter, 16)

            gather(0)
            gather(1)
            count = n_tiles(pool)
            with pool.Fori(1, count) as t:
                gather(t + 1)
                add_rows(t - 1)
            add_rows(count - 1)
            pool.wait_ge(s_scatter, 16 * count)

    s_ln2w, s_var2, s_rstd2, s_y = sem("ln2_weights_landed"), sem("ln2_variance"), sem("ln2_rstd"), sem("y_ready")
    s_acc = [sem(f"acc_landed{t}") for t in range(NT)]
    s_out = sem("y_stored")
    ln2g_sb = at("ln2g_sb", 186, [P, D])
    ln2b_sb = at("ln2b_sb", 190, [P, D])

    with nc.Block() as block:

        @block.sync
        def _(sp):
            for t in range(NT):
                sp.dma_start(res[:, t, :], acc_rows[t * P:(t + 1) * P, :]).then_inc(s_acc[t], 16)
                if t == 0:
                    sp.dma_start(ln2g_sb[:], bcast(ln2_g[0], D)).then_inc(s_ln2w, 16)
                    sp.dma_start(ln2b_sb[:], bcast(ln2_b[0], D)).then_inc(s_ln2w, 16)
            for t in range(NT):
                sp.wait_ge(s_y, t + 1)
                dst = y_prompt[0, t * P:(t + 1) * P, :] if t < NT_P else y_sample[0, (t - NT_P) * P:(t - NT_P + 1) * P, :]
                sp.dma_start(dst, res[:, t, :]).then_inc(s_out, 16)
            sp.wait_ge(s_out, 16 * NT)

        @block.gpsimd
        def _(pool):
            for t in range(NT):
                pool.wait_ge(s_var2, t + 1)
                nc.gpsimd.tensor_tensor(rstd[:, t:t + 1], mv[:, t, 1:2], minus_half[:, 0:1], ALU.pow).then_inc(s_rstd2, 1)

        @block.vector
        def _(dve):
            for t in range(NT):
                dve.wait_ge(s_acc[t], 16)
                nc.vector.bn_stats(stats[:, t % 2, 0, :], res[:, t, 0:HW])
                then(nc.vector.bn_stats(stats[:, t % 2, 1, :], res[:, t, HW:D]))
                then(nc.vector.bn_aggr(mv[:, t, :], stats[:, t % 2, :, :].rearrange("p a b -> p (a b)")))
                nc.vector.tensor_scalar_add(mv[:, t, 1:2], mv[:, t, 1:2], LN_EPS).then_inc(s_var2, 1)
                if t == 0:
                    dve.wait_ge(s_ln2w, 32)
                then(nc.vector.scalar_tensor_tensor(out=res[:, t, :], in0=res[:, t, :], scalar=mv[:, t, 0:1], in1=ln2g_sb[:],
                                                    op0=ALU.subtract, op1=ALU.mult))
                dve.wait_ge(s_rstd2, t + 1)
                nc.vector.scalar_tensor_tensor(out=res[:, t, :], in0=res[:, t, :], scalar=rstd[:, t:t + 1], in1=ln2b_sb[:],
                                               op0=ALU.mult, op1=ALU.add).then_inc(s_y, 1)


def tables():
    import numpy as np

    pos = np.concatenate([np.arange(SEQ_P), np.arange(SEQ_S)]).astype(np.float32)
    inv = (1.0 / (np.float32(10000.0) ** (np.arange(0, ROPE, 2, dtype=np.float32) / np.float32(ROPE)))).astype(np.float32)
    ang = pos[:, None] * inv[None, :]
    by_tile = lambda a: np.ascontiguousarray(a.astype(np.float32).reshape(NT, P, HALF).transpose(1, 0, 2))
    dist = -np.abs(np.arange(P)[:, None] - (np.arange(ALIBI_W)[None, :] - (SEQ_P - P))).astype(np.float32)
    return {"rope_cos": by_tile(np.cos(ang)), "rope_sin": by_tile(np.sin(ang)), "alibi": dist}


_INS = ["x_prompt", "x_sample", "ln0_g", "ln0_b", "w_in", "g_q", "g_kv", "w_uq", "w_ukv", "lam_q1", "lam_k1",
        "lam_q2", "lam_k2", "g_sub", "w_o", "ln1_g", "ln1_b", "w_router", "b_router", "w_gate", "w_up",
        "w_down", "ln2_g", "ln2_b"]


def kernel(**inputs):
    import numpy as np
    import concourse.bacc as bacc
    from concourse.bass_utils import run_bass_kernel_spmd

    nc = bacc.Bacc("TRN2", target_bir_lowering=False, num_devices=1)
    arrays, args = {}, {}
    for name, a in [(n, inputs[n]) for n in _INS] + list(tables().items()):
        arrays[f"in_{name}"] = np.ascontiguousarray(a)
        args[name] = nc.dram_tensor(f"in_{name}", arrays[f"in_{name}"].shape, F, kind="ExternalInput").ap()
    for name, n in (("y_prompt", SEQ_P), ("y_sample", SEQ_S)):
        args[name] = nc.dram_tensor(name, (1, n, D), F, kind="ExternalOutput").ap()
    encoder_trunk(nc, **args)
    r = run_bass_kernel_spmd(nc, [arrays], core_ids=[0])
    return tuple(r.results[0][name] for name in ("y_prompt", "y_sample"))
```

```python
import math

import concourse.bass as bass
from concourse import mybir

F = mybir.dt.float32
FR = mybir.dt.float32r
I32 = mybir.dt.int32
ALU = mybir.AluOpType
ACT = mybir.ActivationFunctionType
AX = mybir.AxisListType.X

P = 128
D = 1024
KD = D // P
SEQ_P, SEQ_S = 512, 256
NT_P, NT_S = SEQ_P // P, SEQ_S // P
NT = NT_P + NT_S
TOK = NT * P
HEADS = 8
NOPE, ROPE, VDIM = 64, 32, 64
HALF = ROPE // 2
QK = NOPE + ROPE
QR, KVR = 256, 128
CW = QR + KVR + ROPE
DH = 4
DHD = 64
DW = DH * 2 * DHD
IN_W = CW + 3 * DW
NE, NG, EPG = 16, 4, 4
FF = 512
LN_EPS, RMS_EPS = 1e-5, 1e-6
ALPHA = 2.0 ** 0.25
LAM_INIT = 0.2
MLA_SCALE = QK ** -0.5
DIFF_SCALE = DHD ** -0.5
ALIBI_W = 2 * SEQ_P - P
SEQS = ((0, SEQ_P, NT_P), (SEQ_P, SEQ_S, NT_S))
MAX_MORE = (2 * TOK - 1) // P
MAX_TILES = NE + MAX_MORE + 1
KB = 1024


def encoder_trunk(nc, x_prompt, x_sample, ln0_g, ln0_b, w_in, g_q, g_kv, w_uq, w_ukv, lam_q1, lam_k1,
                  lam_q2, lam_k2, g_sub, w_o, ln1_g, ln1_b, w_router, b_router, w_gate, w_up, w_down,
                  ln2_g, ln2_b, rope_cos, rope_sin, alibi, y_prompt, y_sample):
    base = 16640
    used = [0]

    def at(name, kb, shape, dt=F):
        n = 1
        for s in shape[1:]:
            n *= s
        assert base + kb * KB + 4 * n <= nc.sbuf_usable_end, name
        return nc.alloc_sbuf_tensor_at(name, list(shape), dt, offset=base + int(kb * KB))

    def small(name, shape, dt=F):
        n = 4
        for s in shape[1:]:
            n *= s
        off = used[0]
        used[0] += (n + 31) // 32 * 32
        assert used[0] <= 6 * KB, name
        return nc.alloc_sbuf_tensor_at(name, list(shape), dt, offset=base + off)

    def sem(name):
        return nc.alloc_semaphore(name)

    def f32(ap):
        return ap.bitcast(F)

    def bcast(vec, n):
        return vec.rearrange("(a n) -> a n", a=1).to_broadcast([P, n])

    ident = small("ident", [P, P])
    cos = small("cos", [P, NT, HALF])
    sin = small("sin", [P, NT, HALF])
    minus_half = small("minus_half", [P, 2 * NT])
    gq_col = small("gq_col", [P, 3])
    gsub_col = small("gsub_col", [P, 1])
    lam_col = small("lam_col", [P, 1])
    res = at("res", 6, [P, NT, D])
    psum = [nc.alloc_psum_tensor(f"bank{i}", [P, 512], F) for i in range(8)]

    xT_h = at("xT_h", 30, [P, KD, TOK], FR)
    xT_l = at("xT_l", 54, [P, KD, TOK], FR)
    WB = 256
    w_raw = [at(f"w_raw{i}", 78 + 8 * i, [P, KD * WB]) for i in range(2)]
    w_h = [at(f"w_h{i}", 94 + 8 * i, [P, KD * WB], FR) for i in range(2)]
    w_l = [at(f"w_l{i}", 110 + 8 * i, [P, KD * WB], FR) for i in range(2)]
    dqT = at("dqT", 126, [P, DH, TOK])
    dkT = at("dkT", 138, [P, DH, TOK])
    dv = at("dv", 150, [P, NT, DW])
    cT_h = at("cT_h", 162, [P, 3, TOK], FR)
    cT_l = at("cT_l", 171, [P, 3, TOK], FR)
    craw = at("craw", 180, [P, NT, CW])
    ln_g = at("ln_g", 190, [P, D])
    ln_b = at("ln_b", 194, [P, D])
    junk = at("junk", 198, [P, QR])
    kr = at("kr", 199, [P, NT, ROPE])
    ropetmp = at("ropetmp", 200, [P, 4, HEADS, HALF])
    lam_in = at("lam_in", 202, [P, 4, DHD])
    lam_prod = at("lam_prod", 203, [P, 2, DHD])
    q_tok = at("q_tok", 30, [P, NT, HEADS, QK])
    k_tok = at("k_tok", 48, [P, NT, HEADS, QK])
    v_tok = at("v_tok", 66, [P, NT, HEADS, VDIM])
    stats = small("stats", [P, 2, 2, 6])
    mv = small("mv", [P, NT, 2])
    rstd = small("rstd", [P, NT])
    ssq = small("ssq", [P, 2, NT])
    rms = small("rms", [P, 2, NT])
    lam_e = small("lam_e", [P, 2])
    lam_s = small("lam_s", [P, 2])

    s_const = sem("const_landed")
    s_lam_in = sem("lam_landed")
    s_lnw = sem("ln_weights_landed")
    s_x = [sem(f"x_landed{t}") for t in range(NT)]
    s_w = [sem(f"w_landed{i}") for i in range(2)]
    s_ident = sem("ident_ready")
    s_var = sem("variance_ready")
    s_rstd = sem("rstd_ready")
    s_dve = sem("dve_step")
    s_pool = sem("pool_step")
    s_act = sem("act_step")
    s_xln = sem("xln_ready")
    s_tp = sem("transposed")
    s_th = sem("transposed_high")
    s_tl = sem("transposed_low")
    s_wh = sem("w_high")
    s_wl = sem("w_low")
    s_proj = sem("projected")
    s_pev = sem("projection_out")
    s_ssq = sem("square_sums_ready")
    s_rms = sem("rms_ready")
    s_kr = sem("k_rope_ready")
    s_lam = sem("lambda_parts")
    s_kfill = sem("k_rope_filled")

    dve_steps = [0]

    def then(ins):
        dve_steps[0] += 1
        ins.then_inc(s_dve, 1)
        nc.vector.wait_ge(s_dve, dve_steps[0])

    w_in_v = w_in[0].rearrange("(c p) n -> p c n", p=P)
    blocks = [(w_in_v[:, :, 0:QR], KD, QR), (w_in_v[:, :, QR:CW], KD, CW - QR)]
    for i in range(3 * DW // WB):
        blocks.append((w_in_v[:, :, CW + i * WB:CW + (i + 1) * WB], KD, WB))
    blocks.append((w_uq[0].rearrange("(c p) n -> p c n", p=P), QR // P, HEADS * QK))
    blocks.append((w_ukv[0].rearrange("(c p) n -> p c n", p=P), 1, HEADS * (NOPE + VDIM)))
    NB = len(blocks)
    UQ, UKV = NB - 2, NB - 1
    BANKS = 6

    def wview(t, b):
        _, c, n = blocks[b]
        return t[b % 2][:, 0:c * n].rearrange("p (c n) -> p c n", c=c)

    def groups(b):
        if b < 2:
            return [("c", b, t) for t in range(NT)]
        if b < 6:
            return [("qk", b, f, s) for f in range(2) for s in range(2)]
        if b < 8:
            return [("v", b, t) for t in range(NT)]
        return [("uq" if b == UQ else "ukv", b, t, hf) for t in range(NT) for hf in range(2)]

    order = [g for t in range(NT) for g in (("c", 0, t), ("c", 1, t))]
    for b in range(2, NB):
        order += groups(b)
    first_of = {b: next(i for i, g in enumerate(order) if g[1] == b) for b in range(NB)}
    last_of = {b: max(i for i, g in enumerate(order) if g[1] == b) for b in range(NB)}
    NX = 2 * NT

    def xhalf(t, hf, hi_lo):
        return hi_lo[:, 4 * hf:4 * hf + 4, t * P:(t + 1) * P]

    with nc.Block() as block:

        @block.sync
        def _(sp):
            def load_w(b):
                if b >= 2:
                    sp.wait_ge(s_wl, 2 * (b - 2) + 2)
                sp.dma_start(wview(w_raw, b), blocks[b][0]).then_inc(s_w[b % 2], 16)

            def load_x(t):
                src = x_prompt[0, t * P:(t + 1) * P, :] if t < NT_P else x_sample[0, (t - NT_P) * P:(t - NT_P + 1) * P, :]
                sp.dma_start(res[:, t, :], src).then_inc(s_x[t], 16)

            load_x(0)
            sp.dma_start(ln_g[:], bcast(ln0_g, D)).then_inc(s_lnw, 16)
            sp.dma_start(ln_b[:], bcast(ln0_b, D)).then_inc(s_lnw, 16)
            load_w(0)
            load_x(1)
            load_w(1)
            for t in range(2, NT):
                load_x(t)
            sp.dma_start(cos[:], rope_cos).then_inc(s_const, 16)
            sp.dma_start(sin[:], rope_sin).then_inc(s_const, 16)
            with nc.allow_non_contiguous_dma("a column of gains"):
                sp.dma_start(gq_col[:, 0:2], g_q[0].rearrange("(c p) -> p c", p=P)).then_inc(s_const, 16)
                sp.dma_start(gq_col[:, 2:3], g_kv[0].rearrange("(c p) -> p c", p=P)).then_inc(s_const, 16)
                sp.dma_start(gsub_col[:], g_sub[0].rearrange("(c p) -> p c", p=P)).then_inc(s_const, 16)
            for i, v in enumerate((lam_q1, lam_k1, lam_q2, lam_k2)):
                sp.dma_start(lam_in[:, i, :], bcast(v[0], DHD)).then_inc(s_lam_in, 16)
            for b in range(2, NB):
                load_w(b)

        @block.gpsimd
        def _(pool):
            nc.gpsimd.memset(ident[:], 0.0).then_inc(s_pool, 1)
            nc.gpsimd.memset(minus_half[:], -0.5).then_inc(s_pool, 1)
            pool.wait_ge(s_pool, 2)
            nc.gpsimd.affine_select(out=ident[:], in_=ident[:], compare_op=ALU.not_equal, fill=1.0, base=0,
                                    pattern=[[-1, P]], channel_multiplier=1).then_inc(s_ident, 1)
            for t in range(NT):
                pool.wait_ge(s_var, t + 1)
                nc.gpsimd.tensor_tensor(rstd[:, t:t + 1], mv[:, t, 1:2], minus_half[:, 0:1], ALU.pow).then_inc(s_rstd, 1)
            pool.wait_ge(s_ssq, 1)
            nc.gpsimd.tensor_tensor(rms[:].rearrange("p a t -> p (a t)"), ssq[:].rearrange("p a t -> p (a t)"),
                                    minus_half[:], ALU.pow).then_inc(s_rms, 1)
            pool.wait_ge(s_kr, 1)
            for t in range(NT):
                pool.wait_ge(s_pev, last_of[7] + 1)
                nc.gpsimd.tensor_copy(k_tok[:, t, :, NOPE:QK],
                                      kr[:, t, :].unsqueeze(1).to_broadcast([P, HEADS, ROPE])).then_inc(s_kfill, 1)

        @block.tensor
        def _(pe):
            def transpose_x(t):
                pe.wait_ge(s_xln, t + 1)
                for hf in range(2):
                    q = 2 * t + hf
                    if q >= 2:
                        pe.wait_ge(s_tl, q - 1)
                    for j in range(4):
                        c = 4 * hf + j
                        last = nc.tensor.transpose(psum[q % 2][:, j * P:(j + 1) * P], res[:, t, c * P:(c + 1) * P], ident[:])
                    last.then_inc(s_tp, 1)

            def transpose_c():
                pe.wait_ge(s_pev, last_of[1] + 1)
                q = NX
                for j in range(3):
                    for t0, _, nt in SEQS:
                        pe.wait_ge(s_tl, q - 1)
                        for i in range(nt):
                            last = nc.tensor.transpose(psum[q % 2][:, i * P:(i + 1) * P],
                                                       craw[:, t0 // P + i, j * P:(j + 1) * P], ident[:])
                        last.then_inc(s_tp, 1)
                        q += 1

            def product(o, out, pairs):
                if o >= BANKS:
                    pe.wait_ge(s_pev, o - BANKS + 1)
                n = 3 * len(pairs)
                i = 0
                for ah, al, bh, bl in pairs:
                    for a, b in ((ah, bh), (al, bh), (ah, bl)):
                        last = nc.tensor.matmul(out, a, b, start=(i == 0), stop=(i == n - 1))
                        i += 1
                return last

            pe.wait_ge(s_ident, 1)
            transpose_x(0)
            for o, g in enumerate(order):
                kind, b = g[0], g[1]
                _, kc, n = blocks[b]
                wh, wl = wview(w_h, b), wview(w_l, b)
                bank = psum[2 + o % BANKS]
                if kind == "c" and b == 0:
                    if g[2] + 1 < NT:
                        transpose_x(g[2] + 1)
                    pe.wait_ge(s_tl, 2 * g[2] + 2)
                if o == first_of[b]:
                    pe.wait_ge(s_wl, 2 * b + 2)
                if o == first_of[3]:
                    transpose_c()
                if o == first_of[UQ]:
                    pe.wait_ge(s_tl, NX + 6)
                if kind in ("c", "v"):
                    t = g[2]
                    ts = slice(t * P, (t + 1) * P)
                    last = product(o, bank[:, 0:n], [(xT_h[:, c, ts], xT_l[:, c, ts], wh[:, c, :], wl[:, c, :])
                                                     for c in range(kc)])
                elif kind == "qk":
                    t0, nn, _ = SEQS[g[3]]
                    fs, ts = slice(g[2] * P, (g[2] + 1) * P), slice(t0, t0 + nn)
                    last = product(o, bank[:, 0:nn], [(wh[:, c, fs], wl[:, c, fs], xT_h[:, c, ts], xT_l[:, c, ts])
                                                      for c in range(kc)])
                else:
                    t, hf = g[2], g[3]
                    ts, c0 = slice(t * P, (t + 1) * P), (0 if kind == "uq" else 2)
                    w = n // 2
                    last = product(o, bank[:, 0:w], [(cT_h[:, c0 + c, ts], cT_l[:, c0 + c, ts],
                                                      wh[:, c, hf * w:(hf + 1) * w], wl[:, c, hf * w:(hf + 1) * w])
                                                     for c in range(kc)])
                last.then_inc(s_proj, 1)

        @block.scalar
        def _(act):
            def x_high(t):
                for hf in range(2):
                    q = 2 * t + hf
                    act.wait_ge(s_tp, q + 1)
                    nc.scalar.activation(xhalf(t, hf, xT_h), psum[q % 2][:].rearrange("p (c n) -> p c n", c=4),
                                         ACT.Copy).then_inc(s_th, 1)

            def c_high():
                act.wait_ge(s_const, 5 * 16)
                q = NX
                for j in range(3):
                    for t0, nn, _ in SEQS:
                        act.wait_ge(s_tp, q + 1)
                        nc.scalar.activation(cT_h[:, j, t0:t0 + nn], psum[q % 2][:, 0:nn], ACT.Copy,
                                             scale=gq_col[:, j:j + 1]).then_inc(s_th, 1)
                        q += 1

            def w_high(b):
                act.wait_ge(s_w[b % 2], 16 * (b // 2 + 1))
                if b >= 2:
                    act.wait_ge(s_proj, last_of[b - 2] + 1)
                w = blocks[b][1] * blocks[b][2] // 2
                for hf in range(2):
                    nc.scalar.activation(w_h[b % 2][:, hf * w:(hf + 1) * w], w_raw[b % 2][:, hf * w:(hf + 1) * w],
                                         ACT.Copy).then_inc(s_wh, 1)

            def c_squares():
                act.wait_ge(s_pev, last_of[1] + 1)
                k = 0
                for t in range(NT):
                    for i, (lo, n) in enumerate(((0, QR), (QR, KVR))):
                        if k:
                            act.wait_ge(s_act, k)
                        nc.scalar.activation(junk[:, 0:n], craw[:, t, lo:lo + n], ACT.Square,
                                             accum_out=ssq[:, i, t:t + 1]).then_inc(s_act, 1)
                        k += 1

            def out(o):
                g = order[o]
                kind, b = g[0], g[1]
                bank = psum[2 + o % BANKS]
                act.wait_ge(s_proj, o + 1)
                if kind == "c":
                    t = g[2]
                    lo, n = (0, QR) if b == 0 else (QR, CW - QR)
                    nc.scalar.activation(craw[:, t, lo:lo + n], bank[:, 0:n], ACT.Copy).then_inc(s_pev, 1)
                elif kind == "qk":
                    h = 2 * (b - 2) + g[2]
                    t0, nn, _ = SEQS[g[3]]
                    dst = dqT[:, h, t0:t0 + nn] if h < DH else dkT[:, h - DH, t0:t0 + nn]
                    nc.scalar.activation(dst, bank[:, 0:nn], ACT.Copy,
                                         scale=DIFF_SCALE if h < DH else 1.0).then_inc(s_pev, 1)
                elif kind == "v":
                    nc.scalar.activation(dv[:, g[2], (b - 6) * WB:(b - 5) * WB], bank[:, 0:WB], ACT.Copy).then_inc(s_pev, 1)
                elif kind == "uq":
                    t, hf = g[2], g[3]
                    nc.scalar.activation(q_tok[:, t, 4 * hf:4 * hf + 4, :],
                                         bank[:, 0:4 * QK].rearrange("p (h n) -> p h n", h=4),
                                         ACT.Copy, scale=rms[:, 0, t:t + 1]).then_inc(s_pev, 1)
                else:
                    t, hf = g[2], g[3]
                    kv = bank[:].rearrange("p (h n) -> p h n", h=4)
                    nc.scalar.activation(k_tok[:, t, 4 * hf:4 * hf + 4, 0:NOPE], kv[:, :, 0:NOPE], ACT.Copy,
                                         scale=rms[:, 1, t:t + 1])
                    nc.scalar.activation(v_tok[:, t, 4 * hf:4 * hf + 4, :], kv[:, :, NOPE:NOPE + VDIM], ACT.Copy,
                                         scale=rms[:, 1, t:t + 1]).then_inc(s_pev, 1)

            w_high(0)
            x_high(0)
            w_high(1)
            for o, g in enumerate(order):
                b = g[1]
                if g[0] == "c" and b == 0 and g[2] + 1 < NT:
                    x_high(g[2] + 1)
                out(o)
                if o == last_of[1]:
                    w_high(2)
                    c_squares()
                    act.wait_ge(s_lam, 1)
                    nc.scalar.activation(lam_e[:], lam_s[:], ACT.Exp).then_inc(s_lam, 1)
                    w_high(3)
                elif o == last_of[b] and b + 2 < NB and b >= 2:
                    w_high(b + 2)
                if o == last_of[2]:
                    c_high()
                    act.wait_ge(s_rms, 2)

        @block.vector
        def _(dve):
            def ln_stats(t):
                dve.wait_ge(s_x[t], 16)
                for i in range(2):
                    last = nc.vector.bn_stats(stats[:, t % 2, i, :], res[:, t, i * 512:(i + 1) * 512])
                    then(last)
                then(nc.vector.bn_aggr(mv[:, t, :], stats[:, t % 2, :, :].rearrange("p a b -> p (a b)")))
                nc.vector.tensor_scalar_add(mv[:, t, 1:2], mv[:, t, 1:2], LN_EPS).then_inc(s_var, 1)

            def ln_apply(t):
                if t == 0:
                    dve.wait_ge(s_lnw, 32)
                then(nc.vector.scalar_tensor_tensor(out=res[:, t, :], in0=res[:, t, :], scalar=mv[:, t, 0:1], in1=ln_g[:],
                                                    op0=ALU.subtract, op1=ALU.mult))
                dve.wait_ge(s_rstd, t + 1)
                nc.vector.scalar_tensor_tensor(out=res[:, t, :], in0=res[:, t, :], scalar=rstd[:, t:t + 1], in1=ln_b[:],
                                               op0=ALU.mult, op1=ALU.add).then_inc(s_xln, 1)

            def x_low(t):
                for hf in range(2):
                    q = 2 * t + hf
                    dve.wait_ge(s_th, q + 1)
                    nc.vector.tensor_tensor(xhalf(t, hf, xT_l), psum[q % 2][:].rearrange("p (c n) -> p c n", c=4),
                                            f32(xhalf(t, hf, xT_h)), ALU.subtract).then_inc(s_tl, 1)

            def w_low(b):
                w = blocks[b][1] * blocks[b][2] // 2
                for hf in range(2):
                    dve.wait_ge(s_wh, 2 * b + hf + 1)
                    nc.vector.tensor_tensor(w_l[b % 2][:, hf * w:(hf + 1) * w], w_raw[b % 2][:, hf * w:(hf + 1) * w],
                                            f32(w_h[b % 2][:, hf * w:(hf + 1) * w]), ALU.subtract).then_inc(s_wl, 1)

            def rotate(x1, x2, c, s, shape):
                a = [ropetmp[:, i] for i in range(4)] if shape == "heads" else [
                    ropetmp[:, i].rearrange("p h n -> p (h n)")[:, 0:NT * HALF].rearrange("p (t n) -> p t n", n=HALF)
                    for i in range(4)]
                nc.vector.tensor_tensor(a[0], x1, c, ALU.mult)
                nc.vector.tensor_tensor(a[1], x2, s, ALU.mult)
                nc.vector.tensor_tensor(a[2], x2, c, ALU.mult)
                then(nc.vector.tensor_tensor(a[3], x1, s, ALU.mult))
                nc.vector.tensor_tensor(x1 if shape == "heads" else kr[:, :, 0:HALF], a[0], a[1], ALU.subtract)
                return nc.vector.tensor_tensor(x2 if shape == "heads" else kr[:, :, HALF:ROPE], a[2], a[3], ALU.add)

            ln_stats(0)
            ln_apply(0)
            w_low(0)
            w_low(1)
            for t in range(NT):
                if t + 1 < NT:
                    ln_stats(t + 1)
                x_low(t)
                if t + 1 < NT:
                    ln_apply(t + 1)
            dve.wait_ge(s_lam_in, 64)
            lv = lam_in[:].rearrange("p (a b) n -> p a b n", b=2)
            then(nc.vector.tensor_tensor(lam_prod[:], lv[:, :, 0, :], lv[:, :, 1, :], ALU.mult))
            nc.vector.reduce_sum(lam_s[:], lam_prod[:], axis=AX).then_inc(s_lam, 1)
            w_low(2)
            dve.wait_ge(s_act, 2 * NT)
            nc.vector.tensor_scalar(ssq[:, 0, :], ssq[:, 0, :], 1.0 / QR, RMS_EPS, ALU.mult, ALU.add)
            nc.vector.tensor_scalar(ssq[:, 1, :], ssq[:, 1, :], 1.0 / KVR, RMS_EPS, ALU.mult, ALU.add).then_inc(s_ssq, 1)
            dve.wait_ge(s_lam, 2)
            then(nc.vector.tensor_tensor(lam_col[:], lam_e[:, 0:1], lam_e[:, 1:2], ALU.subtract))
            then(nc.vector.tensor_scalar_add(lam_col[:], lam_col[:], LAM_INIT))
            w_low(3)
            dve.wait_ge(s_rms, 1)
            nc.vector.tensor_scalar_mul(rms[:, 0, :], rms[:, 0, :], MLA_SCALE).then_inc(s_rms, 1)
            dve.wait_ge(s_const, 5 * 16)
            nc.vector.tensor_scalar_mul(gsub_col[:], gsub_col[:], 1.0 - LAM_INIT)
            rotate(craw[:, :, QR + KVR:QR + KVR + HALF], craw[:, :, QR + KVR + HALF:CW], cos[:], sin[:], "kr").then_inc(s_kr, 1)
            q = NX
            for j in range(3):
                for t0, nn, _ in SEQS:
                    dve.wait_ge(s_th, q + 1)
                    nc.vector.scalar_tensor_tensor(out=cT_l[:, j, t0:t0 + nn], in0=psum[q % 2][:, 0:nn],
                                                   scalar=gq_col[:, j:j + 1], in1=f32(cT_h[:, j, t0:t0 + nn]),
                                                   op0=ALU.mult, op1=ALU.subtract).then_inc(s_tl, 1)
                    q += 1
            for b in range(4, NB):
                w_low(b)
            for t in range(NT):
                dve.wait_ge(s_pev, first_of[UQ] + 2 * t + 2)
                then(rotate(q_tok[:, t, :, NOPE:NOPE + HALF], q_tok[:, t, :, NOPE + HALF:QK],
                            cos[:, t, :].unsqueeze(1).to_broadcast([P, HEADS, HALF]),
                            sin[:, t, :].unsqueeze(1).to_broadcast([P, HEADS, HALF]), "heads"))

    def wait(eng, semaphore, value):
        if not isinstance(value, int) or value > 0:
            eng.wait_ge(semaphore, value)
            if eng is nc.gpsimd and not isinstance(value, int):
                eng.sem_inc(s_passed, 1)

    s_passed = sem("passed_wait")

    def over(eng, n, body):
        body(0, True, False)
        with eng.Fori(1, n - 1) as i:
            body(i, False, False)
        body(n - 1, False, True)

    AHEAD, BEHIND = 4, 4
    mixD_h = at("mixD_h", 162, [P, DH, TOK], FR)
    mixD_l = at("mixD_l", 174, [P, DH, TOK], FR)
    q_h = [[at(f"q_h{x}{m}", 78 + 6 * m + 4 * x, [P, SEQS[x][1]], FR) for m in range(2)] for x in range(2)]
    q_l = [[at(f"q_l{x}{m}", 80 + 6 * m + 3 * x, [P, SEQS[x][1]], FR) for m in range(2)] for x in range(2)]
    kk_h = [at(f"kk_h{x}", 90 + 4 * x, [P, SEQS[x][1]], FR) for x in range(2)]
    kk_l = [at(f"kk_l{x}", 92 + 3 * x, [P, SEQS[x][1]], FR) for x in range(2)]
    vv_h = [at(f"vv_h{x}", 96 + 4 * x, [P, SEQS[x][2], P], FR) for x in range(2)]
    vv_l = [at(f"vv_l{x}", 98 + 3 * x, [P, SEQS[x][2], P], FR) for x in range(2)]
    dpT_h = [at(f"dpT_h{i}", 102 + 4 * i, [P, 512], FR) for i in range(2)]
    dpT_l = [at(f"dpT_l{i}", 104 + 4 * i, [P, 512], FR) for i in range(2)]
    o_sb = [at(f"o_sb{i}", 110 + 0.5 * i, [P, P]) for i in range(2)]
    o_junk = at("o_junk", 111, [P, P])
    bias_t = at("bias_t", 112, [P, ALIBI_W])
    NEE = 3
    ee = [[at(f"ee{i}{m}", 186 + 4 * i + 2 * m, [P, 512]) for m in range(2)] for i in range(NEE)]
    pp = [at(f"pp{i}", 198 + 2 * i, [P, 512]) for i in range(2)]
    negmax = small("negmax", [P, NEE, 2])
    esum = small("esum", [P, NEE, 2])
    erec = small("erec", [P, NEE, 2])
    osq = small("osq", [P, 2])
    orstd = small("orstd", [P, 2])

    s_alibi = sem("alibi_landed")
    s_zero = sem("zero_rows_ready")
    s_qkh, s_qkl = sem("diff_qk_high"), sem("diff_qk_low")
    s_vh, s_vl = sem("diff_v_high"), sem("diff_v_low")
    s_sc, s_bias, s_exp = sem("diff_scores"), sem("diff_biased"), sem("diff_exp")
    s_rec, s_e2, s_p = sem("diff_reciprocals"), sem("diff_second_scaled"), sem("diff_probs")
    s_pt, s_pth, s_ptl = sem("diff_probs_T"), sem("diff_probs_T_high"), sem("diff_probs_T_low")
    s_pv, s_sq, s_or = sem("diff_out"), sem("diff_out_squares"), sem("diff_out_rstd")
    s_osb, s_ot, s_oth, s_otl = sem("diff_out_normed"), sem("diff_out_T"), sem("mixD_high"), sem("mixD_low")

    def dtile(i):
        x = int(i >= NT_P)
        return x, SEQS[x][1], SEQS[x][2], i - NT_P * x

    def on_tile(n, slot, first, last, h, work, distance):
        j = slot + distance
        if not (first and j < 0) and not (last and j >= n):
            work(h + j // n, j % n)

    def cuts(i, last, h, *work):
        for slots, cut in work:
            if i in slots and not (last and slots[i][0]):
                cut(h + slots[i][0], slots[i][1])

    def stage(hp, k):
        x = k % 2
        t0, _, nt = SEQS[x]
        for dst, src in ((stage_q, q_tok), (stage_k, k_tok)):
            last = nc.gpsimd.tensor_copy(dst[x][:].unsqueeze(2), src[:, t0 // P:t0 // P + nt, bass.ds(2 * hp + k // 2, 1), :])
        last.then_inc(m_stage, 1)

    stage_q = [at(f"stage_q{x}", 202 + 3 * x, [P, SEQS[x][2], QK]) for x in range(2)]
    stage_k = [at(f"stage_k{x}", 203.5 + 2.25 * x, [P, SEQS[x][2], QK]) for x in range(2)]
    m_stage = sem("mla_staged")

    def head_slots(first, last):
        return range(-AHEAD if first else 0, NT + (BEHIND if last else 0))

    def g_of(h, i):
        return h * NT + i

    QK_HIGH, QK_LOW = {0: (1, 0), 3: (1, 1)}, {1: (1, 0), 4: (1, 1)}
    V_HIGH, V_LOW = {5: (1, 0), 2: (0, 1)}, {0: (0, 0), 3: (0, 1)}

    turned_probs, turned_out = psum[4], psum[5][:, 0:P]

    def out_bank(i):
        return psum[6 + i % 2][:, 0:P]

    with nc.Block() as block:

        @block.sync
        def _(sp):
            sp.dma_start(bias_t[:], alibi).then_inc(s_alibi, 16)

        @block.tensor
        def _(pe):
            def scores(h, i):
                x, n, _, qt = dtile(i)
                g = g_of(h, i)
                if qt == 0:
                    wait(pe, s_qkl, 6 * h + 3 * x + 3)
                for m in range(2):
                    wait(pe, s_bias, 2 * g - 4 + m + 1)
                    qs = slice(qt * P, (qt + 1) * P)
                    out = psum[2 * (i % 2) + m][:, 0:n]
                    nc.tensor.matmul(out, q_h[x][m][:, qs], kk_h[x][:], start=True, stop=False)
                    nc.tensor.matmul(out, q_l[x][m][:, qs], kk_h[x][:], start=False, stop=False)
                    nc.tensor.matmul(out, q_h[x][m][:, qs], kk_l[x][:], start=False, stop=True).then_inc(s_sc, 1)

            def turn_probs(h, i):
                g = g_of(h, i)
                wait(pe, s_p, g + 1)
                wait(pe, s_ptl, g)
                for j in range(dtile(i)[2]):
                    t = nc.tensor.transpose(turned_probs[:, j * P:(j + 1) * P], pp[i % 2][:, j * P:(j + 1) * P], ident[:])
                t.then_inc(s_pt, 1)

            def output(h, i):
                x, _, nk, qt = dtile(i)
                g = g_of(h, i)
                wait(pe, s_ptl, g + 1)
                wait(pe, s_osb, g - 1)
                if qt == 0:
                    wait(pe, s_vl, 2 * h + x + 1)
                k = 0
                for j in range(nk):
                    js = slice(j * P, (j + 1) * P)
                    for a, b in ((dpT_h, vv_h), (dpT_l, vv_h), (dpT_h, vv_l)):
                        t = nc.tensor.matmul(out_bank(i), a[i % 2][:, js], b[x][:, j, :],
                                             start=(k == 0), stop=(k == 3 * nk - 1))
                        k += 1
                t.then_inc(s_pv, 1)

            def turn_output(h, i):
                g = g_of(h, i)
                wait(pe, s_osb, g + 1)
                wait(pe, s_otl, g)
                nc.tensor.transpose(turned_out, o_sb[i % 2][:], ident[:]).then_inc(s_ot, 1)

            def head(h, first, last):
                for i in head_slots(first, last):
                    on_tile(NT, i, first, last, h, turn_probs, 0)
                    on_tile(NT, i, first, last, h, scores, 4)
                    on_tile(NT, i, first, last, h, output, -1)
                    on_tile(NT, i, first, last, h, turn_output, -3)

            pe.wait_ge(s_zero, 4)
            over(pe, DH, head)

        @block.scalar
        def _(act):
            def cut_qk(h, x):
                t0, n, _ = SEQS[x]
                wait(act, s_sc, 2 * g_of(h, (NT_P - 1, NT - 1)[x] - NT) + 2)
                for m in range(2):
                    r = slice(64 * m, 64 * m + 64)
                    nc.scalar.activation(q_h[x][m][r, :], dqT[r, h, t0:t0 + n], ACT.Copy).then_inc(s_qkh, 1)
                nc.scalar.activation(kk_h[x][:], dkT[:, h, t0:t0 + n], ACT.Copy).then_inc(s_qkh, 1)

            def cut_v(h, x):
                t0, _, nt = SEQS[x]
                wait(act, s_pv, g_of(h, (NT_P - 1, NT - 1)[x] - NT) + 1)
                nc.scalar.activation(vv_h[x][:], dv[:, t0 // P:t0 // P + nt, bass.ds(h * P, P)], ACT.Copy).then_inc(s_vh, 1)

            def exp(h, i):
                n = dtile(i)[1]
                for m in range(2):
                    wait(act, s_bias, 2 * g_of(h, i) + m + 1)
                    e = ee[i % NEE][m][:, 0:n]
                    nc.scalar.activation(e, e, ACT.Exp, scale=-1.0, bias=negmax[:, i % NEE, m:m + 1],
                                         accum_out=esum[:, i % NEE, m:m + 1]).then_inc(s_exp, 1)

            def probs_high(h, i):
                g = g_of(h, i)
                n = dtile(i)[1]
                wait(act, s_pt, g + 1)
                wait(act, s_pv, g - 1)
                nc.scalar.activation(dpT_h[i % 2][:, 0:n], turned_probs[:, 0:n], ACT.Copy).then_inc(s_pth, 1)

            def squares(h, i):
                g = g_of(h, i)
                wait(act, s_pv, g + 1)
                wait(act, s_sq, g)
                nc.scalar.activation(o_junk[:], out_bank(i), ACT.Square, scale=P ** -0.5,
                                     accum_out=osq[:, i % 2:i % 2 + 1]).then_inc(s_sq, 1)

            def normed(h, i):
                g = g_of(h, i)
                wait(act, s_or, 2 * g + 2)
                wait(act, s_ot, g - 1)
                nc.scalar.activation(o_sb[i % 2][:], out_bank(i), ACT.Copy, scale=orstd[:, i % 2:i % 2 + 1]).then_inc(s_osb, 1)

            def mix_high(h, i):
                wait(act, s_ot, g_of(h, i) + 1)
                nc.scalar.activation(mixD_h[:, h, i * P:(i + 1) * P], turned_out, ACT.Copy, scale=gsub_col[:]).then_inc(s_oth, 1)

            def head(h, first, last):
                for i in head_slots(first, last):
                    on_tile(NT, i, first, last, h, squares, -2)
                    on_tile(NT, i, first, last, h, mix_high, -4)
                    on_tile(NT, i, first, last, h, probs_high, 0)
                    on_tile(NT, i, first, last, h, exp, 3)
                    on_tile(NT, i, first, last, h, normed, -2)
                    cuts(i, last, h, (QK_HIGH, cut_qk), (V_HIGH, cut_v))

            cut_qk(0, 0)
            cut_qk(0, 1)
            cut_v(0, 0)
            over(act, DH, head)

        @block.gpsimd
        def _(pool):
            for x in range(2):
                for m in range(2):
                    r = slice(64 - 64 * m, 128 - 64 * m)
                    nc.gpsimd.memset(f32(q_h[x][m][r, :]), 0.0)
                    nc.gpsimd.memset(f32(q_l[x][m][r, :]), 0.0).then_inc(s_zero, 1)

            def second(h, i):
                wait(pool, s_rec, g_of(h, i) + 1)
                e = ee[i % NEE][1][:, 0:dtile(i)[1]]
                nc.gpsimd.tensor_scalar(e, e, erec[:, i % NEE, 1:2], lam_col[:], ALU.mult, ALU.mult).then_inc(s_e2, 1)

            def rstd_of(h, i):
                wait(pool, s_sq, g_of(h, i) + 1)
                o = orstd[:, i % 2:i % 2 + 1]
                nc.gpsimd.tensor_scalar_add(o, osq[:, i % 2:i % 2 + 1], LN_EPS).then_inc(s_or, 1)
                wait(pool, s_or, 2 * g_of(h, i) + 1)
                nc.gpsimd.tensor_tensor(o, o, minus_half[:, 0:1], ALU.pow).then_inc(s_or, 1)

            def head(h, first, last):
                for i in head_slots(first, last):
                    on_tile(NT, i, first, last, h, rstd_of, -2)
                    on_tile(NT, i, first, last, h, second, 2)

            pool.wait_ge(s_zero, 4)
            stage(0, 0)
            stage(0, 1)
            over(pool, DH, head)

        @block.vector
        def _(dve):
            s_in = sem("bias_table_ready")

            def cut_qk(h, x):
                t0, n, _ = SEQS[x]
                for m in range(2):
                    r = slice(64 * m, 64 * m + 64)
                    wait(dve, s_qkh, 6 * h + 3 * x + m + 1)
                    nc.vector.tensor_tensor(q_l[x][m][r, :], dqT[r, h, t0:t0 + n], f32(q_h[x][m][r, :]), ALU.subtract).then_inc(s_qkl, 1)
                wait(dve, s_qkh, 6 * h + 3 * x + 3)
                nc.vector.tensor_tensor(kk_l[x][:], dkT[:, h, t0:t0 + n], f32(kk_h[x][:]), ALU.subtract).then_inc(s_qkl, 1)

            def cut_v(h, x):
                t0, _, nt = SEQS[x]
                wait(dve, s_vh, 2 * h + x + 1)
                nc.vector.tensor_tensor(vv_l[x][:], dv[:, t0 // P:t0 // P + nt, bass.ds(h * P, P)],
                                        f32(vv_h[x][:]), ALU.subtract).then_inc(s_vl, 1)

            def biased(h, i):
                x, n, _, qt = dtile(i)
                if i == 0:
                    wait(dve, s_bias, 2 * g_of(h, 0))
                    nc.vector.tensor_scalar_mul(bias_t[:], bias_t[:], 0.25).then_inc(s_in, 1)
                    wait(dve, s_in, h + 1)
                wait(dve, s_p, g_of(h, i) - NEE + 1)
                for m in range(2):
                    wait(dve, s_sc, 2 * g_of(h, i) + m + 1)
                    dve.sem_inc(s_passed, 1)
                    lo = SEQ_P - P - qt * P
                    nc.vector.tensor_tensor_reduce(out=ee[i % NEE][m][:, 0:n], in0=psum[2 * (i % 2) + m][:, 0:n],
                                                   in1=bias_t[:, lo:lo + n], scale=-1.0, scalar=3.0e38, op0=ALU.add,
                                                   op1=ALU.min, accum_out=negmax[:, i % NEE, m:m + 1]).then_inc(s_bias, 1)

            def reciprocals(h, i):
                g = g_of(h, i)
                wait(dve, s_exp, 2 * g + 2)
                nc.vector.reciprocal(erec[:, i % NEE, :], esum[:, i % NEE, :]).then_inc(s_rec, 1)

            def probs(h, i):
                n = dtile(i)[1]
                g = g_of(h, i)
                wait(dve, s_e2, g + 1)
                wait(dve, s_pt, g - 1)
                nc.vector.scalar_tensor_tensor(out=pp[i % 2][:, 0:n], in0=ee[i % NEE][0][:, 0:n], scalar=erec[:, i % NEE, 0:1],
                                               in1=ee[i % NEE][1][:, 0:n], op0=ALU.mult, op1=ALU.subtract).then_inc(s_p, 1)

            def probs_low(h, i):
                n = dtile(i)[1]
                wait(dve, s_pth, g_of(h, i) + 1)
                nc.vector.tensor_tensor(dpT_l[i % 2][:, 0:n], turned_probs[:, 0:n], f32(dpT_h[i % 2][:, 0:n]),
                                        ALU.subtract).then_inc(s_ptl, 1)

            def mix_low(h, i):
                wait(dve, s_oth, g_of(h, i) + 1)
                ts = slice(i * P, (i + 1) * P)
                nc.vector.scalar_tensor_tensor(out=mixD_l[:, h, ts], in0=turned_out, scalar=gsub_col[:],
                                               in1=f32(mixD_h[:, h, ts]), op0=ALU.mult, op1=ALU.subtract).then_inc(s_otl, 1)

            def head(h, first, last):
                for i in head_slots(first, last):
                    on_tile(NT, i, first, last, h, biased, 3)
                    on_tile(NT, i, first, last, h, probs_low, 0)
                    on_tile(NT, i, first, last, h, probs, 1)
                    on_tile(NT, i, first, last, h, mix_low, -4)
                    cuts(i, last, h, (QK_LOW, cut_qk), (V_LOW, cut_v))
                    on_tile(NT, i, first, last, h, reciprocals, 2)

            cut_qk(0, 0)
            cut_qk(0, 1)
            dve.wait_ge(s_alibi, 16)
            over(dve, DH, head)

    TP = 2 * NT
    M_AHEAD, M_BEHIND = 4, 2
    START = (0, NT_P, NT, NT + NT_P)
    mixM_h = at("mixM_h", 126, [P, HEADS // 2, TOK], FR)
    mixM_l = at("mixM_l", 138, [P, HEADS // 2, TOK], FR)
    mq_h = [at(f"mq_h{x}", 83 + 8 * x, [P, SEQS[x][1]], FR) for x in range(2)]
    mq_l = [at(f"mq_l{x}", 85 + 7 * x, [P, SEQS[x][1]], FR) for x in range(2)]
    mk_h = [at(f"mk_h{x}", 87 + 6 * x, [P, SEQS[x][1]], FR) for x in range(2)]
    mk_l = [at(f"mk_l{x}", 89 + 5 * x, [P, SEQS[x][1]], FR) for x in range(2)]
    mv_h = [at(f"mv_h{x}", 95 + 4 * x, [P, SEQS[x][2], P], FR) for x in range(2)]
    mv_l = [at(f"mv_l{x}", 97 + 3 * x, [P, SEQS[x][2], P], FR) for x in range(2)]
    pT_h = [at(f"pT_h{x}", 102 + 16 * x, [P, SEQS[x][2], SEQS[x][1]], FR) for x in range(2)]
    pT_l = [at(f"pT_l{x}", 110 + 10 * x, [P, SEQS[x][2], SEQS[x][1]], FR) for x in range(2)]
    NME = 4
    me = [at(f"me{i}", 186 + 2 * i, [P, 512]) for i in range(NME)]
    mmax = small("mmax", [P, 2])
    msum = small("msum", [P, 2])
    mrec = small("mrec", [P, 2])

    m_tq = sem("mla_qk_T")
    m_qh, m_ql = sem("mla_qk_high"), sem("mla_qk_low")
    m_vh, m_vl = sem("mla_v_high"), sem("mla_v_low")
    m_sc, m_max, m_exp, m_rec = sem("mla_scores"), sem("mla_max"), sem("mla_exp"), sem("mla_reciprocal")
    m_p = [sem("mla_even_probs"), sem("mla_odd_probs")]
    m_pt, m_pth, m_ptl = sem("mla_probs_T"), sem("mla_probs_T_high"), sem("mla_probs_T_low")
    m_pv, m_mh, m_ml = sem("mla_out"), sem("mixM_high"), sem("mixM_low")

    def mtile(i):
        k = max(j for j in range(4) if START[j] <= i)
        x = k % 2
        return k, x, SEQS[x][1], SEQS[x][2], i - START[k]

    def pair_slots(first, last):
        return range(-M_AHEAD if first else 0, TP + (M_BEHIND if last else 0))

    STAGE_SLOTS = {2: (1, 0), 6: (1, 1), 8: (1, 2), 0: (0, 3)}
    TURN_SLOTS = {6: (1, 0), 10: (1, 1), 0: (0, 2), 4: (0, 3)}
    V_SLOTS = {0: (0, 0), 2: (0, 1)}
    PV_SLOTS = {4: (0, 0, (0, 1)), 5: (0, 0, (2, 3)), 6: (0, 1, (0, 1)), 10: (0, 2, (0, 1)), 11: (0, 2, (2, 3)),
                0: (-1, 3, (0, 1))}
    MIX_SLOTS = {6: (0, 0), 7: (0, 1), 0: (-1, 2), 1: (-1, 3)}

    def at_slot(slots, i, first, last, hp, f):
        if i >= 0 and i % TP in slots:
            d, *rest = slots[i % TP]
            d += i // TP
            if not (first and d < 0) and not (last and d > 0):
                f(hp + d, *rest)

    def unit_last(w_pair, k):
        return w_pair * TP + (START[k + 1] if k < 3 else TP) - 1

    with nc.Block() as block:

        @block.tensor
        def _(pe):
            def turn(hp, k):
                x = k % 2
                w = 4 * hp + k
                wait(pe, m_stage, w + 1)
                wait(pe, m_ql, 2 * w)
                for bank, src in ((4, stage_q), (5, stage_k)):
                    for t in range(SEQS[x][2]):
                        last = nc.tensor.transpose(psum[bank][0:QK, t * P:(t + 1) * P], src[x][:, t, :], ident[:])
                    last.then_inc(m_tq, 1)

            def scores(hp, i):
                k, x, n, _, qt = mtile(i)
                g = hp * TP + i
                if qt == 0:
                    wait(pe, m_ql, 8 * hp + 2 * k + 2)
                wait(pe, m_exp, g - 1)
                qs = slice(qt * P, (qt + 1) * P)
                out = psum[i % 2][:, 0:n]
                nc.tensor.matmul(out, mq_h[x][0:QK, qs], mk_h[x][0:QK, :], start=True, stop=False)
                nc.tensor.matmul(out, mq_l[x][0:QK, qs], mk_h[x][0:QK, :], start=False, stop=False)
                nc.tensor.matmul(out, mq_h[x][0:QK, qs], mk_l[x][0:QK, :], start=False, stop=True).then_inc(m_sc, 1)

            def turn_probs(hp, i):
                g = hp * TP + i
                wait(pe, m_p[i % 2], (TP // 2) * hp + i // 2 + 1)
                wait(pe, m_ptl, g - 1)
                for j in range(mtile(i)[3]):
                    t = nc.tensor.transpose(psum[2 + i % 2][:, j * P:(j + 1) * P], me[i % NME][:, j * P:(j + 1) * P], ident[:])
                t.then_inc(m_pt, 1)

            def product(hp, k, js):
                x = k % 2
                _, n, nk = SEQS[x]
                if js[0] == 0:
                    wait(pe, m_ptl, unit_last(hp, k) + 1)
                    wait(pe, m_vl, 2 * hp + x + 1)
                    wait(pe, m_ml, 4 * hp + k - 1)
                for j in js:
                    for i, (a, b) in enumerate(((mv_h, pT_h), (mv_l, pT_h), (mv_h, pT_l))):
                        last = nc.tensor.matmul(psum[6 + k % 2][:, 0:n], a[x][:, j, :], b[x][:, j, :],
                                                start=(j == 0 and i == 0), stop=(j == nk - 1 and i == 2))
                if js[-1] == nk - 1:
                    last.then_inc(m_pv, 1)

            def pair(hp, first, last):
                for i in pair_slots(first, last):
                    on_tile(TP, i, first, last, hp, turn_probs, 0)
                    at_slot(TURN_SLOTS, i, first, last, hp, turn)
                    on_tile(TP, i, first, last, hp, scores, 4)
                    at_slot(PV_SLOTS, i, first, last, hp, product)

            turn(0, 0)
            turn(0, 1)
            over(pe, HEADS // 2, pair)

        @block.scalar
        def _(act):
            def cut_qk(hp, k):
                x = k % 2
                n = SEQS[x][1]
                w = 4 * hp + k
                wait(act, m_sc, unit_last(hp, k) - NT + 1)
                for j, dst in enumerate((mq_h, mk_h)):
                    wait(act, m_tq, 2 * w + j + 1)
                    nc.scalar.activation(dst[x][0:QK, :], psum[4 + j][0:QK, 0:n], ACT.Copy).then_inc(m_qh, 1)

            def cut_v(hp, x):
                t0, _, nt = SEQS[x]
                wait(act, m_pv, 4 * hp + x - 1)
                nc.scalar.activation(mv_h[x][:].rearrange("p t (h n) -> p t h n", h=2),
                                     v_tok[:, t0 // P:t0 // P + nt, bass.ds(2 * hp, 2), :], ACT.Copy).then_inc(m_vh, 1)

            def exp(hp, i):
                n = mtile(i)[2]
                g = hp * TP + i
                wait(act, m_max, g + 1)
                wait(act, m_pt, g - NME + 1)
                nc.scalar.activation(me[i % NME][:, 0:n], psum[i % 2][:, 0:n], ACT.Exp, bias=mmax[:, i % 2:i % 2 + 1],
                                     accum_out=msum[:, i % 2:i % 2 + 1]).then_inc(m_exp, 1)

            def normalise(hp, i):
                if i % 2 == 1:
                    n = mtile(i)[2]
                    wait(act, m_rec, hp * TP + i + 1)
                    e = me[i % NME][:, 0:n]
                    nc.scalar.activation(e, e, ACT.Copy, scale=mrec[:, i % 2:i % 2 + 1]).then_inc(m_p[1], 1)

            def probs_high(hp, i):
                k, x, n, nk, qt = mtile(i)
                wait(act, m_pt, hp * TP + i + 1)
                if qt == 0:
                    wait(act, m_pv, 4 * hp + k - 1)
                nc.scalar.activation(pT_h[x][:, :, qt * P:(qt + 1) * P], psum[2 + i % 2][:, 0:n].rearrange("p (j q) -> p j q", q=P),
                                     ACT.Copy).then_inc(m_pth, 1)

            def mix_high(hp, k):
                t0, n, _ = SEQS[k % 2]
                r = slice(VDIM * (k // 2), VDIM * (k // 2) + VDIM)
                wait(act, m_pv, 4 * hp + k + 1)
                nc.scalar.activation(mixM_h[r, hp, t0:t0 + n], psum[6 + k % 2][r, 0:n], ACT.Copy).then_inc(m_mh, 1)

            def pair(hp, first, last):
                for i in pair_slots(first, last):
                    on_tile(TP, i, first, last, hp, probs_high, 0)
                    on_tile(TP, i, first, last, hp, exp, 3)
                    on_tile(TP, i, first, last, hp, normalise, 2)
                    at_slot(MIX_SLOTS, i, first, last, hp, mix_high)
                    at_slot(TURN_SLOTS, i, first, last, hp, cut_qk)
                    at_slot(V_SLOTS, i, first, last, hp, cut_v)

            cut_qk(0, 0)
            cut_qk(0, 1)
            over(act, HEADS // 2, pair)

        @block.gpsimd
        def _(pool):
            def restage(hp, k):
                wait(pool, m_tq, 2 * (4 * hp + k) - 2)
                stage(hp, k)

            def normalise(hp, i):
                if i % 2 == 0:
                    n = mtile(i)[2]
                    wait(pool, m_rec, hp * TP + i + 1)
                    e = me[i % NME][:, 0:n]
                    nc.gpsimd.tensor_scalar(e, e, mrec[:, i % 2:i % 2 + 1], None, ALU.mult).then_inc(m_p[0], 1)

            def pair(hp, first, last):
                for i in pair_slots(first, last):
                    on_tile(TP, i, first, last, hp, normalise, 2)
                    at_slot(STAGE_SLOTS, i, first, last, hp, restage)

            restage(0, 2)
            over(pool, HEADS // 2, pair)

        @block.vector
        def _(dve):
            def cut_qk(hp, k):
                x = k % 2
                n = SEQS[x][1]
                for j, (hi, lo) in enumerate(((mq_h, mq_l), (mk_h, mk_l))):
                    wait(dve, m_qh, 2 * (4 * hp + k) + j + 1)
                    nc.vector.tensor_tensor(lo[x][0:QK, :], psum[4 + j][0:QK, 0:n], f32(hi[x][0:QK, :]), ALU.subtract).then_inc(m_ql, 1)

            def cut_v(hp, x):
                t0, _, nt = SEQS[x]
                wait(dve, m_vh, 2 * hp + x + 1)
                nc.vector.tensor_tensor(mv_l[x][:].rearrange("p t (h n) -> p t h n", h=2),
                                        v_tok[:, t0 // P:t0 // P + nt, bass.ds(2 * hp, 2), :],
                                        f32(mv_h[x][:]).rearrange("p t (h n) -> p t h n", h=2),
                                        ALU.subtract).then_inc(m_vl, 1)

            def maximum(hp, i):
                n = mtile(i)[2]
                wait(dve, m_sc, hp * TP + i + 1)
                nc.vector.tensor_reduce(mmax[:, i % 2:i % 2 + 1], psum[i % 2][:, 0:n], axis=AX, op=ALU.max,
                                        negate=True).then_inc(m_max, 1)

            def reciprocal(hp, i):
                g = hp * TP + i
                wait(dve, m_exp, g + 1)
                wait(dve, m_p[i % 2], (TP // 2) * hp + i // 2)
                nc.vector.reciprocal(mrec[:, i % 2:i % 2 + 1], msum[:, i % 2:i % 2 + 1]).then_inc(m_rec, 1)

            def probs_low(hp, i):
                k, x, n, nk, qt = mtile(i)
                wait(dve, m_pth, hp * TP + i + 1)
                qs = slice(qt * P, (qt + 1) * P)
                nc.vector.tensor_tensor(pT_l[x][:, :, qs], psum[2 + i % 2][:, 0:n].rearrange("p (j q) -> p j q", q=P),
                                        f32(pT_h[x][:, :, qs]), ALU.subtract).then_inc(m_ptl, 1)

            def mix_low(hp, k):
                t0, n, _ = SEQS[k % 2]
                r = slice(VDIM * (k // 2), VDIM * (k // 2) + VDIM)
                wait(dve, m_mh, 4 * hp + k + 1)
                nc.vector.tensor_tensor(mixM_l[r, hp, t0:t0 + n], psum[6 + k % 2][r, 0:n], f32(mixM_h[r, hp, t0:t0 + n]),
                                        ALU.subtract).then_inc(m_ml, 1)

            def pair(hp, first, last):
                for i in pair_slots(first, last):
                    on_tile(TP, i, first, last, hp, maximum, 3)
                    on_tile(TP, i, first, last, hp, reciprocal, 2)
                    on_tile(TP, i, first, last, hp, probs_low, 0)
                    at_slot(MIX_SLOTS, i, first, last, hp, mix_low)
                    at_slot(TURN_SLOTS, i, first, last, hp, cut_qk)
                    at_slot(V_SLOTS, i, first, last, hp, cut_v)

            cut_qk(0, 0)
            cut_qk(0, 1)
            over(dve, HEADS // 2, pair)

    HW = D // 2
    wo_raw = [at(f"wo_raw{c}", 30 + 2 * c, [P, HW]) for c in range(KD)]
    wo_h = [at(f"wo_h{c}", 46 + 2 * c, [P, HW], FR) for c in range(KD)]
    wo_l = [at(f"wo_l{c}", 62 + 2 * c, [P, HW], FR) for c in range(KD)]
    ln1g_sb = at("ln1g_sb", 186, [P, D])
    ln1b_sb = at("ln1b_sb", 190, [P, D])
    ax = [at(f"ax{i}", 194 + 4 * i, [P, D]) for i in range(2)]
    x1T = at("x1T", 202, [P, KD, P])
    raw = {X: [at(f"raw{X}{i}", 78 + 16 * n + 4 * i, [P, 2 * FF]) for i in range(4)] for n, X in enumerate("GUD")}
    wh_ = {X: [at(f"e{X}h{i}", kb + 4 * i, [P, 2 * FF], FR) for i in range(4)] for X, kb in (("G", 6), ("D", 38), ("U", 126))}
    wl_ = {X: [at(f"e{X}l{i}", kb + 4 * i, [P, 2 * FF], FR) for i in range(4)] for X, kb in (("G", 22), ("D", 54))}
    wl_["U"] = [at(f"eUl{i}", (142, 146, 182, 186)[i], [P, 2 * FF], FR) for i in range(4)]
    x1_rows = nc.dram_tensor("x1_rows", (TOK + P, D), F).ap()
    acc_rows = nc.dram_tensor("acc_rows", (TOK + P, D), F).ap()

    cursor = [150 * KB]

    def tmp(name, shape, dt=F):
        n = 4
        for v in shape[1:]:
            n *= v
        off = cursor[0]
        cursor[0] += (n + 31) // 32 * 32
        assert cursor[0] <= 162 * KB, name
        return nc.alloc_sbuf_tensor_at(name, list(shape), dt, offset=base + off)

    wr_sb = tmp("wr_sb", [P, KD, NE])
    br_sb = tmp("br_sb", [P, NE])
    before = tmp("before", [P, P])
    ones = tmp("ones", [P, P])
    i128 = tmp("i128", [P, P])
    i32a = tmp("i32a", [P, P], I32)
    itile = tmp("itile", [P, MAX_TILES])
    irank = tmp("irank", [P, NE])
    grank = tmp("grank", [P, NG])
    iexp = tmp("iexp", [P, NE])
    tok1 = tmp("tok1", [P, NT])
    padrow = tmp("padrow", [P, 1])
    sg = tmp("sg", [P, NT, NE])
    bs = tmp("bs", [P, NT, NE])
    g6 = [tmp(f"g6_{i}", [P, NT * NG]) for i in range(6)]
    r1 = tmp("r1", [P, NT])
    r2 = tmp("r2", [P, NT])
    mb = [tmp(f"mb{i}", [P, NT, NE]) for i in range(2)]
    t16 = tmp("t16", [P, NT, NE])
    picks = tmp("picks", [P, 2, NT, NE])
    prod = tmp("prod", [P, 2, NT, NE])
    member = tmp("member", [P, NT, NE])
    pos = tmp("pos", [P, NT, NE])
    more = tmp("more", [P, NE])
    upto = tmp("upto", [P, NE])
    cnt_i = tmp("cnt_i", [P, NE], I32)
    first_more = tmp("first_more", [P, NE])
    gate = tmp("gate", [P, 2, NT])
    place = tmp("place", [P, 2, NT])
    place_i = tmp("place_i", [P, 2, NT], I32)
    blk = tmp("blk", [P, 2, NT])
    low = tmp("low", [P, 2, NT])
    exp_of = tmp("exp_of", [P, 2, NT])
    tile_of = tmp("tile_of", [P, 2, NT])
    hot = tmp("hot", [P, 2, P])
    vals = tmp("vals", [P, 2, 2, MAX_TILES])
    le = tmp("le", [1, MAX_MORE + 1, NE])
    te_f = tmp("te_f", [1, MAX_TILES])
    idx_f = tmp("idx_f", [P, MAX_TILES])
    idx_tab = small("idx_tab", [P, MAX_TILES], I32)
    gate_tab = small("gate_tab", [P, MAX_TILES])
    tile_expert = small("tile_expert", [1, MAX_TILES], I32)
    n_more_sb = small("n_more_sb", [1, 1], I32)

    s_ln1w, s_rt = sem("ln1_weights_landed"), sem("router_weights_landed")
    s_wo = [sem(f"wo_landed{c}") for c in range(KD)]
    s_woh, s_wol, s_wou = sem("wo_high"), sem("wo_low"), sem("wo_chunk_used")
    s_o0, s_o1, s_y0, s_y1 = sem("o_first_half"), sem("o_second_half"), sem("o_first_half_out"), sem("o_second_half_out")
    s_var1, s_rstd1, s_x1 = sem("ln1_variance"), sem("ln1_rstd"), sem("x1_ready")
    s_x1t, s_x1e, s_log = sem("x1_transposed"), sem("x1T_ready"), sem("logits")
    s_ax, s_x1st, s_stored = sem("scaled_x1"), sem("x1_stored"), [sem(f"scaled_x1_stored{i}") for i in range(2)]
    s_zrow, s_zst = sem("zero_rows"), sem("zero_rows_stored")
    s_consts = sem("router_constants")
    s_rexp, s_member, s_prefix = sem("router_exp"), sem("router_members"), sem("router_prefix")
    s_hot, s_hotused, s_slots = sem("one_hots"), sem("one_hots_used"), sem("slot_table")
    s_hi = {X: sem(f"e{X}_high") for X in "GUD"}
    s_lo = {X: sem(f"e{X}_low") for X in "GUD"}
    s_raw = {X: [sem(f"raw{X}{i}_landed") for i in range(4)] for X in "GUD"}

    def unit_src(X, e, i):
        if X == "D":
            return w_down[0, bass.ds(e, 1), i * P:(i + 1) * P, :].rearrange("a p n -> p (a n)")
        w = w_gate if X == "G" else w_up
        return w[0, bass.ds(e, 1), 2 * i * P:(2 * i + 2) * P, :].rearrange("a (c p) n -> p (a c) n", p=P)

    def unit_dst(X, i):
        return raw[X][i][:] if X == "D" else raw[X][i][:].rearrange("p (c n) -> p c n", c=2)

    def mix(c, hi):
        t = (mixM_h if hi else mixM_l) if c < KD // 2 else (mixD_h if hi else mixD_l)
        return t[:, c % (KD // 2), :]

    with nc.Block() as block:

        @block.sync
        def _(sp):
            for u in range(2 * KD):
                n, c = u // KD, u % KD
                if n:
                    sp.wait_ge(s_wol, u - KD + 1)
                sp.dma_start(wo_raw[c][:], w_o[0, c * P:(c + 1) * P, n * HW:(n + 1) * HW]).then_inc(s_wo[c], 16)
                if u == KD - 1:
                    sp.dma_start(ln1g_sb[:], bcast(ln1_g[0], D)).then_inc(s_ln1w, 16)
                    sp.dma_start(ln1b_sb[:], bcast(ln1_b[0], D)).then_inc(s_ln1w, 16)
                    sp.dma_start(wr_sb[:], w_router.rearrange("(c p) n -> p c n", p=P)).then_inc(s_rt, 16)
                    sp.dma_start(br_sb[:], bcast(b_router, NE)).then_inc(s_rt, 16)
                    for X in "GUD":
                        for i in range(4):
                            sp.dma_start(unit_dst(X, i), unit_src(X, 0, i)).then_inc(s_raw[X][i], 16)
            sp.wait_ge(s_zrow, 1)
            sp.dma_start(x1_rows[TOK:TOK + P, :], ax[1][:]).then_inc(s_zst, 16)
            sp.dma_start(acc_rows[TOK:TOK + P, :], ax[1][:]).then_inc(s_zst, 16)
            for t in range(NT):
                sp.wait_ge(s_x1, t + 1)
                sp.dma_start(x1_rows[t * P:(t + 1) * P, :], res[:, t, :]).then_inc(s_x1st, 16)
                sp.wait_ge(s_ax, t + 1)
                sp.dma_start(acc_rows[t * P:(t + 1) * P, :], ax[t % 2][:]).then_inc(s_stored[t % 2], 16)
            sp.wait_ge(s_zst, 32)
            for i in range(2):
                sp.wait_ge(s_stored[i], 16 * (NT // 2))
            sp.wait_ge(s_x1st, 16 * NT)
            for X in "UG":
                for i in range(4):
                    sp.wait_ge(s_lo[X], i + 1)
                    sp.dma_start(unit_dst(X, i), unit_src(X, 1, i)).then_inc(s_raw[X][i], 16)

        @block.tensor
        def _(pe):
            def second_half(t):
                wait(pe, s_y1, t - 1)
                ts = slice(t * P, (t + 1) * P)
                out = psum[6 + t % 2][:]
                for c in range(KD):
                    if t == 0:
                        pe.wait_ge(s_wol, KD + c + 1)
                    nc.tensor.matmul(out, mix(c, True)[:, ts], wo_h[c][:], start=(c == 0), stop=False)
                    nc.tensor.matmul(out, mix(c, False)[:, ts], wo_h[c][:], start=False, stop=False)
                    last = nc.tensor.matmul(out, mix(c, True)[:, ts], wo_l[c][:], start=False, stop=(c == KD - 1))
                last.then_inc(s_o1, 1)

            def turn_x1(t):
                pe.wait_ge(s_x1, t + 1)
                pe.wait_ge(s_y0, 2)
                wait(pe, s_x1e, 2 * t)
                for hf in range(2):
                    for j in range(4):
                        c = 4 * hf + j
                        last = nc.tensor.transpose(psum[hf][:, j * P:(j + 1) * P], res[:, t, c * P:(c + 1) * P], ident[:])
                    last.then_inc(s_x1t, 1)

            def logits(t):
                pe.wait_ge(s_x1e, 2 * t + 2)
                pe.wait_ge(s_rt, 32)
                pe.wait_ge(s_y0, 3)
                for c in range(KD):
                    last = nc.tensor.matmul(psum[2][:, t * NE:(t + 1) * NE], x1T[:, c, :], wr_sb[:, c, :],
                                            start=(c == 0), stop=(c == KD - 1))
                last.then_inc(s_log, 1)

            for c in range(KD):
                pe.wait_ge(s_wol, c + 1)
                for t in range(NT):
                    ts = slice(t * P, (t + 1) * P)
                    out = psum[t][:]
                    nc.tensor.matmul(out, mix(c, True)[:, ts], wo_h[c][:], start=(c == 0), stop=False)
                    nc.tensor.matmul(out, mix(c, False)[:, ts], wo_h[c][:], start=False, stop=False)
                    last = nc.tensor.matmul(out, mix(c, True)[:, ts], wo_l[c][:], start=False, stop=(c == KD - 1))
                    if c == KD - 1:
                        last.then_inc(s_o0, 1)
                if c < KD - 1:
                    last.then_inc(s_wou, 1)
            for t in range(NT):
                second_half(t)
                if t >= 2:
                    logits(t - 2)
                if t >= 1:
                    turn_x1(t - 1)
            logits(NT - 2)
            turn_x1(NT - 1)
            logits(NT - 1)

            pe.wait_ge(s_member, 1)
            pe.wait_ge(s_consts, 1)
            pe.wait_ge(s_y0, NT)
            m = member[:].rearrange("p t e -> p (t e)")
            nc.tensor.matmul(psum[3][:, 0:NT * NE], before[:], m, start=True, stop=False)
            for d in range(1, NT):
                nc.tensor.matmul(psum[3][:, d * NE:NT * NE], ones[:], m[:, 0:(NT - d) * NE], start=False, stop=(d == NT - 1))
            for t in range(NT):
                last = nc.tensor.matmul(psum[4][:, 0:NE], ones[:], member[:, t, :], start=(t == 0), stop=(t == NT - 1))
            last.then_inc(s_prefix, 1)
            for n in range(2 * NT):
                pe.wait_ge(s_hot, n + 1)
                nc.tensor.matmul(psum[5][:, 0:2 * MAX_TILES], hot[:, n % 2, :], vals[:, n % 2].rearrange("p a b -> p (a b)"),
                                 start=(n == 0), stop=(n == 2 * NT - 1)).then_inc(s_slots, 1)

        @block.scalar
        def _(act):
            def wo_high(u):
                n, c = u // KD, u % KD
                act.wait_ge(s_wo[c], 16 * (n + 1))
                if n:
                    if c < KD - 1:
                        act.wait_ge(s_wou, c + 1)
                    else:
                        act.wait_ge(s_o0, NT)
                nc.scalar.activation(wo_h[c][:], wo_raw[c][:], ACT.Copy).then_inc(s_woh, 1)

            for u in range(2 * KD):
                wo_high(u)
            act.wait_ge(s_zst, 32)
            for t in range(NT):
                act.wait_ge(s_x1, t + 1)
                if t >= 2:
                    act.wait_ge(s_stored[t % 2], 16 * (t // 2))
                for hf in range(2):
                    act.wait_ge(s_x1t, 2 * t + hf + 1)
                    wait(act, s_log, t)
                    nc.scalar.activation(x1T[:, 4 * hf:4 * hf + 4, :], psum[hf][:].rearrange("p (c n) -> p c n", c=4),
                                         ACT.Copy).then_inc(s_x1e, 1)
                nc.scalar.activation(ax[t % 2][:], res[:, t, :], ACT.Copy, scale=ALPHA).then_inc(s_ax, 1)
            act.wait_ge(s_log, NT)
            nc.scalar.activation(sg[:], psum[2][:, 0:NT * NE].rearrange("p (t e) -> p t e", t=NT), ACT.Exp,
                                 scale=-1.0).then_inc(s_rexp, 1)

            def high0(X, units=range(4)):
                for i in units:
                    act.wait_ge(s_raw[X][i], 16)
                    nc.scalar.activation(wh_[X][i][:], raw[X][i][:], ACT.Copy).then_inc(s_hi[X], 1)

            act.wait_ge(s_o1, NT)
            high0("U")
            act.wait_ge(s_x1st, 16 * NT)
            act.wait_ge(s_ax, NT)
            act.wait_ge(s_x1t, 2 * NT)
            high0("G")
            high0("D", (0, 1))

        @block.gpsimd
        def _(pool):
            n = [0]

            def done(ins):
                n[0] += 1
                ins.then_inc(s_pool2, 1)
                pool.wait_ge(s_pool2, n[0])

            s_pool2 = sem("router_pool_step")
            nc.gpsimd.memset(ax[1][:], 0.0).then_inc(s_zrow, 1)
            done(nc.gpsimd.memset(before[:], 1.0))
            nc.gpsimd.memset(ones[:], 1.0)
            done(nc.gpsimd.affine_select(out=before[:], in_=before[:], compare_op=ALU.is_gt, fill=0.0, base=0,
                                         pattern=[[1, P]], channel_multiplier=-1))

            def counted(dst, pattern, base0, mult):
                w = 1
                for _, k in pattern:
                    w *= k
                done(nc.gpsimd.iota(i32a[:, 0:w], pattern=pattern, base=base0, channel_multiplier=mult))
                done(nc.gpsimd.tensor_copy(dst, i32a[:, 0:w]))

            counted(i128[:], [[1, P]], 0, 0)
            counted(itile[:], [[1, MAX_TILES]], 0, 0)
            counted(irank[:], [[-1, NE]], NE, 0)
            counted(grank[:], [[-1, NG]], NG, 0)
            counted(iexp[:], [[1, NE]], 0, 0)
            counted(tok1[:], [[P, NT]], 1, 1)
            counted(padrow[:], [[1, 1]], TOK + 1, 1)
            nc.gpsimd.memset(te_f[:], 0.0).then_inc(s_consts, 1)
            for t in range(NT):
                pool.wait_ge(s_var1, t + 1)
                nc.gpsimd.tensor_tensor(rstd[:, t:t + 1], mv[:, t, 1:2], minus_half[:, 0:1], ALU.pow).then_inc(s_rstd1, 1)
            for X, units in (("U", range(4)), ("G", range(4)), ("D", range(2))):
                for i in units:
                    pool.wait_ge(s_hi[X], i + 1)
                    if X == "U" and i == 3:
                        pool.wait_ge(s_x1, NT)
                    nc.gpsimd.tensor_tensor(wl_[X][i][:], raw[X][i][:], f32(wh_[X][i][:]), ALU.subtract).then_inc(s_lo[X], 1)

        @block.vector
        def _(dve):
            def wo_low(u):
                c = u % KD
                dve.wait_ge(s_woh, u + 1)
                nc.vector.tensor_tensor(wo_l[c][:], wo_raw[c][:], f32(wo_h[c][:]), ALU.subtract).then_inc(s_wol, 1)

            for u in range(2 * KD):
                wo_low(u)
            for t in range(NT):
                dve.wait_ge(s_o0, t + 1)
                nc.vector.scalar_tensor_tensor(out=res[:, t, 0:HW], in0=res[:, t, 0:HW], scalar=ALPHA, in1=psum[t][:],
                                               op0=ALU.mult, op1=ALU.add).then_inc(s_y0, 1)
            dve.wait_ge(s_ln1w, 32)
            for t in range(NT):
                dve.wait_ge(s_o1, t + 1)
                nc.vector.scalar_tensor_tensor(out=res[:, t, HW:D], in0=res[:, t, HW:D], scalar=ALPHA, in1=psum[6 + t % 2][:],
                                               op0=ALU.mult, op1=ALU.add).then_inc(s_y1, 1)
                dve.wait_ge(s_y0, t + 1)
                nc.vector.bn_stats(stats[:, t % 2, 0, :], res[:, t, 0:HW])
                dve.wait_ge(s_y1, t + 1)
                then(nc.vector.bn_stats(stats[:, t % 2, 1, :], res[:, t, HW:D]))
                then(nc.vector.bn_aggr(mv[:, t, :], stats[:, t % 2, :, :].rearrange("p a b -> p (a b)")))
                nc.vector.tensor_scalar_add(mv[:, t, 1:2], mv[:, t, 1:2], LN_EPS).then_inc(s_var1, 1)
                then(nc.vector.scalar_tensor_tensor(out=res[:, t, :], in0=res[:, t, :], scalar=mv[:, t, 0:1], in1=ln1g_sb[:],
                                                    op0=ALU.subtract, op1=ALU.mult))
                dve.wait_ge(s_rstd1, t + 1)
                nc.vector.scalar_tensor_tensor(out=res[:, t, :], in0=res[:, t, :], scalar=rstd[:, t:t + 1], in1=ln1b_sb[:],
                                               op0=ALU.mult, op1=ALU.add).then_inc(s_x1, 1)

            tt, ts = nc.vector.tensor_tensor, nc.vector.tensor_scalar
            tne = [P, NT, NE]

            dve.wait_ge(s_rexp, 1)
            dve.wait_ge(s_rt, 32)
            dve.wait_ge(s_consts, 1)
            then(nc.vector.tensor_scalar_add(sg[:], sg[:], 1.0))
            then(nc.vector.reciprocal(sg[:], sg[:]))
            then(tt(bs[:], sg[:], br_sb[:].unsqueeze(1).to_broadcast(tne), ALU.add))
            four = bs[:].rearrange("p t (g k) -> p (t g) k", k=EPG)
            a, b, c, d = (four[:, :, i] for i in range(4))
            tt(g6[0][:], a, b, ALU.max)
            tt(g6[1][:], a, b, ALU.min)
            tt(g6[2][:], c, d, ALU.max)
            then(tt(g6[3][:], c, d, ALU.min))
            tt(g6[4][:], g6[0][:], g6[2][:], ALU.max)
            tt(g6[5][:], g6[0][:], g6[2][:], ALU.min)
            then(tt(g6[1][:], g6[1][:], g6[3][:], ALU.max))
            then(tt(g6[5][:], g6[5][:], g6[1][:], ALU.max))
            then(tt(g6[0][:], g6[4][:], g6[5][:], ALU.add))

            def first_best(val, rank, work, n, out, best):
                full = [P, NT, n]
                then(nc.vector.tensor_reduce(best, val, axis=AX, op=ALU.max))
                then(tt(work, val, best.unsqueeze(2).to_broadcast(full), ALU.is_equal))
                then(tt(work, work, rank[:].unsqueeze(1).to_broadcast(full), ALU.mult))
                then(nc.vector.tensor_reduce(best, work, axis=AX, op=ALU.max))
                then(tt(out, work, best.unsqueeze(2).to_broadcast(full), ALU.is_equal))

            def by_group(t):
                return t[:].rearrange("p (t g) -> p t g", g=NG)

            first_best(by_group(g6[0]), grank, by_group(g6[1]), NG, by_group(g6[2]), r1[:])
            BIG = 1.0e30
            inside = g6[2][:].unsqueeze(2).to_broadcast([P, NT * NG, EPG])
            k4 = lambda t: t[:].rearrange("p t (g k) -> p (t g) k", k=EPG)
            then(tt(k4(mb[0]), k4(bs), inside, ALU.mult))
            then(ts(g6[3][:], g6[2][:], BIG, -BIG, ALU.mult, ALU.add))
            then(tt(k4(mb[0]), k4(mb[0]), g6[3][:].unsqueeze(2).to_broadcast([P, NT * NG, EPG]), ALU.add))
            first_best(mb[0][:], irank, t16[:], NE, picks[:, 0], r1[:])
            then(nc.vector.scalar_tensor_tensor(out=mb[1][:], in0=picks[:, 0], scalar=-BIG, in1=mb[0][:], op0=ALU.mult, op1=ALU.add))
            first_best(mb[1][:], irank, t16[:], NE, picks[:, 1], r1[:])
            tt(member[:], picks[:, 0], picks[:, 1], ALU.add).then_inc(s_member, 1)

            def both(x):
                return x.unsqueeze(1).to_broadcast([P, 2, NT, NE])

            def pick(dst, table):
                for k in range(2):
                    then(tt(prod[:, k], picks[:, k], table, ALU.mult))
                then(nc.vector.tensor_reduce(dst, prod[:].rearrange("p a t e -> p (a t) e"), axis=AX, op=ALU.add))

            flat = lambda t: t[:].rearrange("p a t -> p (a t)")
            pick(flat(gate), sg[:])
            then(tt(r1[:], gate[:, 0, :], gate[:, 1, :], ALU.add))
            then(nc.vector.reciprocal(r2[:], r1[:]))
            then(tt(gate[:], gate[:], r2[:].unsqueeze(1).to_broadcast([P, 2, NT]), ALU.mult))
            pick(flat(exp_of), iexp[:].unsqueeze(1).to_broadcast(tne))
            dve.wait_ge(s_prefix, 1)
            then(nc.vector.tensor_copy(pos[:], psum[3][:, 0:NT * NE].rearrange("p (t e) -> p t e", t=NT)))
            then(ts(more[:], psum[4][:, 0:NE], 1.0, -1.0, ALU.max, ALU.add))
            then(nc.vector.tensor_copy(cnt_i[:], more[:]))
            then(nc.vector.tensor_single_scalar(cnt_i[:], cnt_i[:], 7, op=ALU.logical_shift_right))
            then(nc.vector.tensor_copy(more[:], cnt_i[:]))
            then(nc.vector.tensor_tensor_scan(out=upto[:], data0=ones[:, 0:NE], data1=more[:], initial=0.0, op0=ALU.mult, op1=ALU.add))
            then(tt(first_more[:], upto[:], more[:], ALU.subtract))
            then(tt(first_more[:], first_more[:], iexp[:], ALU.subtract))
            then(nc.vector.tensor_scalar_add(first_more[:], first_more[:], NE - 1.0))
            pick(flat(place), pos[:])
            then(nc.vector.tensor_copy(place_i[:], place[:]))
            then(nc.vector.tensor_single_scalar(place_i[:], place_i[:], 7, op=ALU.logical_shift_right))
            then(nc.vector.tensor_copy(blk[:], place_i[:]))
            then(nc.vector.scalar_tensor_tensor(out=flat(low), in0=flat(blk), scalar=-float(P), in1=flat(place), op0=ALU.mult, op1=ALU.add))
            pick(flat(tile_of), first_more[:].unsqueeze(1).to_broadcast(tne))
            then(tt(flat(tile_of), flat(tile_of), flat(blk), ALU.add))
            then(nc.vector.scalar_tensor_tensor(out=flat(tile_of), in0=flat(blk), scalar=0.5, in1=flat(tile_of), op0=ALU.is_gt, op1=ALU.mult))
            then(tt(flat(tile_of), flat(tile_of), flat(exp_of), ALU.add))
            for n in range(2 * NT):
                k, t = n // NT, n % NT
                if n >= 2:
                    dve.wait_ge(s_slots, n - 1)
                ts(hot[:, n % 2, :], i128[:], low[:, k, t:t + 1], None, ALU.is_equal)
                ts(vals[:, n % 2, 0, :], itile[:], tile_of[:, k, t:t + 1], tok1[:, t:t + 1], ALU.is_equal, ALU.mult)
                ts(vals[:, n % 2, 1, :], itile[:], tile_of[:, k, t:t + 1], gate[:, k, t:t + 1], ALU.is_equal, ALU.mult).then_inc(s_hot, 1)
            then(tt(le[:], upto[0:1, :].unsqueeze(1).to_broadcast([1, MAX_MORE + 1, NE]),
                    itile[0:1, 0:MAX_MORE + 1].unsqueeze(2).to_broadcast([1, MAX_MORE + 1, NE]), ALU.is_le))
            then(nc.vector.tensor_reduce(te_f[:, NE:MAX_TILES], le[:], axis=AX, op=ALU.add))
            then(nc.vector.tensor_copy(te_f[:, 0:NE], iexp[0:1, :]))
            then(nc.vector.tensor_scalar_min(te_f[:], te_f[:], NE - 1.0))
            then(nc.vector.tensor_copy(tile_expert[:], te_f[:]))
            then(nc.vector.tensor_copy(n_more_sb[:], upto[0:1, NE - 1:NE]))
            dve.wait_ge(s_slots, 2 * NT)
            then(nc.vector.tensor_copy(gate_tab[:], psum[5][:, MAX_TILES:2 * MAX_TILES]))
            then(ts(idx_f[:], psum[5][:, 0:MAX_TILES], 0.0, padrow[:], ALU.is_equal, ALU.mult))
            then(tt(idx_f[:], idx_f[:], psum[5][:, 0:MAX_TILES], ALU.add))
            then(nc.vector.tensor_scalar_add(idx_f[:], idx_f[:], -1.0))
            then(nc.vector.tensor_copy(idx_tab[:], idx_f[:]))

    gsil = at("gsil", 170, [P, FF])
    hid = at("hid", 172, [P, FF])
    hT_h = at("hT_h", 174, [P, FF], FR)
    hT_l = at("hT_l", 176, [P, FF], FR)
    yg = at("yg", 178, [P, D])
    xg = at("xg", 190, [P, D])
    xgT_h = at("xgT_h", 162, [P, KD, P], FR)
    xgT_l = at("xgT_l", 166, [P, KD, P], FR)
    idx_g = small("idx_g", [P, 1], I32)
    idx_s = small("idx_s", [P, 1], I32)
    gate_col = small("gate_col", [P, 1])

    s_used = {X: sem(f"e{X}_used") for X in "GUD"}
    used0 = {"G": 0, "U": 0, "D": 4}
    s_idxg, s_idxs, s_gcol = sem("gather_index"), sem("scatter_index"), sem("gate_column")
    s_gather, s_scatter = sem("rows_gathered"), sem("rows_added")
    s_tx, s_xh, s_xl = sem("xg_transposed"), sem("xgT_high"), sem("xgT_low")
    s_silu, s_hid = sem("silu"), sem("hidden")
    s_ht, s_hh, s_hl = sem("hidden_transposed"), sem("hT_high"), sem("hT_low")
    s_yg = sem("expert_rows")

    def iterate(eng, iteration):
        count = eng.value_load(n_more_sb[0:1, 0:1], min_val=0, max_val=MAX_MORE) + NE
        iteration(1, False)
        with eng.Fori(2, count - 1) as t:
            iteration(t, False)
        iteration(count - 1, True)
        return count

    with nc.Block() as block:

        @block.sync
        def _(sp):
            def load(X, t):
                e = sp.value_load(tile_expert[0:1, bass.ds(t, 1)], min_val=0, max_val=NE - 1)
                for i in range(4):
                    sp.wait_ge(s_lo[X], 4 * t + i - 3)
                    sp.dma_start(unit_dst(X, i), unit_src(X, e, i)).then_inc(s_raw[X][i], 16)

            load("G", 2)
            count = sp.value_load(n_more_sb[0:1, 0:1], min_val=0, max_val=MAX_MORE) + NE
            with sp.Fori(1, count - 2) as t:
                load("D", t)
                load("U", t + 1)
                load("G", t + 2)
            load("D", count - 2)
            load("U", count - 1)
            load("D", count - 1)

        @block.tensor
        def _(pe):
            def turn_x(t):
                wait(pe, s_gather, 16 * t + 16)
                wait(pe, s_xl, 2 * t)
                for hf in range(2):
                    for j in range(4):
                        c = 4 * hf + j
                        last = nc.tensor.transpose(psum[4 + hf][:, j * P:(j + 1) * P], xg[:, c * P:(c + 1) * P], ident[:])
                    last.then_inc(s_tx, 1)

            def inner(X, t, units):
                out = psum["GU".index(X)][:]
                for i in units:
                    if i == 0:
                        wait(pe, s_silu if X == "G" else s_hid, t)
                    wait(pe, s_xl, 2 * t + 1 + i // 2)
                    wait(pe, s_lo[X], 4 * t + i + 1)
                    for j in range(2):
                        c, cs = 2 * i + j, slice(j * FF, (j + 1) * FF)
                        nc.tensor.matmul(out, xgT_h[:, c, :], wh_[X][i][:, cs], start=(c == 0), stop=False)
                        nc.tensor.matmul(out, xgT_l[:, c, :], wh_[X][i][:, cs], start=False, stop=False)
                        last = nc.tensor.matmul(out, xgT_h[:, c, :], wl_[X][i][:, cs], start=False, stop=(c == KD - 1))
                    last.then_inc(s_used[X], 1)

            def turn_h(t):
                wait(pe, s_hid, t + 1)
                wait(pe, s_hl, t)
                for j in range(4):
                    last = nc.tensor.transpose(psum[6][:, j * P:(j + 1) * P], hid[:, j * P:(j + 1) * P], ident[:])
                last.then_inc(s_ht, 1)

            def down(t):
                wait(pe, s_hl, t + 1)
                wait(pe, s_yg, t)
                for c in range(4):
                    wait(pe, s_lo["D"], 4 * t + c + 1)
                    cs = slice(c * P, (c + 1) * P)
                    for n in range(2):
                        out, ns = psum[2 + n][:], slice(n * FF, (n + 1) * FF)
                        nc.tensor.matmul(out, hT_h[:, cs], wh_["D"][c][:, ns], start=(c == 0), stop=False)
                        nc.tensor.matmul(out, hT_l[:, cs], wh_["D"][c][:, ns], start=False, stop=False)
                        last = nc.tensor.matmul(out, hT_h[:, cs], wl_["D"][c][:, ns], start=False, stop=(c == 3))
                    last.then_inc(s_used["D"], 1)

            def iteration(t, last):
                inner("G", t, (0, 1))
                turn_h(t - 1)
                inner("G", t, (2, 3))
                down(t - 1)
                if not last:
                    turn_x(t + 1)
                inner("U", t, range(4))

            pe.sem_inc(s_used["D"], used0["D"])
            turn_x(0)
            inner("G", 0, range(4))
            turn_x(1)
            inner("U", 0, range(4))
            count = iterate(pe, iteration)
            turn_h(count - 1)
            down(count - 1)

        @block.scalar
        def _(act):
            def high(X, t, units=range(4)):
                for i in units:
                    wait(act, s_raw[X][i], 16 * t + 16)
                    wait(act, s_used[X], used0[X] + 4 * t + i - 3)
                    nc.scalar.activation(wh_[X][i][:], raw[X][i][:], ACT.Copy).then_inc(s_hi[X], 1)

            def x_high(t, hf):
                wait(act, s_tx, 2 * t + hf + 1)
                wait(act, s_used["U"], 4 * t - 2 + 2 * hf)
                nc.scalar.activation(xgT_h[:, 4 * hf:4 * hf + 4, :], psum[4 + hf][:].rearrange("p (c n) -> p c n", c=4),
                                     ACT.Copy).then_inc(s_xh, 1)

            def silu(t):
                wait(act, s_used["G"], 4 * t + 4)
                wait(act, s_hid, t)
                nc.scalar.activation(gsil[:], psum[0][:], ACT.Silu).then_inc(s_silu, 1)

            def h_high(t):
                wait(act, s_ht, t + 1)
                wait(act, s_used["D"], used0["D"] + 4 * t)
                nc.scalar.activation(hT_h[:], psum[6][:], ACT.Copy).then_inc(s_hh, 1)

            def rows(t):
                wait(act, s_used["D"], used0["D"] + 4 * t + 4)
                wait(act, s_gcol, t + 1)
                wait(act, s_scatter, 16 * t)
                nc.scalar.activation(yg[:, 0:FF], psum[2][:], ACT.Copy, scale=gate_col[:])
                nc.scalar.activation(yg[:, FF:D], psum[3][:], ACT.Copy, scale=gate_col[:]).then_inc(s_yg, 1)

            def iteration(t, last):
                x_high(t, 1)
                high("D", t - 1, (2, 3))
                h_high(t - 1)
                high("U", t)
                silu(t)
                if not last:
                    high("G", t + 1)
                rows(t - 1)
                high("D", t, (0, 1))
                if not last:
                    x_high(t + 1, 0)

            x_high(0, 0)
            x_high(0, 1)
            silu(0)
            high("G", 1)
            x_high(1, 0)
            count = iterate(act, iteration)
            high("D", count - 1, (2, 3))
            h_high(count - 1)
            rows(count - 1)

        @block.vector
        def _(dve):
            def low_part(X, t, units=range(4)):
                for i in units:
                    wait(dve, s_hi[X], 4 * t + i + 1)
                    nc.vector.tensor_tensor(wl_[X][i][:], raw[X][i][:], f32(wh_[X][i][:]), ALU.subtract).then_inc(s_lo[X], 1)

            def x_low(t, hf):
                wait(dve, s_xh, 2 * t + hf + 1)
                hs = slice(4 * hf, 4 * hf + 4)
                nc.vector.tensor_tensor(xgT_l[:, hs, :], psum[4 + hf][:].rearrange("p (c n) -> p c n", c=4),
                                        f32(xgT_h[:, hs, :]), ALU.subtract).then_inc(s_xl, 1)

            def hidden(t):
                wait(dve, s_silu, t + 1)
                wait(dve, s_used["U"], 4 * t + 4)
                wait(dve, s_ht, t)
                nc.vector.tensor_tensor(hid[:], gsil[:], psum[1][:], ALU.mult).then_inc(s_hid, 1)

            def h_low(t):
                wait(dve, s_hh, t + 1)
                nc.vector.tensor_tensor(hT_l[:], psum[6][:], f32(hT_h[:]), ALU.subtract).then_inc(s_hl, 1)

            def iteration(t, last):
                x_low(t, 1)
                hidden(t - 1)
                low_part("D", t - 1, (2, 3))
                h_low(t - 1)
                low_part("U", t)
                if not last:
                    low_part("G", t + 1)
                low_part("D", t, (0, 1))
                if not last:
                    x_low(t + 1, 0)

            x_low(0, 0)
            x_low(0, 1)
            low_part("G", 1)
            x_low(1, 0)
            count = iterate(dve, iteration)
            hidden(count - 1)
            low_part("D", count - 1, (2, 3))
            h_low(count - 1)

        @block.gpsimd
        def _(pool):
            def gather(t):
                wait(pool, s_gather, 16 * t)
                nc.gpsimd.tensor_copy(idx_g[:], idx_tab[:, bass.ds(t, 1)]).then_inc(s_idxg, 1)
                wait(pool, s_idxg, t + 1)
                wait(pool, s_tx, 2 * t)
                pool.indirect_dma_start(out=xg[:], out_offset=None, in_=x1_rows,
                                        in_offset=bass.IndirectOffsetOnAxis(ap=idx_g[:, 0:1], axis=0),
                                        bounds_check=TOK + P - 1, oob_is_err=False).then_inc(s_gather, 16)

            def add_rows(t):
                wait(pool, s_yg, t)
                nc.gpsimd.tensor_copy(gate_col[:], gate_tab[:, bass.ds(t, 1)]).then_inc(s_gcol, 1)
                wait(pool, s_scatter, 16 * t)
                nc.gpsimd.tensor_copy(idx_s[:], idx_tab[:, bass.ds(t, 1)]).then_inc(s_idxs, 1)
                wait(pool, s_idxs, t + 1)
                wait(pool, s_yg, t + 1)
                pool.indirect_dma_start(out=acc_rows, out_offset=bass.IndirectOffsetOnAxis(ap=idx_s[:, 0:1], axis=0),
                                        in_=yg[:], in_offset=None, bounds_check=TOK + P - 1, oob_is_err=True,
                                        compute_op=ALU.add).then_inc(s_scatter, 16)

            def iteration(t, last):
                if not last:
                    gather(t + 1)
                add_rows(t - 1)

            gather(0)
            gather(1)
            count = iterate(pool, iteration)
            add_rows(count - 1)
            pool.wait_ge(s_scatter, 16 * count)

    s_ln2w, s_var2, s_rstd2, s_y = sem("ln2_weights_landed"), sem("ln2_variance"), sem("ln2_rstd"), sem("y_ready")
    s_acc = s_x
    s_out = sem("y_stored")
    ln2g_sb = at("ln2g_sb", 186, [P, D])
    ln2b_sb = at("ln2b_sb", 190, [P, D])

    with nc.Block() as block:

        @block.sync
        def _(sp):
            for t in range(NT):
                sp.dma_start(res[:, t, :], acc_rows[t * P:(t + 1) * P, :]).then_inc(s_acc[t], 16)
                if t == 0:
                    sp.dma_start(ln2g_sb[:], bcast(ln2_g[0], D)).then_inc(s_ln2w, 16)
                    sp.dma_start(ln2b_sb[:], bcast(ln2_b[0], D)).then_inc(s_ln2w, 16)
            for t in range(NT):
                sp.wait_ge(s_y, t + 1)
                dst = y_prompt[0, t * P:(t + 1) * P, :] if t < NT_P else y_sample[0, (t - NT_P) * P:(t - NT_P + 1) * P, :]
                sp.dma_start(dst, res[:, t, :]).then_inc(s_out, 16)
            sp.wait_ge(s_out, 16 * NT)

        @block.gpsimd
        def _(pool):
            for t in range(NT):
                pool.wait_ge(s_var2, t + 1)
                nc.gpsimd.tensor_tensor(rstd[:, t:t + 1], mv[:, t, 1:2], minus_half[:, 0:1], ALU.pow).then_inc(s_rstd2, 1)

        @block.vector
        def _(dve):
            for t in range(NT):
                dve.wait_ge(s_acc[t], 32)
                nc.vector.bn_stats(stats[:, t % 2, 0, :], res[:, t, 0:HW])
                then(nc.vector.bn_stats(stats[:, t % 2, 1, :], res[:, t, HW:D]))
                then(nc.vector.bn_aggr(mv[:, t, :], stats[:, t % 2, :, :].rearrange("p a b -> p (a b)")))
                nc.vector.tensor_scalar_add(mv[:, t, 1:2], mv[:, t, 1:2], LN_EPS).then_inc(s_var2, 1)
                if t == 0:
                    dve.wait_ge(s_ln2w, 32)
                then(nc.vector.scalar_tensor_tensor(out=res[:, t, :], in0=res[:, t, :], scalar=mv[:, t, 0:1], in1=ln2g_sb[:],
                                                    op0=ALU.subtract, op1=ALU.mult))
                dve.wait_ge(s_rstd2, t + 1)
                nc.vector.scalar_tensor_tensor(out=res[:, t, :], in0=res[:, t, :], scalar=rstd[:, t:t + 1], in1=ln2b_sb[:],
                                               op0=ALU.mult, op1=ALU.add).then_inc(s_y, 1)


def tables():
    import numpy as np

    pos = np.concatenate([np.arange(SEQ_P), np.arange(SEQ_S)]).astype(np.float32)
    inv = (1.0 / (np.float32(10000.0) ** (np.arange(0, ROPE, 2, dtype=np.float32) / np.float32(ROPE)))).astype(np.float32)
    ang = pos[:, None] * inv[None, :]
    by_tile = lambda a: np.ascontiguousarray(a.astype(np.float32).reshape(NT, P, HALF).transpose(1, 0, 2))
    dist = -np.abs(np.arange(P)[:, None] - (np.arange(ALIBI_W)[None, :] - (SEQ_P - P))).astype(np.float32)
    return {"rope_cos": by_tile(np.cos(ang)), "rope_sin": by_tile(np.sin(ang)), "alibi": dist}


_INS = ["x_prompt", "x_sample", "ln0_g", "ln0_b", "w_in", "g_q", "g_kv", "w_uq", "w_ukv", "lam_q1", "lam_k1",
        "lam_q2", "lam_k2", "g_sub", "w_o", "ln1_g", "ln1_b", "w_router", "b_router", "w_gate", "w_up",
        "w_down", "ln2_g", "ln2_b"]


def kernel(**inputs):
    import numpy as np
    import concourse.bacc as bacc
    from concourse.bass_utils import run_bass_kernel_spmd

    nc = bacc.Bacc("TRN2", target_bir_lowering=False, num_devices=1)
    arrays, args = {}, {}
    for name, a in [(n, inputs[n]) for n in _INS] + list(tables().items()):
        arrays[f"in_{name}"] = np.ascontiguousarray(a)
        args[name] = nc.dram_tensor(f"in_{name}", arrays[f"in_{name}"].shape, F, kind="ExternalInput").ap()
    for name, n in (("y_prompt", SEQ_P), ("y_sample", SEQ_S)):
        args[name] = nc.dram_tensor(name, (1, n, D), F, kind="ExternalOutput").ap()
    encoder_trunk(nc, **args)
    r = run_bass_kernel_spmd(nc, [arrays], core_ids=[0])
    return tuple(r.results[0][name] for name in ("y_prompt", "y_sample"))
```

```python
import math

import concourse.bass as bass
from concourse import mybir

F = mybir.dt.float32
FR = mybir.dt.float32r
I32 = mybir.dt.int32
ALU = mybir.AluOpType
ACT = mybir.ActivationFunctionType
AX = mybir.AxisListType.X

P = 128
D = 1024
KD = D // P
SEQ_P, SEQ_S = 512, 256
NT_P, NT_S = SEQ_P // P, SEQ_S // P
NT = NT_P + NT_S
TOK = NT * P
HEADS = 8
NOPE, ROPE, VDIM = 64, 32, 64
HALF = ROPE // 2
QK = NOPE + ROPE
QR, KVR = 256, 128
CW = QR + KVR + ROPE
DH = 4
DHD = 64
DW = DH * 2 * DHD
IN_W = CW + 3 * DW
NE, NG, EPG = 16, 4, 4
FF = 512
LN_EPS, RMS_EPS = 1e-5, 1e-6
ALPHA = 2.0 ** 0.25
LAM_INIT = 0.2
MLA_SCALE = QK ** -0.5
DIFF_SCALE = DHD ** -0.5
ALIBI_W = 2 * SEQ_P - P
SEQS = ((0, SEQ_P, NT_P), (SEQ_P, SEQ_S, NT_S))
MAX_MORE = (2 * TOK - 1) // P
MAX_TILES = NE + MAX_MORE + 1
KB = 1024


def encoder_trunk(nc, x_prompt, x_sample, ln0_g, ln0_b, w_in, g_q, g_kv, w_uq, w_ukv, lam_q1, lam_k1,
                  lam_q2, lam_k2, g_sub, w_o, ln1_g, ln1_b, w_router, b_router, w_gate, w_up, w_down,
                  ln2_g, ln2_b, rope_cos, rope_sin, alibi, y_prompt, y_sample):
    base = 16640
    used = [0]

    def at(name, kb, shape, dt=F):
        n = 1
        for s in shape[1:]:
            n *= s
        assert base + kb * KB + 4 * n <= nc.sbuf_usable_end, name
        return nc.alloc_sbuf_tensor_at(name, list(shape), dt, offset=base + int(kb * KB))

    def small(name, shape, dt=F):
        n = 4
        for s in shape[1:]:
            n *= s
        off = used[0]
        used[0] += (n + 31) // 32 * 32
        assert used[0] <= 6 * KB, name
        return nc.alloc_sbuf_tensor_at(name, list(shape), dt, offset=base + off)

    def sem(name):
        return nc.alloc_semaphore(name)

    def f32(ap):
        return ap.bitcast(F)

    def bcast(vec, n):
        return vec.rearrange("(a n) -> a n", a=1).to_broadcast([P, n])

    ident = small("ident", [P, P])
    cos = small("cos", [P, NT, HALF])
    sin = small("sin", [P, NT, HALF])
    minus_half = small("minus_half", [P, 2 * NT])
    gq_col = small("gq_col", [P, 3])
    gsub_col = small("gsub_col", [P, 1])
    lam_col = small("lam_col", [P, 1])
    res = at("res", 6, [P, NT, D])
    psum = [nc.alloc_psum_tensor(f"bank{i}", [P, 512], F) for i in range(8)]

    xT_h = at("xT_h", 30, [P, KD, TOK], FR)
    xT_l = at("xT_l", 54, [P, KD, TOK], FR)
    WB = 256
    w_raw = [at(f"w_raw{i}", 78 + 8 * i, [P, KD * WB]) for i in range(2)]
    w_h = [at(f"w_h{i}", 94 + 8 * i, [P, KD * WB], FR) for i in range(2)]
    w_l = [at(f"w_l{i}", 110 + 8 * i, [P, KD * WB], FR) for i in range(2)]
    dqT = at("dqT", 126, [P, DH, TOK])
    dkT = at("dkT", 138, [P, DH, TOK])
    dv = at("dv", 150, [P, NT, DW])
    cT_h = at("cT_h", 162, [P, 3, TOK], FR)
    cT_l = at("cT_l", 171, [P, 3, TOK], FR)
    craw = at("craw", 180, [P, NT, CW])
    ln_g = at("ln_g", 190, [P, D])
    ln_b = at("ln_b", 194, [P, D])
    junk = at("junk", 198, [P, QR])
    kr = at("kr", 199, [P, NT, ROPE])
    ropetmp = at("ropetmp", 200, [P, 4, HEADS, HALF])
    lam_in = at("lam_in", 202, [P, 4, DHD])
    lam_prod = at("lam_prod", 203, [P, 2, DHD])
    q_tok = at("q_tok", 30, [P, NT, HEADS, QK])
    k_tok = at("k_tok", 48, [P, NT, HEADS, QK])
    v_tok = at("v_tok", 66, [P, NT, HEADS, VDIM])
    stats = small("stats", [P, 2, 2, 6])
    mv = small("mv", [P, NT, 2])
    rstd = small("rstd", [P, NT])
    ssq = small("ssq", [P, 2, NT])
    rms = small("rms", [P, 2, NT])
    lam_e = small("lam_e", [P, 2])
    lam_s = small("lam_s", [P, 2])

    s_const = sem("const_landed")
    s_lam_in = sem("lam_landed")
    s_lnw = sem("ln_weights_landed")
    s_x = [sem(f"x_landed{t}") for t in range(NT)]
    s_w = [sem(f"w_landed{i}") for i in range(2)]
    s_ident = sem("ident_ready")
    s_var = sem("variance_ready")
    s_rstd = sem("rstd_ready")
    s_dve = sem("dve_step")
    s_pool = sem("pool_step")
    s_act = sem("act_step")
    s_xln = sem("xln_ready")
    s_tp = sem("transposed")
    s_th = sem("transposed_high")
    s_tl = sem("transposed_low")
    s_wh = sem("w_high")
    s_wl = sem("w_low")
    s_proj = sem("projected")
    s_pev = sem("projection_out")
    s_ssq = sem("square_sums_ready")
    s_rms = sem("rms_ready")
    s_kr = sem("k_rope_ready")
    s_lam = sem("lambda_parts")
    s_kfill = sem("k_rope_filled")

    dve_steps = [0]

    def step(ins):
        dve_steps[0] += 1
        ins.then_inc(s_dve, 1)
        return dve_steps[0]

    def then(ins):
        nc.vector.wait_ge(s_dve, step(ins))

    w_in_v = w_in[0].rearrange("(c p) n -> p c n", p=P)
    blocks = [(w_in_v[:, :, 0:QR], KD, QR), (w_in_v[:, :, QR:CW], KD, CW - QR)]
    for i in range(3 * DW // WB):
        blocks.append((w_in_v[:, :, CW + i * WB:CW + (i + 1) * WB], KD, WB))
    blocks.append((w_uq[0].rearrange("(c p) n -> p c n", p=P), QR // P, HEADS * QK))
    blocks.append((w_ukv[0].rearrange("(c p) n -> p c n", p=P), 1, HEADS * (NOPE + VDIM)))
    NB = len(blocks)
    UQ = NB - 2
    BANKS = 6

    def wview(t, b):
        _, c, n = blocks[b]
        return t[b % 2][:, 0:c * n].rearrange("p (c n) -> p c n", c=c)

    def groups(b):
        if b < 2:
            return [("c", b, t) for t in range(NT)]
        if b < 6:
            return [("qk", b, f, s) for f in range(2) for s in range(2)]
        if b < 8:
            return [("v", b, t) for t in range(NT)]
        return [("uq" if b == UQ else "ukv", b, t, hf) for t in range(NT) for hf in range(2)]

    order = [g for t in range(NT) for g in (("c", 0, t), ("c", 1, t))]
    for b in range(2, NB):
        order += groups(b)
    first_of = {b: next(i for i, g in enumerate(order) if g[1] == b) for b in range(NB)}
    last_of = {b: max(i for i, g in enumerate(order) if g[1] == b) for b in range(NB)}
    NX, NC = 2 * NT, 6

    def xhalf(t, hf, hi_lo):
        return hi_lo[:, 4 * hf:4 * hf + 4, t * P:(t + 1) * P]

    with nc.Block() as block:

        @block.sync
        def _(sp):
            def load_w(b):
                if b >= 2:
                    sp.wait_ge(s_wl, 2 * (b - 2) + 2)
                sp.dma_start(wview(w_raw, b), blocks[b][0]).then_inc(s_w[b % 2], 16)

            def load_x(t):
                src = x_prompt[0, t * P:(t + 1) * P, :] if t < NT_P else x_sample[0, (t - NT_P) * P:(t - NT_P + 1) * P, :]
                sp.dma_start(res[:, t, :], src).then_inc(s_x[t], 16)

            load_x(0)
            sp.dma_start(ln_g[:], bcast(ln0_g, D)).then_inc(s_lnw, 16)
            sp.dma_start(ln_b[:], bcast(ln0_b, D)).then_inc(s_lnw, 16)
            load_w(0)
            load_x(1)
            load_w(1)
            for t in range(2, NT):
                load_x(t)
            sp.dma_start(cos[:], rope_cos).then_inc(s_const, 16)
            sp.dma_start(sin[:], rope_sin).then_inc(s_const, 16)
            with nc.allow_non_contiguous_dma("a column of gains"):
                sp.dma_start(gq_col[:, 0:2], g_q[0].rearrange("(c p) -> p c", p=P)).then_inc(s_const, 16)
                sp.dma_start(gq_col[:, 2:3], g_kv[0].rearrange("(c p) -> p c", p=P)).then_inc(s_const, 16)
                sp.dma_start(gsub_col[:], g_sub[0].rearrange("(c p) -> p c", p=P)).then_inc(s_const, 16)
            for i, v in enumerate((lam_q1, lam_k1, lam_q2, lam_k2)):
                sp.dma_start(lam_in[:, i, :], bcast(v[0], DHD)).then_inc(s_lam_in, 16)
            for b in range(2, NB):
                load_w(b)

        @block.gpsimd
        def _(pool):
            nc.gpsimd.memset(ident[:], 0.0).then_inc(s_pool, 1)
            nc.gpsimd.memset(minus_half[:], -0.5).then_inc(s_pool, 1)
            pool.wait_ge(s_pool, 2)
            nc.gpsimd.affine_select(out=ident[:], in_=ident[:], compare_op=ALU.not_equal, fill=1.0, base=0,
                                    pattern=[[-1, P]], channel_multiplier=1).then_inc(s_ident, 1)
            for t in range(NT):
                pool.wait_ge(s_var, t + 1)
                nc.gpsimd.tensor_tensor(rstd[:, t:t + 1], mv[:, t, 1:2], minus_half[:, 0:1], ALU.pow).then_inc(s_rstd, 1)
                if t < 2:
                    w = blocks[t][1] * blocks[t][2] // 2
                    for hf in range(2):
                        ws = slice(hf * w, (hf + 1) * w)
                        pool.wait_ge(s_wh, 2 * t + hf + 1)
                        nc.gpsimd.tensor_tensor(w_l[t][:, ws], w_raw[t][:, ws], f32(w_h[t][:, ws]), ALU.subtract).then_inc(s_wl, 1)
            pool.wait_ge(s_ssq, 1)
            nc.gpsimd.tensor_tensor(rms[:].rearrange("p a t -> p (a t)"), ssq[:].rearrange("p a t -> p (a t)"),
                                    minus_half[:], ALU.pow).then_inc(s_rms, 1)
            pool.wait_ge(s_kr, 1)
            for t in range(NT):
                pool.wait_ge(s_pev, last_of[7] + 1)
                nc.gpsimd.tensor_copy(k_tok[:, t, :, NOPE:QK],
                                      kr[:, t, :].unsqueeze(1).to_broadcast([P, HEADS, ROPE])).then_inc(s_kfill, 1)

        @block.tensor
        def _(pe):
            def transpose_x(t):
                pe.wait_ge(s_xln, t + 1)
                for hf in range(2):
                    q = 2 * t + hf
                    if q >= 2:
                        pe.wait_ge(s_tl, q - 1)
                    for j in range(4):
                        c = 4 * hf + j
                        last = nc.tensor.transpose(psum[q % 2][:, j * P:(j + 1) * P], res[:, t, c * P:(c + 1) * P], ident[:])
                    last.then_inc(s_tp, 1)

            def transpose_c(p):
                pe.wait_ge(s_pev, last_of[1] + 1)
                q = NX + p
                j, (t0, _, nt) = p // 2, SEQS[p % 2]
                pe.wait_ge(s_tl, q - 1)
                for i in range(nt):
                    last = nc.tensor.transpose(psum[q % 2][:, i * P:(i + 1) * P],
                                               craw[:, t0 // P + i, j * P:(j + 1) * P], ident[:])
                last.then_inc(s_tp, 1)

            def product(o, out, pairs):
                if o >= BANKS:
                    pe.wait_ge(s_pev, o - BANKS + 1)
                n = 3 * len(pairs)
                i = 0
                second_half = 2 * order[o][1] + 2 if o == first_of[order[o][1]] and len(pairs) > 1 else 0
                for ah, al, bh, bl in pairs:
                    if second_half and i == n // 2:
                        pe.wait_ge(s_wl, second_half)
                    for a, b in ((ah, bh), (al, bh), (ah, bl)):
                        last = nc.tensor.matmul(out, a, b, start=(i == 0), stop=(i == n - 1))
                        i += 1
                return last

            pe.wait_ge(s_ident, 1)
            transpose_x(0)
            for o, g in enumerate(order):
                kind, b = g[0], g[1]
                _, kc, n = blocks[b]
                wh, wl = wview(w_h, b), wview(w_l, b)
                bank = psum[2 + o % BANKS]
                if kind == "c" and b == 1 and g[2] + 1 < NT:
                    transpose_x(g[2] + 1)
                if kind == "c" and b == 0:
                    pe.wait_ge(s_tl, 2 * g[2] + 2)
                if o == first_of[b]:
                    pe.wait_ge(s_wl, 2 * b + (1 if kc > 1 else 2))
                if 0 <= o - first_of[3] - 1 < NC:
                    transpose_c(o - first_of[3] - 1)
                if o == first_of[UQ]:
                    pe.wait_ge(s_tl, NX + 6)
                if kind in ("c", "v"):
                    t = g[2]
                    ts = slice(t * P, (t + 1) * P)
                    last = product(o, bank[:, 0:n], [(xT_h[:, c, ts], xT_l[:, c, ts], wh[:, c, :], wl[:, c, :])
                                                     for c in range(kc)])
                elif kind == "qk":
                    t0, nn, _ = SEQS[g[3]]
                    fs, ts = slice(g[2] * P, (g[2] + 1) * P), slice(t0, t0 + nn)
                    last = product(o, bank[:, 0:nn], [(wh[:, c, fs], wl[:, c, fs], xT_h[:, c, ts], xT_l[:, c, ts])
                                                      for c in range(kc)])
                else:
                    t, hf = g[2], g[3]
                    ts, c0 = slice(t * P, (t + 1) * P), (0 if kind == "uq" else 2)
                    w = n // 2
                    last = product(o, bank[:, 0:w], [(cT_h[:, c0 + c, ts], cT_l[:, c0 + c, ts],
                                                      wh[:, c, hf * w:(hf + 1) * w], wl[:, c, hf * w:(hf + 1) * w])
                                                     for c in range(kc)])
                last.then_inc(s_proj, 1)

        @block.scalar
        def _(act):
            def x_high(t):
                for hf in range(2):
                    q = 2 * t + hf
                    act.wait_ge(s_tp, q + 1)
                    nc.scalar.activation(xhalf(t, hf, xT_h), psum[q % 2][:].rearrange("p (c n) -> p c n", c=4),
                                         ACT.Copy).then_inc(s_th, 1)

            def c_high(p):
                act.wait_ge(s_const, 5 * 16)
                q = NX + p
                j, (t0, nn, _) = p // 2, SEQS[p % 2]
                act.wait_ge(s_tp, q + 1)
                nc.scalar.activation(cT_h[:, j, t0:t0 + nn], psum[q % 2][:, 0:nn], ACT.Copy,
                                     scale=gq_col[:, j:j + 1]).then_inc(s_th, 1)

            def w_high(b):
                act.wait_ge(s_w[b % 2], 16 * (b // 2 + 1))
                if b >= 2:
                    act.wait_ge(s_proj, last_of[b - 2] + 1)
                w = blocks[b][1] * blocks[b][2] // 2
                for hf in range(2):
                    nc.scalar.activation(w_h[b % 2][:, hf * w:(hf + 1) * w], w_raw[b % 2][:, hf * w:(hf + 1) * w],
                                         ACT.Copy).then_inc(s_wh, 1)

            def c_squares():
                act.wait_ge(s_pev, last_of[1] + 1)
                k = 0
                for t in range(NT):
                    for i, (lo, n) in enumerate(((0, QR), (QR, KVR))):
                        if k:
                            act.wait_ge(s_act, k)
                        nc.scalar.activation(junk[:, 0:n], craw[:, t, lo:lo + n], ACT.Square,
                                             accum_out=ssq[:, i, t:t + 1]).then_inc(s_act, 1)
                        k += 1

            def out(o):
                g = order[o]
                kind, b = g[0], g[1]
                bank = psum[2 + o % BANKS]
                act.wait_ge(s_proj, o + 1)
                if kind == "c":
                    t = g[2]
                    lo, n = (0, QR) if b == 0 else (QR, CW - QR)
                    nc.scalar.activation(craw[:, t, lo:lo + n], bank[:, 0:n], ACT.Copy).then_inc(s_pev, 1)
                elif kind == "qk":
                    h = 2 * (b - 2) + g[2]
                    t0, nn, _ = SEQS[g[3]]
                    dst = dqT[:, h, t0:t0 + nn] if h < DH else dkT[:, h - DH, t0:t0 + nn]
                    nc.scalar.activation(dst, bank[:, 0:nn], ACT.Copy,
                                         scale=DIFF_SCALE if h < DH else 1.0).then_inc(s_pev, 1)
                elif kind == "v":
                    nc.scalar.activation(dv[:, g[2], (b - 6) * WB:(b - 5) * WB], bank[:, 0:WB], ACT.Copy).then_inc(s_pev, 1)
                elif kind == "uq":
                    t, hf = g[2], g[3]
                    nc.scalar.activation(q_tok[:, t, 4 * hf:4 * hf + 4, :],
                                         bank[:, 0:4 * QK].rearrange("p (h n) -> p h n", h=4),
                                         ACT.Copy, scale=rms[:, 0, t:t + 1]).then_inc(s_pev, 1)
                else:
                    t, hf = g[2], g[3]
                    kv = bank[:].rearrange("p (h n) -> p h n", h=4)
                    nc.scalar.activation(k_tok[:, t, 4 * hf:4 * hf + 4, 0:NOPE], kv[:, :, 0:NOPE], ACT.Copy,
                                         scale=rms[:, 1, t:t + 1])
                    nc.scalar.activation(v_tok[:, t, 4 * hf:4 * hf + 4, :], kv[:, :, NOPE:NOPE + VDIM], ACT.Copy,
                                         scale=rms[:, 1, t:t + 1]).then_inc(s_pev, 1)

            w_high(0)
            x_high(0)
            w_high(1)
            for o, g in enumerate(order):
                b = g[1]
                if g[0] == "c" and b == 1 and g[2] + 1 < NT:
                    x_high(g[2] + 1)
                if o == last_of[1]:
                    w_high(2)
                out(o)
                if 0 <= o - first_of[3] < NC:
                    c_high(o - first_of[3])
                if o == last_of[1]:
                    c_squares()
                    act.wait_ge(s_lam, 1)
                    nc.scalar.activation(lam_e[:], lam_s[:], ACT.Exp).then_inc(s_lam, 1)
                    w_high(3)
                elif o == last_of[b] and b + 2 < NB and b >= 2:
                    w_high(b + 2)
                if o == last_of[5]:
                    act.wait_ge(s_rms, 2)

        @block.vector
        def _(dve):
            def ln_stats(t):
                dve.wait_ge(s_x[t], 16)
                for i in range(2):
                    last = nc.vector.bn_stats(stats[:, t % 2, i, :], res[:, t, i * 512:(i + 1) * 512])
                    then(last)
                then(nc.vector.bn_aggr(mv[:, t, :], stats[:, t % 2, :, :].rearrange("p a b -> p (a b)")))
                nc.vector.tensor_scalar_add(mv[:, t, 1:2], mv[:, t, 1:2], LN_EPS).then_inc(s_var, 1)

            def ln_apply(t):
                if t == 0:
                    dve.wait_ge(s_lnw, 32)
                then(nc.vector.scalar_tensor_tensor(out=res[:, t, :], in0=res[:, t, :], scalar=mv[:, t, 0:1], in1=ln_g[:],
                                                    op0=ALU.subtract, op1=ALU.mult))
                dve.wait_ge(s_rstd, t + 1)
                nc.vector.scalar_tensor_tensor(out=res[:, t, :], in0=res[:, t, :], scalar=rstd[:, t:t + 1], in1=ln_b[:],
                                               op0=ALU.mult, op1=ALU.add).then_inc(s_xln, 1)

            def x_low(t):
                for hf in range(2):
                    q = 2 * t + hf
                    dve.wait_ge(s_th, q + 1)
                    nc.vector.tensor_tensor(xhalf(t, hf, xT_l), psum[q % 2][:].rearrange("p (c n) -> p c n", c=4),
                                            f32(xhalf(t, hf, xT_h)), ALU.subtract).then_inc(s_tl, 1)

            def w_low(b):
                w = blocks[b][1] * blocks[b][2] // 2
                for hf in range(2):
                    dve.wait_ge(s_wh, 2 * b + hf + 1)
                    nc.vector.tensor_tensor(w_l[b % 2][:, hf * w:(hf + 1) * w], w_raw[b % 2][:, hf * w:(hf + 1) * w],
                                            f32(w_h[b % 2][:, hf * w:(hf + 1) * w]), ALU.subtract).then_inc(s_wl, 1)

            def rotate(x1, x2, c, s, shape):
                a = [ropetmp[:, i] for i in range(4)] if shape == "heads" else [
                    ropetmp[:, i].rearrange("p h n -> p (h n)")[:, 0:NT * HALF].rearrange("p (t n) -> p t n", n=HALF)
                    for i in range(4)]
                nc.vector.tensor_tensor(a[0], x1, c, ALU.mult)
                nc.vector.tensor_tensor(a[1], x2, s, ALU.mult)
                nc.vector.tensor_tensor(a[2], x2, c, ALU.mult)
                then(nc.vector.tensor_tensor(a[3], x1, s, ALU.mult))
                nc.vector.tensor_tensor(x1 if shape == "heads" else kr[:, :, 0:HALF], a[0], a[1], ALU.subtract)
                return nc.vector.tensor_tensor(x2 if shape == "heads" else kr[:, :, HALF:ROPE], a[2], a[3], ALU.add)

            ln_stats(0)
            ln_apply(0)
            for t in range(NT):
                if t + 1 < NT:
                    ln_stats(t + 1)
                x_low(t)
                if t + 1 < NT:
                    ln_apply(t + 1)
            dve.wait_ge(s_lam_in, 64)
            lv = lam_in[:].rearrange("p (a b) n -> p a b n", b=2)
            then(nc.vector.tensor_tensor(lam_prod[:], lv[:, :, 0, :], lv[:, :, 1, :], ALU.mult))
            nc.vector.reduce_sum(lam_s[:], lam_prod[:], axis=AX).then_inc(s_lam, 1)
            w_low(2)
            dve.wait_ge(s_act, 2 * NT)
            nc.vector.tensor_scalar(ssq[:, 0, :], ssq[:, 0, :], 1.0 / QR, RMS_EPS, ALU.mult, ALU.add)
            nc.vector.tensor_scalar(ssq[:, 1, :], ssq[:, 1, :], 1.0 / KVR, RMS_EPS, ALU.mult, ALU.add).then_inc(s_ssq, 1)
            dve.wait_ge(s_lam, 2)
            then(nc.vector.tensor_tensor(lam_col[:], lam_e[:, 0:1], lam_e[:, 1:2], ALU.subtract))
            then(nc.vector.tensor_scalar_add(lam_col[:], lam_col[:], LAM_INIT))
            w_low(3)
            dve.wait_ge(s_rms, 1)
            nc.vector.tensor_scalar_mul(rms[:, 0, :], rms[:, 0, :], MLA_SCALE).then_inc(s_rms, 1)
            dve.wait_ge(s_const, 5 * 16)
            nc.vector.tensor_scalar_mul(gsub_col[:], gsub_col[:], 1.0 - LAM_INIT)
            rotate(craw[:, :, QR + KVR:QR + KVR + HALF], craw[:, :, QR + KVR + HALF:CW], cos[:], sin[:], "kr").then_inc(s_kr, 1)
            for b in range(4, NB):
                w_low(b)
                for p in {4: range(0, 4), 5: range(4, NC)}.get(b, ()):
                    q = NX + p
                    j, (t0, nn, _) = p // 2, SEQS[p % 2]
                    dve.wait_ge(s_th, q + 1)
                    nc.vector.scalar_tensor_tensor(out=cT_l[:, j, t0:t0 + nn], in0=psum[q % 2][:, 0:nn],
                                                   scalar=gq_col[:, j:j + 1], in1=f32(cT_h[:, j, t0:t0 + nn]),
                                                   op0=ALU.mult, op1=ALU.subtract).then_inc(s_tl, 1)
            for t in range(NT):
                dve.wait_ge(s_pev, first_of[UQ] + 2 * t + 2)
                then(rotate(q_tok[:, t, :, NOPE:NOPE + HALF], q_tok[:, t, :, NOPE + HALF:QK],
                            cos[:, t, :].unsqueeze(1).to_broadcast([P, HEADS, HALF]),
                            sin[:, t, :].unsqueeze(1).to_broadcast([P, HEADS, HALF]), "heads"))

    def wait(eng, semaphore, value):
        if not isinstance(value, int) or value > 0:
            eng.wait_ge(semaphore, value)
            if eng is nc.gpsimd and not isinstance(value, int):
                eng.sem_inc(s_passed, 1)

    s_passed = sem("passed_wait")

    def over(eng, n, body):
        body(0, True, False)
        with eng.Fori(1, n - 1) as i:
            body(i, False, False)
        body(n - 1, False, True)

    AHEAD, BEHIND = 4, 4
    mixD_h = at("mixD_h", 162, [P, DH, TOK], FR)
    mixD_l = at("mixD_l", 174, [P, DH, TOK], FR)
    q_h = [[at(f"q_h{x}{m}", 78 + 6 * m + 4 * x, [P, SEQS[x][1]], FR) for m in range(2)] for x in range(2)]
    q_l = [[at(f"q_l{x}{m}", 80 + 6 * m + 3 * x, [P, SEQS[x][1]], FR) for m in range(2)] for x in range(2)]
    kk_h = [at(f"kk_h{x}", 90 + 4 * x, [P, SEQS[x][1]], FR) for x in range(2)]
    kk_l = [at(f"kk_l{x}", 92 + 3 * x, [P, SEQS[x][1]], FR) for x in range(2)]
    vv_h = [at(f"vv_h{x}", 96 + 4 * x, [P, SEQS[x][2], P], FR) for x in range(2)]
    vv_l = [at(f"vv_l{x}", 98 + 3 * x, [P, SEQS[x][2], P], FR) for x in range(2)]
    dpT_h = [at(f"dpT_h{i}", 102 + 4 * i, [P, 512], FR) for i in range(2)]
    dpT_l = [at(f"dpT_l{i}", 104 + 4 * i, [P, 512], FR) for i in range(2)]
    o_sb = [at(f"o_sb{i}", 110 + 0.5 * i, [P, P]) for i in range(2)]
    o_junk = at("o_junk", 111, [P, P])
    bias_t = at("bias_t", 112, [P, ALIBI_W])
    NEE = 3
    ee = [[at(f"ee{i}{m}", 186 + 4 * i + 2 * m, [P, 512]) for m in range(2)] for i in range(NEE)]
    pp = [at(f"pp{i}", 198 + 2 * i, [P, 512]) for i in range(2)]
    negmax = small("negmax", [P, NEE, 2])
    esum = small("esum", [P, NEE, 2])
    erec = small("erec", [P, NEE, 2])
    osq = small("osq", [P, 2])
    orstd = small("orstd", [P, 2])

    s_alibi = sem("alibi_landed")
    s_zero = sem("zero_rows_ready")
    s_qkh, s_ql, s_kl = sem("diff_qk_high"), sem("diff_q_low"), sem("diff_k_low")
    s_vh, s_vl = sem("diff_v_high"), sem("diff_v_low")
    s_sc, s_bias, s_exp = sem("diff_scores"), sem("diff_biased"), sem("diff_exp")
    s_rec, s_e2, s_p = sem("diff_reciprocals"), sem("diff_second_scaled"), sem("diff_probs")
    s_pt, s_pth, s_ptl = sem("diff_probs_T"), sem("diff_probs_T_high"), sem("diff_probs_T_low")
    s_pv, s_sq, s_or = sem("diff_out"), sem("diff_out_squares"), sem("diff_out_rstd")
    s_osb, s_ot, s_oth, s_otl = sem("diff_out_normed"), sem("diff_out_T"), sem("mixD_high"), sem("mixD_low")

    def dtile(i):
        x = int(i >= NT_P)
        return x, SEQS[x][1], SEQS[x][2], i - NT_P * x

    def on_tile(n, slot, first, last, h, work, distance):
        j = slot + distance
        if not (first and j < 0) and not (last and j >= n):
            work(h + j // n, j % n)

    def cuts(i, last, h, *work):
        for slots, cut in work:
            if i in slots and not (last and slots[i][0]):
                cut(h + slots[i][0], slots[i][1])

    def stage(hp, k):
        x = k % 2
        t0, _, nt = SEQS[x]
        for dst, src in ((stage_q, q_tok), (stage_k, k_tok)):
            last = nc.gpsimd.tensor_copy(dst[x][:].unsqueeze(2), src[:, t0 // P:t0 // P + nt, bass.ds(2 * hp + k // 2, 1), :])
        last.then_inc(m_stage, 1)

    stage_q = [at(f"stage_q{x}", 202 + 3 * x, [P, SEQS[x][2], QK]) for x in range(2)]
    stage_k = [at(f"stage_k{x}", 203.5 + 2.25 * x, [P, SEQS[x][2], QK]) for x in range(2)]
    m_stage = sem("mla_staged")

    def head_slots(first, last):
        return range(-AHEAD if first else 0, NT + (BEHIND if last else 0))

    def g_of(h, i):
        return h * NT + i

    QK_HIGH, QK_LOW = {0: (1, 0), 3: (1, 1)}, {1: (1, 0), 4: (1, 1)}
    V_HIGH, V_LOW = {5: (1, 0), 2: (0, 1)}, {0: (0, 0), 3: (0, 1)}

    turned_probs, turned_out = psum[4], psum[5][:, 0:P]

    def out_bank(i):
        return psum[6 + i % 2][:, 0:P]

    TP = 2 * NT
    M_AHEAD, M_BEHIND = 4, 3
    START = (0, NT_P, NT, NT + NT_P)
    mixM_h = at("mixM_h", 126, [P, HEADS // 2, TOK], FR)
    mixM_l = at("mixM_l", 138, [P, HEADS // 2, TOK], FR)
    mq_h = [at(f"mq_h{x}", 83 + 8 * x, [P, SEQS[x][1]], FR) for x in range(2)]
    mq_l = [at(f"mq_l{x}", 85 + 7 * x, [P, SEQS[x][1]], FR) for x in range(2)]
    mk_h = [at(f"mk_h{x}", 87 + 6 * x, [P, SEQS[x][1]], FR) for x in range(2)]
    mk_l = [at(f"mk_l{x}", 89 + 5 * x, [P, SEQS[x][1]], FR) for x in range(2)]
    mv_h = [at(f"mv_h{x}", 95 + 4 * x, [P, SEQS[x][2], P], FR) for x in range(2)]
    mv_l = [at(f"mv_l{x}", 97 + 3 * x, [P, SEQS[x][2], P], FR) for x in range(2)]
    pT_h = [at(f"pT_h{x}", 102 + 16 * x, [P, SEQS[x][2], SEQS[x][1]], FR) for x in range(2)]
    pT_l = [at(f"pT_l{x}", 110 + 10 * x, [P, SEQS[x][2], SEQS[x][1]], FR) for x in range(2)]
    NME = 4
    me = [at(f"me{i}", 186 + 2 * i, [P, 512]) for i in range(NME)]
    SCORE_BANKS = (0, 1, 7)
    NSB = len(SCORE_BANKS)
    mmax = small("mmax", [P, NSB])
    msum = small("msum", [P, NSB])
    mrec = small("mrec", [P, NSB])

    m_tq = sem("mla_qk_T")
    m_qh, m_ql = sem("mla_qk_high"), sem("mla_qk_low")
    m_vh, m_vl = sem("mla_v_high"), sem("mla_v_low")
    m_sc, m_max, m_exp, m_rec = sem("mla_scores"), sem("mla_max"), sem("mla_exp"), sem("mla_reciprocal")
    m_p = [sem("mla_even_probs"), sem("mla_odd_probs")]
    m_pt, m_pth, m_ptl = sem("mla_probs_T"), sem("mla_probs_T_high"), sem("mla_probs_T_low")
    m_pv, m_mh, m_ml = sem("mla_out"), sem("mixM_high"), sem("mixM_low")

    def mtile(i):
        k = max(j for j in range(4) if START[j] <= i)
        x = k % 2
        return k, x, SEQS[x][1], SEQS[x][2], i - START[k]

    def pair_slots(first, last):
        return range(-M_AHEAD if first else 0, TP + (M_BEHIND if last else 0))

    STAGE_SLOTS = {2: (1, 0), 6: (1, 1), 8: (1, 2), 0: (0, 3)}
    TURN_SLOTS = {6: (1, 0), 10: (1, 1), 0: (0, 2), 4: (0, 3)}
    V_SLOTS = {0: (0, 0), 2: (0, 1)}
    PV_SLOTS = {4: (0, 0, (0, 1)), 5: (0, 0, (2, 3)), 7: (0, 1, (0, 1)), 10: (0, 2, (0, 1)), 11: (0, 2, (2, 3)),
                1: (-1, 3, (0, 1))}
    MIX_SLOTS = {6: (0, 0), 8: (0, 1), 0: (-1, 2), 2: (-1, 3)}

    def at_slot(slots, i, first, last, hp, f):
        if i >= 0 and i % TP in slots:
            d, *rest = slots[i % TP]
            d += i // TP
            if not (first and d < 0) and not (last and d > 0):
                f(hp + d, *rest)

    def unit_last(w_pair, k):
        return w_pair * TP + (START[k + 1] if k < 3 else TP) - 1

    def turn_unit(k, banks):
        x = k % 2
        for bank, src in zip(banks, (stage_q, stage_k)):
            for t in range(SEQS[x][2]):
                last = nc.tensor.transpose(psum[bank][0:QK, t * P:(t + 1) * P], src[x][:, t, :], ident[:])
            last.then_inc(m_tq, 1)

    def unit_high(k, j, bank):
        x = k % 2
        nc.scalar.activation((mq_h, mk_h)[j][x][0:QK, :], psum[bank][0:QK, 0:SEQS[x][1]], ACT.Copy).then_inc(m_qh, 1)

    def unit_low(k, j, bank):
        x = k % 2
        hi, lo = ((mq_h, mq_l), (mk_h, mk_l))[j]
        nc.vector.tensor_tensor(lo[x][0:QK, :], psum[bank][0:QK, 0:SEQS[x][1]], f32(hi[x][0:QK, :]), ALU.subtract).then_inc(m_ql, 1)

    with nc.Block() as block:

        @block.sync
        def _(sp):
            sp.dma_start(bias_t[:], alibi).then_inc(s_alibi, 16)

        @block.tensor
        def _(pe):
            def scores(h, i):
                x, n, _, qt = dtile(i)
                g = g_of(h, i)
                if qt == 0:
                    wait(pe, s_zero, 2 * x + 2)
                    wait(pe, s_ql, 4 * h + 2 * x + 2)
                    wait(pe, s_kl, 2 * h + x + 1)
                for m in range(2):
                    wait(pe, s_bias, 2 * g - 4 + m + 1)
                    qs = slice(qt * P, (qt + 1) * P)
                    out = psum[2 * (i % 2) + m][:, 0:n]
                    nc.tensor.matmul(out, q_h[x][m][:, qs], kk_h[x][:], start=True, stop=False)
                    nc.tensor.matmul(out, q_l[x][m][:, qs], kk_h[x][:], start=False, stop=False)
                    nc.tensor.matmul(out, q_h[x][m][:, qs], kk_l[x][:], start=False, stop=True).then_inc(s_sc, 1)

            def turn_probs(h, i):
                g = g_of(h, i)
                wait(pe, s_p, g + 1)
                wait(pe, s_ptl, g)
                for j in range(dtile(i)[2]):
                    t = nc.tensor.transpose(turned_probs[:, j * P:(j + 1) * P], pp[i % 2][:, j * P:(j + 1) * P], ident[:])
                t.then_inc(s_pt, 1)

            def output(h, i):
                x, _, nk, qt = dtile(i)
                g = g_of(h, i)
                wait(pe, s_ptl, g + 1)
                wait(pe, s_osb, g - 1)
                if qt == 0:
                    wait(pe, s_vl, 2 * h + x + 1)
                k = 0
                for j in range(nk):
                    js = slice(j * P, (j + 1) * P)
                    for a, b in ((dpT_h, vv_h), (dpT_l, vv_h), (dpT_h, vv_l)):
                        t = nc.tensor.matmul(out_bank(i), a[i % 2][:, js], b[x][:, j, :],
                                             start=(k == 0), stop=(k == 3 * nk - 1))
                        k += 1
                t.then_inc(s_pv, 1)

            def turn_output(h, i):
                g = g_of(h, i)
                wait(pe, s_osb, g + 1)
                wait(pe, s_otl, g)
                nc.tensor.transpose(turned_out, o_sb[i % 2][:], ident[:]).then_inc(s_ot, 1)

            def head(h, first, last):
                for i in head_slots(first, last):
                    on_tile(NT, i, first, last, h, turn_probs, 0)
                    on_tile(NT, i, first, last, h, output, -1)
                    on_tile(NT, i, first, last, h, scores, 4)
                    on_tile(NT, i, first, last, h, turn_output, -3)
                    if last and i == NT - 3:
                        pe.wait_ge(m_stage, 2)
                        pe.wait_ge(s_bias, 2 * DH * NT)
                        turn_unit(0, (0, 1))
                        turn_unit(1, (2, 3))

            over(pe, DH, head)

        @block.scalar
        def _(act):
            def cut_qk(h, x):
                t0, n, _ = SEQS[x]
                wait(act, s_sc, 2 * g_of(h, (NT_P - 1, NT - 1)[x] - NT) + 2)
                nc.scalar.activation(kk_h[x][:], dkT[:, h, t0:t0 + n], ACT.Copy).then_inc(s_qkh, 1)
                for m in range(2):
                    r = slice(64 * m, 64 * m + 64)
                    nc.scalar.activation(q_h[x][m][r, :], dqT[r, h, t0:t0 + n], ACT.Copy).then_inc(s_qkh, 1)

            def cut_v(h, x):
                t0, _, nt = SEQS[x]
                wait(act, s_pv, g_of(h, (NT_P - 1, NT - 1)[x] - NT) + 1)
                nc.scalar.activation(vv_h[x][:], dv[:, t0 // P:t0 // P + nt, bass.ds(h * P, P)], ACT.Copy).then_inc(s_vh, 1)

            def exp(h, i):
                n = dtile(i)[1]
                for m in range(2):
                    wait(act, s_bias, 2 * g_of(h, i) + m + 1)
                    e = ee[i % NEE][m][:, 0:n]
                    nc.scalar.activation(e, e, ACT.Exp, scale=-1.0, bias=negmax[:, i % NEE, m:m + 1],
                                         accum_out=esum[:, i % NEE, m:m + 1]).then_inc(s_exp, 1)

            def probs_high(h, i):
                g = g_of(h, i)
                n = dtile(i)[1]
                wait(act, s_pt, g + 1)
                wait(act, s_pv, g - 1)
                nc.scalar.activation(dpT_h[i % 2][:, 0:n], turned_probs[:, 0:n], ACT.Copy).then_inc(s_pth, 1)

            def squares(h, i):
                g = g_of(h, i)
                wait(act, s_pv, g + 1)
                wait(act, s_sq, g)
                nc.scalar.activation(o_junk[:], out_bank(i), ACT.Square, scale=P ** -0.5,
                                     accum_out=osq[:, i % 2:i % 2 + 1]).then_inc(s_sq, 1)

            def normed(h, i):
                g = g_of(h, i)
                wait(act, s_or, 2 * g + 2)
                wait(act, s_ot, g - 1)
                nc.scalar.activation(o_sb[i % 2][:], out_bank(i), ACT.Copy, scale=orstd[:, i % 2:i % 2 + 1]).then_inc(s_osb, 1)

            def mix_high(h, i):
                wait(act, s_ot, g_of(h, i) + 1)
                nc.scalar.activation(mixD_h[:, h, i * P:(i + 1) * P], turned_out, ACT.Copy, scale=gsub_col[:]).then_inc(s_oth, 1)

            def head(h, first, last):
                for i in head_slots(first, last):
                    on_tile(NT, i, first, last, h, squares, -2)
                    on_tile(NT, i, first, last, h, mix_high, -4)
                    on_tile(NT, i, first, last, h, probs_high, 0)
                    on_tile(NT, i, first, last, h, exp, 3)
                    on_tile(NT, i, first, last, h, normed, -2)
                    cuts(i, last, h, (QK_HIGH, cut_qk), (V_HIGH, cut_v))
                    if last and i == NT - 2:
                        act.wait_ge(s_sc, 2 * DH * NT)
                        for u in range(4):
                            act.wait_ge(m_tq, u + 1)
                            unit_high(u // 2, u % 2, u)

            cut_qk(0, 0)
            cut_qk(0, 1)
            cut_v(0, 0)
            over(act, DH, head)

        @block.gpsimd
        def _(pool):
            for x in range(2):
                for m in range(2):
                    r = slice(64 - 64 * m, 128 - 64 * m)
                    nc.gpsimd.memset(f32(q_h[x][m][r, :]), 0.0)
                    nc.gpsimd.memset(f32(q_l[x][m][r, :]), 0.0).then_inc(s_zero, 1)

            def second(h, i):
                wait(pool, s_rec, g_of(h, i) + 1)
                e = ee[i % NEE][1][:, 0:dtile(i)[1]]
                nc.gpsimd.tensor_scalar(e, e, erec[:, i % NEE, 1:2], lam_col[:], ALU.mult, ALU.mult).then_inc(s_e2, 1)

            def rstd_of(h, i):
                wait(pool, s_sq, g_of(h, i) + 1)
                o = orstd[:, i % 2:i % 2 + 1]
                nc.gpsimd.tensor_scalar_add(o, osq[:, i % 2:i % 2 + 1], LN_EPS).then_inc(s_or, 1)
                wait(pool, s_or, 2 * g_of(h, i) + 1)
                nc.gpsimd.tensor_tensor(o, o, minus_half[:, 0:1], ALU.pow).then_inc(s_or, 1)

            def head(h, first, last):
                for i in head_slots(first, last):
                    on_tile(NT, i, first, last, h, rstd_of, -2)
                    on_tile(NT, i, first, last, h, second, 2)

            pool.wait_ge(s_zero, 4)
            stage(0, 0)
            stage(0, 1)
            over(pool, DH, head)

        @block.vector
        def _(dve):
            s_in = sem("bias_table_ready")

            def cut_q(h, x):
                t0, n, _ = SEQS[x]
                for m in range(2):
                    r = slice(64 * m, 64 * m + 64)
                    wait(dve, s_qkh, 6 * h + 3 * x + m + 2)
                    nc.vector.tensor_tensor(q_l[x][m][r, :], dqT[r, h, t0:t0 + n], f32(q_h[x][m][r, :]), ALU.subtract).then_inc(s_ql, 1)

            def cut_k(h, x):
                t0, n, _ = SEQS[x]
                wait(dve, s_qkh, 6 * h + 3 * x + 1)
                nc.vector.tensor_tensor(kk_l[x][:], dkT[:, h, t0:t0 + n], f32(kk_h[x][:]), ALU.subtract).then_inc(s_kl, 1)

            def cut_v(h, x):
                t0, _, nt = SEQS[x]
                wait(dve, s_vh, 2 * h + x + 1)
                nc.vector.tensor_tensor(vv_l[x][:], dv[:, t0 // P:t0 // P + nt, bass.ds(h * P, P)],
                                        f32(vv_h[x][:]), ALU.subtract).then_inc(s_vl, 1)

            def biased(h, i):
                x, n, _, qt = dtile(i)
                if i == 0:
                    wait(dve, s_bias, 2 * g_of(h, 0))
                    nc.vector.tensor_scalar_mul(bias_t[:], bias_t[:], 0.25).then_inc(s_in, 1)
                    wait(dve, s_in, h + 1)
                wait(dve, s_p, g_of(h, i) - NEE + 1)
                for m in range(2):
                    wait(dve, s_sc, 2 * g_of(h, i) + m + 1)
                    dve.sem_inc(s_passed, 1)
                    lo = SEQ_P - P - qt * P
                    nc.vector.tensor_tensor_reduce(out=ee[i % NEE][m][:, 0:n], in0=psum[2 * (i % 2) + m][:, 0:n],
                                                   in1=bias_t[:, lo:lo + n], scale=-1.0, scalar=3.0e38, op0=ALU.add,
                                                   op1=ALU.min, accum_out=negmax[:, i % NEE, m:m + 1]).then_inc(s_bias, 1)

            def reciprocals(h, i):
                g = g_of(h, i)
                wait(dve, s_exp, 2 * g + 2)
                nc.vector.reciprocal(erec[:, i % NEE, :], esum[:, i % NEE, :]).then_inc(s_rec, 1)

            def probs(h, i):
                n = dtile(i)[1]
                g = g_of(h, i)
                wait(dve, s_e2, g + 1)
                wait(dve, s_pt, g - 1)
                nc.vector.scalar_tensor_tensor(out=pp[i % 2][:, 0:n], in0=ee[i % NEE][0][:, 0:n], scalar=erec[:, i % NEE, 0:1],
                                               in1=ee[i % NEE][1][:, 0:n], op0=ALU.mult, op1=ALU.subtract).then_inc(s_p, 1)

            def probs_low(h, i):
                n = dtile(i)[1]
                wait(dve, s_pth, g_of(h, i) + 1)
                nc.vector.tensor_tensor(dpT_l[i % 2][:, 0:n], turned_probs[:, 0:n], f32(dpT_h[i % 2][:, 0:n]),
                                        ALU.subtract).then_inc(s_ptl, 1)

            def mix_low(h, i):
                wait(dve, s_oth, g_of(h, i) + 1)
                ts = slice(i * P, (i + 1) * P)
                nc.vector.scalar_tensor_tensor(out=mixD_l[:, h, ts], in0=turned_out, scalar=gsub_col[:],
                                               in1=f32(mixD_h[:, h, ts]), op0=ALU.mult, op1=ALU.subtract).then_inc(s_otl, 1)

            def head(h, first, last):
                for i in head_slots(first, last):
                    on_tile(NT, i, first, last, h, biased, 3)
                    on_tile(NT, i, first, last, h, probs, 1)
                    on_tile(NT, i, first, last, h, probs_low, 0)
                    on_tile(NT, i, first, last, h, mix_low, -4)
                    on_tile(NT, i, first, last, h, reciprocals, 2)
                    cuts(i, last, h, (QK_LOW, cut_k), (QK_LOW, cut_q), (V_LOW, cut_v))
                    if last and i == NT - 1:
                        for u in range(4):
                            dve.wait_ge(m_qh, u + 1)
                            unit_low(u // 2, u % 2, u)

            for x in range(2):
                cut_k(0, x)
                cut_q(0, x)
            dve.wait_ge(s_alibi, 16)
            over(dve, DH, head)

    HW = D // 2
    wo_raw = [[at(f"wo_raw0{c}", 150 + 2 * c if c < 6 else 182 + 2 * c, [P, HW]) for c in range(KD)],
              [at(f"wo_raw1{c}", 30 + 2 * c, [P, HW]) for c in range(KD)]]
    wo_h = [at(f"wo_h{c}", 46 + 2 * c, [P, HW], FR) for c in range(KD)]
    wo_l = [at(f"wo_l{c}", 62 + 2 * c, [P, HW], FR) for c in range(KD)]
    s_wo = [sem(f"wo_landed{c}") for c in range(KD)]
    s_woh, s_wol, s_wou = sem("wo_high"), sem("wo_low"), sem("wo_chunk_used")
    WO_SLOT = 4

    def load_wo(u):
        n, c = u // KD, u % KD
        nc.sync.dma_start(wo_raw[n][c][:], w_o[0, c * P:(c + 1) * P, n * HW:(n + 1) * HW]).then_inc(s_wo[c], 16)

    def wo_high(u):
        nc.scalar.activation(wo_h[u % KD][:], wo_raw[u // KD][u % KD][:], ACT.Copy).then_inc(s_woh, 1)

    def wo_low(u):
        c = u % KD
        nc.vector.wait_ge(s_woh, u + 1)
        nc.vector.tensor_tensor(wo_l[c][:], wo_raw[u // KD][c][:], f32(wo_h[c][:]), ALU.subtract).then_inc(s_wol, 1)

    with nc.Block() as block:

        @block.sync
        def _(sp):
            for u in range(KD):
                load_wo(u)

        @block.tensor
        def _(pe):
            def turn(hp, k):
                w = 4 * hp + k
                wait(pe, m_stage, w + 1)
                wait(pe, m_ql, 2 * w)
                turn_unit(k, (4, 5))

            def scores(hp, i):
                k, x, n, _, qt = mtile(i)
                g = hp * TP + i
                if qt == 0:
                    wait(pe, m_ql, 8 * hp + 2 * k + 2)
                wait(pe, m_exp, g - NSB + 1)
                qs = slice(qt * P, (qt + 1) * P)
                out = psum[SCORE_BANKS[i % NSB]][:, 0:n]
                nc.tensor.matmul(out, mq_h[x][0:QK, qs], mk_h[x][0:QK, :], start=True, stop=False)
                nc.tensor.matmul(out, mq_l[x][0:QK, qs], mk_h[x][0:QK, :], start=False, stop=False)
                nc.tensor.matmul(out, mq_h[x][0:QK, qs], mk_l[x][0:QK, :], start=False, stop=True).then_inc(m_sc, 1)

            def turn_probs(hp, i):
                g = hp * TP + i
                wait(pe, m_p[i % 2], (TP // 2) * hp + i // 2 + 1)
                wait(pe, m_ptl, g - 1)
                for j in range(mtile(i)[3]):
                    t = nc.tensor.transpose(psum[2 + i % 2][:, j * P:(j + 1) * P], me[i % NME][:, j * P:(j + 1) * P], ident[:])
                t.then_inc(m_pt, 1)

            def product(hp, k, js):
                x = k % 2
                _, n, nk = SEQS[x]
                if js[0] == 0:
                    wait(pe, m_ptl, unit_last(hp, k) + 1)
                    wait(pe, m_vl, 2 * hp + x + 1)
                    wait(pe, m_ml, 4 * hp + k)
                for j in js:
                    for i, (a, b) in enumerate(((mv_h, pT_h), (mv_l, pT_h), (mv_h, pT_l))):
                        last = nc.tensor.matmul(psum[6][:, 0:n], a[x][:, j, :], b[x][:, j, :],
                                                start=(j == 0 and i == 0), stop=(j == nk - 1 and i == 2))
                if js[-1] == nk - 1:
                    last.then_inc(m_pv, 1)

            def pair(hp, first, last):
                for i in pair_slots(first, last):
                    on_tile(TP, i, first, last, hp, turn_probs, 0)
                    at_slot(TURN_SLOTS, i, first, last, hp, turn)
                    on_tile(TP, i, first, last, hp, scores, 4)
                    at_slot(PV_SLOTS, i, first, last, hp, product)

            over(pe, HEADS // 2, pair)

        @block.scalar
        def _(act):
            def cut_qk(hp, k):
                wait(act, m_sc, unit_last(hp, k) - NT + 1)
                for j in range(2):
                    wait(act, m_tq, 2 * (4 * hp + k) + j + 1)
                    unit_high(k, j, 4 + j)

            def cut_v(hp, x):
                t0, _, nt = SEQS[x]
                wait(act, m_pv, 4 * hp + x - 1)
                nc.scalar.activation(mv_h[x][:].rearrange("p t (h n) -> p t h n", h=2),
                                     v_tok[:, t0 // P:t0 // P + nt, bass.ds(2 * hp, 2), :], ACT.Copy).then_inc(m_vh, 1)

            def exp(hp, i):
                n = mtile(i)[2]
                g = hp * TP + i
                wait(act, m_max, g + 1)
                wait(act, m_pt, g - NME + 1)
                b = i % NSB
                nc.scalar.activation(me[i % NME][:, 0:n], psum[SCORE_BANKS[b]][:, 0:n], ACT.Exp, bias=mmax[:, b:b + 1],
                                     accum_out=msum[:, b:b + 1]).then_inc(m_exp, 1)

            def normalise(hp, i):
                if i % 2 == 1:
                    n = mtile(i)[2]
                    wait(act, m_rec, hp * TP + i + 1)
                    e = me[i % NME][:, 0:n]
                    nc.scalar.activation(e, e, ACT.Copy, scale=mrec[:, i % NSB:i % NSB + 1]).then_inc(m_p[1], 1)

            def probs_high(hp, i):
                k, x, n, nk, qt = mtile(i)
                wait(act, m_pt, hp * TP + i + 1)
                if qt == 0:
                    wait(act, m_pv, 4 * hp + k - 1)
                nc.scalar.activation(pT_h[x][:, :, qt * P:(qt + 1) * P], psum[2 + i % 2][:, 0:n].rearrange("p (j q) -> p j q", q=P),
                                     ACT.Copy).then_inc(m_pth, 1)

            def mix_high(hp, k):
                t0, n, _ = SEQS[k % 2]
                r = slice(VDIM * (k // 2), VDIM * (k // 2) + VDIM)
                wait(act, m_pv, 4 * hp + k + 1)
                nc.scalar.activation(mixM_h[r, hp, t0:t0 + n], psum[6][r, 0:n], ACT.Copy).then_inc(m_mh, 1)

            def pair(hp, first, last):
                for i in pair_slots(first, last):
                    on_tile(TP, i, first, last, hp, probs_high, 0)
                    at_slot(MIX_SLOTS, i, first, last, hp, mix_high)
                    on_tile(TP, i, first, last, hp, exp, 3)
                    on_tile(TP, i, first, last, hp, normalise, 2)
                    at_slot(TURN_SLOTS, i, first, last, hp, cut_qk)
                    at_slot(V_SLOTS, i, first, last, hp, cut_v)
                    if last and 0 <= i - WO_SLOT < KD:
                        act.wait_ge(s_wo[i - WO_SLOT], 16)
                        act.wait_ge(m_stage, 2 * HEADS)
                        act.wait_ge(m_vl, HEADS)
                        wo_high(i - WO_SLOT)

            over(act, HEADS // 2, pair)

        @block.gpsimd
        def _(pool):
            def restage(hp, k):
                wait(pool, m_tq, 2 * (4 * hp + k) - 2)
                stage(hp, k)

            def normalise(hp, i):
                if i % 2 == 0:
                    n = mtile(i)[2]
                    wait(pool, m_rec, hp * TP + i + 1)
                    e = me[i % NME][:, 0:n]
                    nc.gpsimd.tensor_scalar(e, e, mrec[:, i % NSB:i % NSB + 1], None, ALU.mult).then_inc(m_p[0], 1)

            def pair(hp, first, last):
                for i in pair_slots(first, last):
                    on_tile(TP, i, first, last, hp, normalise, 2)
                    at_slot(STAGE_SLOTS, i, first, last, hp, restage)

            restage(0, 2)
            over(pool, HEADS // 2, pair)

        @block.vector
        def _(dve):
            def cut_qk(hp, k):
                for j in range(2):
                    wait(dve, m_qh, 2 * (4 * hp + k) + j + 1)
                    unit_low(k, j, 4 + j)

            def cut_v(hp, x):
                t0, _, nt = SEQS[x]
                wait(dve, m_vh, 2 * hp + x + 1)
                nc.vector.tensor_tensor(mv_l[x][:].rearrange("p t (h n) -> p t h n", h=2),
                                        v_tok[:, t0 // P:t0 // P + nt, bass.ds(2 * hp, 2), :],
                                        f32(mv_h[x][:]).rearrange("p t (h n) -> p t h n", h=2),
                                        ALU.subtract).then_inc(m_vl, 1)

            def maximum(hp, i):
                n = mtile(i)[2]
                wait(dve, m_sc, hp * TP + i + 1)
                nc.vector.tensor_reduce(mmax[:, i % NSB:i % NSB + 1], psum[SCORE_BANKS[i % NSB]][:, 0:n], axis=AX, op=ALU.max,
                                        negate=True).then_inc(m_max, 1)

            def reciprocal(hp, i):
                g = hp * TP + i
                wait(dve, m_exp, g + 1)
                wait(dve, m_p[(i - NSB) % 2], (TP // 2) * hp + (i - NSB) // 2 + 1)
                nc.vector.reciprocal(mrec[:, i % NSB:i % NSB + 1], msum[:, i % NSB:i % NSB + 1]).then_inc(m_rec, 1)

            def probs_low(hp, i):
                k, x, n, nk, qt = mtile(i)
                wait(dve, m_pth, hp * TP + i + 1)
                qs = slice(qt * P, (qt + 1) * P)
                nc.vector.tensor_tensor(pT_l[x][:, :, qs], psum[2 + i % 2][:, 0:n].rearrange("p (j q) -> p j q", q=P),
                                        f32(pT_h[x][:, :, qs]), ALU.subtract).then_inc(m_ptl, 1)

            def mix_low(hp, k):
                t0, n, _ = SEQS[k % 2]
                r = slice(VDIM * (k // 2), VDIM * (k // 2) + VDIM)
                wait(dve, m_mh, 4 * hp + k + 1)
                nc.vector.tensor_tensor(mixM_l[r, hp, t0:t0 + n], psum[6][r, 0:n], f32(mixM_h[r, hp, t0:t0 + n]),
                                        ALU.subtract).then_inc(m_ml, 1)

            def pair(hp, first, last):
                for i in pair_slots(first, last):
                    on_tile(TP, i, first, last, hp, maximum, 3)
                    on_tile(TP, i, first, last, hp, reciprocal, 2)
                    on_tile(TP, i, first, last, hp, probs_low, 0)
                    at_slot(MIX_SLOTS, i, first, last, hp, mix_low)
                    at_slot(TURN_SLOTS, i, first, last, hp, cut_qk)
                    at_slot(V_SLOTS, i, first, last, hp, cut_v)
                    if last and 0 <= i - WO_SLOT < KD:
                        wo_low(i - WO_SLOT)

            over(dve, HEADS // 2, pair)

    ln1g_sb = at("ln1g_sb", 186, [P, D])
    ln1b_sb = at("ln1b_sb", 190, [P, D])
    ax = [at(f"ax{i}", 194 + 4 * i, [P, D]) for i in range(2)]
    x1T = at("x1T", 202, [P, KD, P])
    raw = {X: [at(f"raw{X}{i}", 78 + 16 * n + 4 * i, [P, 2 * FF]) for i in range(4)] for n, X in enumerate("GUD")}
    raw_g2 = [at(f"rawG2{i}", (70, 194, 198, 202)[i], [P, 2 * FF]) for i in range(4)]

    def raw_of(X, t, i):
        return raw_g2[i] if X == "G" and isinstance(t, int) and t == 2 else raw[X][i]

    wh_ = {X: [at(f"e{X}h{i}", kb + 4 * i, [P, 2 * FF], FR) for i in range(4)] for X, kb in (("G", 6), ("D", 38), ("U", 126))}
    wl_ = {X: [at(f"e{X}l{i}", kb + 4 * i, [P, 2 * FF], FR) for i in range(4)] for X, kb in (("G", 22), ("D", 54))}
    wl_["U"] = [at(f"eUl{i}", (142, 146, 182, 186)[i], [P, 2 * FF], FR) for i in range(4)]
    x1_rows = nc.dram_tensor("x1_rows", (TOK + P, D), F).ap()
    acc_rows = nc.dram_tensor("acc_rows", (TOK + P, D), F).ap()

    cursor = [150 * KB]

    def tmp(name, shape, dt=F):
        n = 4
        for v in shape[1:]:
            n *= v
        off = cursor[0]
        cursor[0] += (n + 31) // 32 * 32
        assert cursor[0] <= 162 * KB, name
        return nc.alloc_sbuf_tensor_at(name, list(shape), dt, offset=base + off)

    wr_sb = tmp("wr_sb", [P, KD, NE])
    br_sb = tmp("br_sb", [P, NE])
    before = tmp("before", [P, P])
    ones = tmp("ones", [P, P])
    i128 = tmp("i128", [P, P])
    i32a = tmp("i32a", [P, P], I32)
    itile = tmp("itile", [P, MAX_TILES])
    irank = tmp("irank", [P, NE])
    grank = tmp("grank", [P, NG])
    iexp = tmp("iexp", [P, NE])
    tok1 = tmp("tok1", [P, NT])
    padrow = tmp("padrow", [P, 1])
    sg = tmp("sg", [P, NT, NE])
    bs = tmp("bs", [P, NT, NE])
    g6 = [tmp(f"g6_{i}", [P, NT * NG]) for i in range(6)]
    r1 = tmp("r1", [P, NT])
    r2 = tmp("r2", [P, NT])
    mb = [tmp(f"mb{i}", [P, NT, NE]) for i in range(2)]
    t16 = tmp("t16", [P, NT, NE])
    picks = tmp("picks", [P, 2, NT, NE])
    prod = tmp("prod", [P, 2, NT, NE])
    member = tmp("member", [P, NT, NE])
    pos = tmp("pos", [P, NT, NE])
    more = tmp("more", [P, NE])
    upto = tmp("upto", [P, NE])
    cnt_i = tmp("cnt_i", [P, NE], I32)
    first_more = tmp("first_more", [P, NE])
    gate = tmp("gate", [P, 2, NT])
    place = tmp("place", [P, 2, NT])
    place_i = tmp("place_i", [P, 2, NT], I32)
    blk = tmp("blk", [P, 2, NT])
    low = tmp("low", [P, 2, NT])
    exp_of = tmp("exp_of", [P, 2, NT])
    tile_of = tmp("tile_of", [P, 2, NT])
    NH = 3
    hot = tmp("hot", [P, NH, P])
    vals = tmp("vals", [P, NH, 2, MAX_TILES])
    le = tmp("le", [1, MAX_MORE + 1, NE])
    te_f = tmp("te_f", [1, MAX_TILES])
    idx_f = tmp("idx_f", [P, MAX_TILES])
    idx_tab = small("idx_tab", [P, MAX_TILES], I32)
    gate_tab = small("gate_tab", [P, MAX_TILES])
    tile_expert = small("tile_expert", [1, MAX_TILES], I32)
    n_more_sb = small("n_more_sb", [1, 1], I32)

    s_ln1w, s_rt = sem("ln1_weights_landed"), sem("router_weights_landed")
    s_o0, s_o1, s_y0, s_y1 = sem("o_first_half"), sem("o_second_half"), sem("o_first_half_out"), sem("o_second_half_out")
    s_var1, s_rstd1, s_x1 = sem("ln1_variance"), sem("ln1_rstd"), sem("x1_ready")
    s_x1t, s_x1e, s_log = sem("x1_transposed"), sem("x1T_ready"), sem("logits")
    s_ax, s_x1st, s_stored = sem("scaled_x1"), sem("x1_stored"), [sem(f"scaled_x1_stored{i}") for i in range(2)]
    s_zrow, s_zst = sem("zero_rows"), sem("zero_rows_stored")
    s_consts = sem("router_constants")
    s_rexp, s_member, s_prefix = sem("router_exp"), sem("router_members"), sem("router_prefix")
    s_low, s_hot, s_vals, s_slots = sem("places_ready"), sem("one_hots"), sem("one_hot_values"), sem("slot_table")
    s_hi = {X: sem(f"e{X}_high") for X in "GUD"}
    s_lo = {X: sem(f"e{X}_low") for X in "GUD"}
    s_raw = {X: [sem(f"raw{X}{i}_landed") for i in range(4)] for X in "GUD"}

    def unit_src(X, e, i):
        if X == "D":
            return w_down[0, bass.ds(e, 1), i * P:(i + 1) * P, :].rearrange("a p n -> p (a n)")
        w = w_gate if X == "G" else w_up
        return w[0, bass.ds(e, 1), 2 * i * P:(2 * i + 2) * P, :].rearrange("a (c p) n -> p (a c) n", p=P)

    def unit_dst(X, i, t=0):
        dst = raw_of(X, t, i)[:]
        return dst if X == "D" else dst.rearrange("p (c n) -> p c n", c=2)

    def mix(c, hi):
        t = (mixM_h if hi else mixM_l) if c < KD // 2 else (mixD_h if hi else mixD_l)
        return t[:, c % (KD // 2), :]

    xg = at("xg", 190, [P, D])
    idx_g = small("idx_g", [P, 1], I32)
    s_idxtab, s_idxg, s_gather = sem("index_table_ready"), sem("gather_index"), sem("rows_gathered")

    def gather_rows():
        nc.gpsimd.indirect_dma_start(out=xg[:], out_offset=None, in_=x1_rows,
                                     in_offset=bass.IndirectOffsetOnAxis(ap=idx_g[:, 0:1], axis=0),
                                     bounds_check=TOK + P - 1, oob_is_err=False).then_inc(s_gather, 16)

    with nc.Block() as block:

        @block.sync
        def _(sp):
            for u in range(KD, 2 * KD):
                load_wo(u)
                if u == 2 * KD - 1:
                    sp.dma_start(ln1g_sb[:], bcast(ln1_g[0], D)).then_inc(s_ln1w, 16)
                    sp.dma_start(ln1b_sb[:], bcast(ln1_b[0], D)).then_inc(s_ln1w, 16)
                    sp.dma_start(wr_sb[:], w_router.rearrange("(c p) n -> p c n", p=P)).then_inc(s_rt, 16)
                    sp.dma_start(br_sb[:], bcast(b_router, NE)).then_inc(s_rt, 16)
                    for X in "GUD":
                        for i in range(4):
                            sp.dma_start(unit_dst(X, i), unit_src(X, 0, i)).then_inc(s_raw[X][i], 16)
            sp.wait_ge(s_zrow, 1)
            sp.dma_start(x1_rows[TOK:TOK + P, :], ax[1][:]).then_inc(s_zst, 16)
            sp.dma_start(acc_rows[TOK:TOK + P, :], ax[1][:]).then_inc(s_zst, 16)
            for t in range(NT):
                sp.wait_ge(s_x1, t + 1)
                sp.dma_start(x1_rows[t * P:(t + 1) * P, :], res[:, t, :]).then_inc(s_x1st, 16)
                sp.wait_ge(s_ax, t + 1)
                sp.dma_start(acc_rows[t * P:(t + 1) * P, :], ax[t % 2][:]).then_inc(s_stored[t % 2], 16)
            sp.wait_ge(s_zst, 32)
            for i in range(2):
                sp.wait_ge(s_stored[i], 16 * (NT // 2))
            sp.wait_ge(s_x1st, 16 * NT)
            for X in "UGD":
                if X == "D":
                    sp.wait_ge(s_o1, NT)
                    sp.wait_ge(s_log, NT)
                    for i in range(4):
                        sp.wait_ge(s_raw["G"][i], 32)
                        sp.dma_start(unit_dst("G", i, 2), unit_src("G", 2, i)).then_inc(s_raw["G"][i], 16)
                for i in range(4):
                    sp.wait_ge(s_lo[X], i + 1)
                    sp.dma_start(unit_dst(X, i), unit_src(X, 1, i)).then_inc(s_raw[X][i], 16)

        @block.tensor
        def _(pe):
            def second_half(t):
                wait(pe, s_y1, t - 1)
                ts = slice(t * P, (t + 1) * P)
                out = psum[6 + t % 2][:]
                for c in range(KD):
                    if t == 0:
                        pe.wait_ge(s_wol, KD + c + 1)
                    nc.tensor.matmul(out, mix(c, True)[:, ts], wo_h[c][:], start=(c == 0), stop=False)
                    nc.tensor.matmul(out, mix(c, False)[:, ts], wo_h[c][:], start=False, stop=False)
                    last = nc.tensor.matmul(out, mix(c, True)[:, ts], wo_l[c][:], start=False, stop=(c == KD - 1))
                last.then_inc(s_o1, 1)

            def turn_x1(t):
                pe.wait_ge(s_x1, t + 1)
                pe.wait_ge(s_y0, 2)
                wait(pe, s_x1e, 2 * t)
                for hf in range(2):
                    for j in range(4):
                        c = 4 * hf + j
                        last = nc.tensor.transpose(psum[hf][:, j * P:(j + 1) * P], res[:, t, c * P:(c + 1) * P], ident[:])
                    last.then_inc(s_x1t, 1)

            def logits(t):
                pe.wait_ge(s_x1e, 2 * t + 2)
                pe.wait_ge(s_rt, 32)
                pe.wait_ge(s_y0, 3)
                for c in range(KD):
                    last = nc.tensor.matmul(psum[2][:, t * NE:(t + 1) * NE], x1T[:, c, :], wr_sb[:, c, :],
                                            start=(c == 0), stop=(c == KD - 1))
                last.then_inc(s_log, 1)

            for c in range(KD):
                pe.wait_ge(s_wol, c + 1)
                for t in range(NT):
                    ts = slice(t * P, (t + 1) * P)
                    out = psum[t][:]
                    nc.tensor.matmul(out, mix(c, True)[:, ts], wo_h[c][:], start=(c == 0), stop=False)
                    nc.tensor.matmul(out, mix(c, False)[:, ts], wo_h[c][:], start=False, stop=False)
                    last = nc.tensor.matmul(out, mix(c, True)[:, ts], wo_l[c][:], start=False, stop=(c == KD - 1))
                    if c == KD - 1:
                        last.then_inc(s_o0, 1)
                if c < KD - 1:
                    last.then_inc(s_wou, 1)
            for t in range(NT):
                second_half(t)
                if t >= 2:
                    logits(t - 2)
                if t >= 1:
                    turn_x1(t - 1)
            logits(NT - 2)
            turn_x1(NT - 1)
            logits(NT - 1)

            pe.wait_ge(s_member, 1)
            pe.wait_ge(s_consts, 1)
            pe.wait_ge(s_y0, NT)
            m = member[:].rearrange("p t e -> p (t e)")
            nc.tensor.matmul(psum[3][:, 0:NT * NE], before[:], m, start=True, stop=False)
            for d in range(1, NT):
                nc.tensor.matmul(psum[3][:, d * NE:NT * NE], ones[:], m[:, 0:(NT - d) * NE], start=False, stop=(d == NT - 1))
            for t in range(NT):
                last = nc.tensor.matmul(psum[4][:, 0:NE], ones[:], member[:, t, :], start=(t == 0), stop=(t == NT - 1))
            last.then_inc(s_prefix, 1)
            for n in range(2 * NT):
                pe.wait_ge(s_hot, n + 1)
                pe.wait_ge(s_vals, n + 1)
                nc.tensor.matmul(psum[5][:, 0:2 * MAX_TILES], hot[:, n % NH, :], vals[:, n % NH].rearrange("p a b -> p (a b)"),
                                 start=(n == 0), stop=(n == 2 * NT - 1)).then_inc(s_slots, 1)

        @block.scalar
        def _(act):
            for u in range(KD, 2 * KD):
                c = u % KD
                act.wait_ge(s_wo[c], 32)
                if c < KD - 1:
                    act.wait_ge(s_wou, c + 1)
                else:
                    act.wait_ge(s_o0, NT)
                wo_high(u)
            act.wait_ge(s_zst, 32)
            for t in range(NT):
                act.wait_ge(s_x1, t + 1)
                if t >= 2:
                    act.wait_ge(s_stored[t % 2], 16 * (t // 2))
                for hf in range(2):
                    act.wait_ge(s_x1t, 2 * t + hf + 1)
                    wait(act, s_log, t)
                    nc.scalar.activation(x1T[:, 4 * hf:4 * hf + 4, :], psum[hf][:].rearrange("p (c n) -> p c n", c=4),
                                         ACT.Copy).then_inc(s_x1e, 1)
                nc.scalar.activation(ax[t % 2][:], res[:, t, :], ACT.Copy, scale=ALPHA).then_inc(s_ax, 1)
            act.wait_ge(s_log, NT)
            nc.scalar.activation(sg[:], psum[2][:, 0:NT * NE].rearrange("p (t e) -> p t e", t=NT), ACT.Exp,
                                 scale=-1.0).then_inc(s_rexp, 1)

            def high0(X):
                for i in range(4):
                    act.wait_ge(s_raw[X][i], 16)
                    nc.scalar.activation(wh_[X][i][:], raw[X][i][:], ACT.Copy).then_inc(s_hi[X], 1)

            act.wait_ge(s_o1, NT)
            high0("U")
            act.wait_ge(s_x1st, 16 * NT)
            act.wait_ge(s_ax, NT)
            act.wait_ge(s_x1t, 2 * NT)
            high0("G")
            high0("D")

        @block.gpsimd
        def _(pool):
            n = [0]

            def done(ins):
                n[0] += 1
                ins.then_inc(s_pool2, 1)
                pool.wait_ge(s_pool2, n[0])

            s_pool2 = sem("router_pool_step")
            nc.gpsimd.memset(ax[1][:], 0.0).then_inc(s_zrow, 1)
            done(nc.gpsimd.memset(before[:], 1.0))
            nc.gpsimd.memset(ones[:], 1.0)
            done(nc.gpsimd.affine_select(out=before[:], in_=before[:], compare_op=ALU.is_gt, fill=0.0, base=0,
                                         pattern=[[1, P]], channel_multiplier=-1))

            def counted(dst, pattern, base0, mult):
                w = 1
                for _, k in pattern:
                    w *= k
                done(nc.gpsimd.iota(i32a[:, 0:w], pattern=pattern, base=base0, channel_multiplier=mult))
                done(nc.gpsimd.tensor_copy(dst, i32a[:, 0:w]))

            counted(i128[:], [[1, P]], 0, 0)
            counted(itile[:], [[1, MAX_TILES]], 0, 0)
            counted(irank[:], [[-1, NE]], NE, 0)
            counted(grank[:], [[-1, NG]], NG, 0)
            counted(iexp[:], [[1, NE]], 0, 0)
            counted(tok1[:], [[P, NT]], 1, 1)
            counted(padrow[:], [[1, 1]], TOK + 1, 1)
            nc.gpsimd.memset(te_f[:], 0.0).then_inc(s_consts, 1)
            for t in range(NT):
                pool.wait_ge(s_var1, t + 1)
                nc.gpsimd.tensor_tensor(rstd[:, t:t + 1], mv[:, t, 1:2], minus_half[:, 0:1], ALU.pow).then_inc(s_rstd1, 1)
            def low0(X, i):
                pool.wait_ge(s_hi[X], i + 1)
                nc.gpsimd.tensor_tensor(wl_[X][i][:], raw[X][i][:], f32(wh_[X][i][:]), ALU.subtract).then_inc(s_lo[X], 1)

            for i in range(4):
                if i == 3:
                    pool.wait_ge(s_x1, NT)
                low0("U", i)
            for i in range(4):
                low0("G", i)
            pool.wait_ge(s_low, 1)
            for n in range(2 * NT):
                if n >= NH:
                    pool.wait_ge(s_slots, n - NH + 1)
                nc.gpsimd.tensor_scalar(hot[:, n % NH, :], i128[:], low[:, n // NT, n % NT:n % NT + 1], None,
                                        ALU.is_equal).then_inc(s_hot, 1)
            pool.wait_ge(s_idxtab, 1)
            nc.gpsimd.tensor_copy(idx_g[:], idx_tab[:, 0:1]).then_inc(s_idxg, 1)
            pool.wait_ge(s_idxg, 1)
            pool.wait_ge(s_x1st, 16 * NT)
            pool.wait_ge(s_zst, 32)
            gather_rows()
            low0("D", 2)
            low0("D", 3)

        @block.vector
        def _(dve):
            for u in range(KD, 2 * KD):
                wo_low(u)
            for t in range(NT):
                dve.wait_ge(s_o0, t + 1)
                nc.vector.scalar_tensor_tensor(out=res[:, t, 0:HW], in0=res[:, t, 0:HW], scalar=ALPHA, in1=psum[t][:],
                                               op0=ALU.mult, op1=ALU.add).then_inc(s_y0, 1)
            dve.wait_ge(s_ln1w, 32)
            for t in range(NT):
                dve.wait_ge(s_o1, t + 1)
                nc.vector.scalar_tensor_tensor(out=res[:, t, HW:D], in0=res[:, t, HW:D], scalar=ALPHA, in1=psum[6 + t % 2][:],
                                               op0=ALU.mult, op1=ALU.add).then_inc(s_y1, 1)
                dve.wait_ge(s_y0, t + 1)
                nc.vector.bn_stats(stats[:, t % 2, 0, :], res[:, t, 0:HW])
                dve.wait_ge(s_y1, t + 1)
                then(nc.vector.bn_stats(stats[:, t % 2, 1, :], res[:, t, HW:D]))
                then(nc.vector.bn_aggr(mv[:, t, :], stats[:, t % 2, :, :].rearrange("p a b -> p (a b)")))
                nc.vector.tensor_scalar_add(mv[:, t, 1:2], mv[:, t, 1:2], LN_EPS).then_inc(s_var1, 1)
                then(nc.vector.scalar_tensor_tensor(out=res[:, t, :], in0=res[:, t, :], scalar=mv[:, t, 0:1], in1=ln1g_sb[:],
                                                    op0=ALU.subtract, op1=ALU.mult))
                dve.wait_ge(s_rstd1, t + 1)
                nc.vector.scalar_tensor_tensor(out=res[:, t, :], in0=res[:, t, :], scalar=rstd[:, t:t + 1], in1=ln1b_sb[:],
                                               op0=ALU.mult, op1=ALU.add).then_inc(s_x1, 1)

            tt, ts = nc.vector.tensor_tensor, nc.vector.tensor_scalar
            tne = [P, NT, NE]

            dve.wait_ge(s_rexp, 1)
            dve.wait_ge(s_rt, 32)
            dve.wait_ge(s_consts, 1)
            then(nc.vector.tensor_scalar_add(sg[:], sg[:], 1.0))
            then(nc.vector.reciprocal(sg[:], sg[:]))
            then(tt(bs[:], sg[:], br_sb[:].unsqueeze(1).to_broadcast(tne), ALU.add))
            four = bs[:].rearrange("p t (g k) -> p (t g) k", k=EPG)
            a, b, c, d = (four[:, :, i] for i in range(4))
            tt(g6[0][:], a, b, ALU.max)
            tt(g6[1][:], a, b, ALU.min)
            tt(g6[2][:], c, d, ALU.max)
            then(tt(g6[3][:], c, d, ALU.min))
            tt(g6[4][:], g6[0][:], g6[2][:], ALU.max)
            tt(g6[5][:], g6[0][:], g6[2][:], ALU.min)
            then(tt(g6[1][:], g6[1][:], g6[3][:], ALU.max))
            then(tt(g6[5][:], g6[5][:], g6[1][:], ALU.max))
            then(tt(g6[0][:], g6[4][:], g6[5][:], ALU.add))

            def first_best(val, rank, work, n, out, best):
                full = [P, NT, n]
                then(nc.vector.tensor_reduce(best, val, axis=AX, op=ALU.max))
                then(tt(work, val, best.unsqueeze(2).to_broadcast(full), ALU.is_equal))
                then(tt(work, work, rank[:].unsqueeze(1).to_broadcast(full), ALU.mult))
                then(nc.vector.tensor_reduce(best, work, axis=AX, op=ALU.max))
                then(tt(out, work, best.unsqueeze(2).to_broadcast(full), ALU.is_equal))

            def by_group(t):
                return t[:].rearrange("p (t g) -> p t g", g=NG)

            first_best(by_group(g6[0]), grank, by_group(g6[1]), NG, by_group(g6[2]), r1[:])
            BIG = 1.0e30
            inside = g6[2][:].unsqueeze(2).to_broadcast([P, NT * NG, EPG])
            k4 = lambda t: t[:].rearrange("p t (g k) -> p (t g) k", k=EPG)
            then(tt(k4(mb[0]), k4(bs), inside, ALU.mult))
            then(ts(g6[3][:], g6[2][:], BIG, -BIG, ALU.mult, ALU.add))
            then(tt(k4(mb[0]), k4(mb[0]), g6[3][:].unsqueeze(2).to_broadcast([P, NT * NG, EPG]), ALU.add))
            first_best(mb[0][:], irank, t16[:], NE, picks[:, 0], r1[:])
            then(nc.vector.scalar_tensor_tensor(out=mb[1][:], in0=picks[:, 0], scalar=-BIG, in1=mb[0][:], op0=ALU.mult, op1=ALU.add))
            first_best(mb[1][:], irank, t16[:], NE, picks[:, 1], r1[:])
            tt(member[:], picks[:, 0], picks[:, 1], ALU.add).then_inc(s_member, 1)

            def pick(dst, table):
                tt(prod[:, 0], picks[:, 0], table, ALU.mult)
                then(tt(prod[:, 1], picks[:, 1], table, ALU.mult))
                then(nc.vector.tensor_reduce(dst, prod[:].rearrange("p a t e -> p (a t) e"), axis=AX, op=ALU.add))

            flat = lambda t: t[:].rearrange("p a t -> p (a t)")
            pick(flat(gate), sg[:])
            then(tt(r1[:], gate[:, 0, :], gate[:, 1, :], ALU.add))
            then(nc.vector.reciprocal(r2[:], r1[:]))
            then(tt(gate[:], gate[:], r2[:].unsqueeze(1).to_broadcast([P, 2, NT]), ALU.mult))
            pick(flat(exp_of), iexp[:].unsqueeze(1).to_broadcast(tne))
            for i in range(2):
                dve.wait_ge(s_hi["D"], i + 1)
                nc.vector.tensor_tensor(wl_["D"][i][:], raw["D"][i][:], f32(wh_["D"][i][:]), ALU.subtract).then_inc(s_lo["D"], 1)
            dve.wait_ge(s_prefix, 1)
            a = step(ts(more[:], psum[4][:, 0:NE], 1.0, -1.0, ALU.max, ALU.add))
            b = step(nc.vector.tensor_copy(pos[:], psum[3][:, 0:NT * NE].rearrange("p (t e) -> p t e", t=NT)))
            dve.wait_ge(s_dve, a)
            a = step(nc.vector.tensor_copy(cnt_i[:], more[:]))
            dve.wait_ge(s_dve, b)
            tt(prod[:, 0], picks[:, 0], pos[:], ALU.mult)
            b = step(tt(prod[:, 1], picks[:, 1], pos[:], ALU.mult))
            dve.wait_ge(s_dve, a)
            a = step(nc.vector.tensor_single_scalar(cnt_i[:], cnt_i[:], 7, op=ALU.logical_shift_right))
            dve.wait_ge(s_dve, b)
            b = step(nc.vector.tensor_reduce(flat(place), prod[:].rearrange("p a t e -> p (a t) e"), axis=AX, op=ALU.add))
            dve.wait_ge(s_dve, a)
            a = step(nc.vector.tensor_copy(more[:], cnt_i[:]))
            dve.wait_ge(s_dve, b)
            b = step(nc.vector.tensor_copy(place_i[:], place[:]))
            dve.wait_ge(s_dve, a)
            a = step(nc.vector.tensor_tensor_scan(out=upto[:], data0=ones[:, 0:NE], data1=more[:], initial=0.0,
                                                  op0=ALU.mult, op1=ALU.add))
            dve.wait_ge(s_dve, b)
            b = step(nc.vector.tensor_single_scalar(place_i[:], place_i[:], 7, op=ALU.logical_shift_right))
            dve.wait_ge(s_dve, a)
            a = step(tt(first_more[:], upto[:], more[:], ALU.subtract))
            dve.wait_ge(s_dve, b)
            b = step(nc.vector.tensor_copy(blk[:], place_i[:]))
            dve.wait_ge(s_dve, a)
            a = step(tt(first_more[:], first_more[:], iexp[:], ALU.subtract))
            dve.wait_ge(s_dve, b)
            nc.vector.scalar_tensor_tensor(out=flat(low), in0=flat(blk), scalar=-float(P), in1=flat(place), op0=ALU.mult,
                                           op1=ALU.add).then_inc(s_low, 1)
            dve.wait_ge(s_dve, a)
            then(nc.vector.tensor_scalar_add(first_more[:], first_more[:], NE - 1.0))
            pick(flat(tile_of), first_more[:].unsqueeze(1).to_broadcast(tne))
            then(tt(flat(tile_of), flat(tile_of), flat(blk), ALU.add))
            then(nc.vector.scalar_tensor_tensor(out=flat(tile_of), in0=flat(blk), scalar=0.5, in1=flat(tile_of), op0=ALU.is_gt, op1=ALU.mult))
            then(tt(flat(tile_of), flat(tile_of), flat(exp_of), ALU.add))
            for n in range(2 * NT):
                k, t = n // NT, n % NT
                if n >= NH:
                    dve.wait_ge(s_slots, n - NH + 1)
                ts(vals[:, n % NH, 0, :], itile[:], tile_of[:, k, t:t + 1], tok1[:, t:t + 1], ALU.is_equal, ALU.mult)
                ts(vals[:, n % NH, 1, :], itile[:], tile_of[:, k, t:t + 1], gate[:, k, t:t + 1], ALU.is_equal, ALU.mult).then_inc(s_vals, 1)
            dve.wait_ge(s_slots, 2 * NT)
            then(ts(idx_f[:], psum[5][:, 0:MAX_TILES], 0.0, padrow[:], ALU.is_equal, ALU.mult))
            then(tt(idx_f[:], idx_f[:], psum[5][:, 0:MAX_TILES], ALU.add))
            then(nc.vector.tensor_scalar_add(idx_f[:], idx_f[:], -1.0))
            nc.vector.tensor_copy(idx_tab[:], idx_f[:]).then_inc(s_idxtab, 1)
            then(nc.vector.tensor_copy(gate_tab[:], psum[5][:, MAX_TILES:2 * MAX_TILES]))
            then(tt(le[:], upto[0:1, :].unsqueeze(1).to_broadcast([1, MAX_MORE + 1, NE]),
                    itile[0:1, 0:MAX_MORE + 1].unsqueeze(2).to_broadcast([1, MAX_MORE + 1, NE]), ALU.is_le))
            then(nc.vector.tensor_reduce(te_f[:, NE:MAX_TILES], le[:], axis=AX, op=ALU.add))
            then(nc.vector.tensor_copy(te_f[:, 0:NE], iexp[0:1, :]))
            then(nc.vector.tensor_scalar_min(te_f[:], te_f[:], NE - 1.0))
            then(nc.vector.tensor_copy(tile_expert[:], te_f[:]))
            then(nc.vector.tensor_copy(n_more_sb[:], upto[0:1, NE - 1:NE]))

    s_ln2w = sem("ln2_weights_landed")
    ln2g_sb = at("ln2g_sb", 150, [P, D])
    ln2b_sb = at("ln2b_sb", 154, [P, D])
    gsil = at("gsil", 170, [P, FF])
    hid = at("hid", 172, [P, FF])
    hT_h = at("hT_h", 174, [P, FF], FR)
    hT_l = at("hT_l", 176, [P, FF], FR)
    yg = at("yg", 178, [P, D])
    xgT_h = at("xgT_h", 162, [P, KD, P], FR)
    xgT_l = at("xgT_l", 166, [P, KD, P], FR)
    idx_s = small("idx_s", [P, 1], I32)
    gate_col = small("gate_col", [P, 1])

    s_used = {X: sem(f"e{X}_used") for X in "GUD"}
    used0 = {"G": 0, "U": 0, "D": 4}
    s_idxs, s_gcol, s_scatter = sem("scatter_index"), sem("gate_column"), sem("rows_added")
    s_tx, s_xh, s_xl = sem("xg_transposed"), sem("xgT_high"), sem("xgT_low")
    s_silu, s_hid = sem("silu"), sem("hidden")
    s_ht, s_hh, s_hl = sem("hidden_transposed"), sem("hT_high"), sem("hT_low")
    s_yg = sem("expert_rows")

    def first_iteration(t):
        return isinstance(t, int) and t == 1

    def iterate(eng, iteration):
        count = eng.value_load(n_more_sb[0:1, 0:1], min_val=0, max_val=MAX_MORE) + NE
        iteration(1, False)
        with eng.Fori(2, count - 1) as t:
            iteration(t, False)
        iteration(count - 1, True)
        return count

    with nc.Block() as block:

        @block.sync
        def _(sp):
            def load(X, t):
                e = sp.value_load(tile_expert[0:1, bass.ds(t, 1)], min_val=0, max_val=NE - 1)
                for i in range(4):
                    sp.wait_ge(s_lo[X], 4 * t + i - 3)
                    sp.dma_start(unit_dst(X, i), unit_src(X, e, i)).then_inc(s_raw[X][i], 16)

            load("U", 2)
            for i in range(4):
                sp.wait_ge(s_raw["G"][i], 48)
                sp.wait_ge(s_lo["G"], 4 + i + 1)
                sp.dma_start(unit_dst("G", i), unit_src("G", 3, i)).then_inc(s_raw["G"][i], 16)
            load("D", 2)
            count = sp.value_load(n_more_sb[0:1, 0:1], min_val=0, max_val=MAX_MORE) + NE
            with sp.Fori(2, count - 2) as t:
                load("U", t + 1)
                load("G", t + 2)
                load("D", t + 1)
            load("U", count - 1)
            load("D", count - 1)
            sp.dma_start(ln2g_sb[:], bcast(ln2_g[0], D)).then_inc(s_ln2w, 16)
            sp.dma_start(ln2b_sb[:], bcast(ln2_b[0], D)).then_inc(s_ln2w, 16)

        @block.tensor
        def _(pe):
            def turn_x(t):
                wait(pe, s_gather, 16 * t + 16)
                wait(pe, s_xl, 2 * t)
                for hf in range(2):
                    for j in range(4):
                        c = 4 * hf + j
                        last = nc.tensor.transpose(psum[4 + hf][:, j * P:(j + 1) * P], xg[:, c * P:(c + 1) * P], ident[:])
                    last.then_inc(s_tx, 1)

            def inner(X, t, units):
                out = psum["GU".index(X)][:]
                for i in units:
                    if i == 0:
                        wait(pe, s_silu if X == "G" else s_hid, t)
                    wait(pe, s_xl, 2 * t + 1 + i // 2)
                    wait(pe, s_lo[X], 4 * t + i + 1)
                    for j in range(2):
                        c, cs = 2 * i + j, slice(j * FF, (j + 1) * FF)
                        nc.tensor.matmul(out, xgT_h[:, c, :], wh_[X][i][:, cs], start=(c == 0), stop=False)
                        nc.tensor.matmul(out, xgT_l[:, c, :], wh_[X][i][:, cs], start=False, stop=False)
                        last = nc.tensor.matmul(out, xgT_h[:, c, :], wl_[X][i][:, cs], start=False, stop=(c == KD - 1))
                    last.then_inc(s_used[X], 1)

            def turn_h(t):
                wait(pe, s_hid, t + 1)
                wait(pe, s_hl, t)
                for j in range(4):
                    last = nc.tensor.transpose(psum[6][:, j * P:(j + 1) * P], hid[:, j * P:(j + 1) * P], ident[:])
                last.then_inc(s_ht, 1)

            def down(t):
                wait(pe, s_hl, t + 1)
                wait(pe, s_yg, t)
                for c in range(4):
                    wait(pe, s_lo["D"], 4 * t + c + 1)
                    cs = slice(c * P, (c + 1) * P)
                    for n in range(2):
                        out, ns = psum[2 + n][:], slice(n * FF, (n + 1) * FF)
                        nc.tensor.matmul(out, hT_h[:, cs], wh_["D"][c][:, ns], start=(c == 0), stop=False)
                        nc.tensor.matmul(out, hT_l[:, cs], wh_["D"][c][:, ns], start=False, stop=False)
                        last = nc.tensor.matmul(out, hT_h[:, cs], wl_["D"][c][:, ns], start=False, stop=(c == 3))
                    last.then_inc(s_used["D"], 1)

            def iteration(t, last):
                inner("G", t, (0, 1))
                turn_h(t - 1)
                inner("G", t, (2, 3))
                down(t - 1)
                if not last:
                    turn_x(t + 1)
                inner("U", t, range(4))

            pe.sem_inc(s_used["D"], used0["D"])
            turn_x(0)
            inner("G", 0, range(4))
            turn_x(1)
            inner("U", 0, range(4))
            count = iterate(pe, iteration)
            turn_h(count - 1)
            down(count - 1)

        @block.scalar
        def _(act):
            def high(X, t, units=range(4)):
                for i in units:
                    wait(act, s_raw[X][i], 16 * t + 16)
                    wait(act, s_used[X], used0[X] + 4 * t + i - 3)
                    nc.scalar.activation(wh_[X][i][:], raw_of(X, t, i)[:], ACT.Copy).then_inc(s_hi[X], 1)

            def x_high(t, hf):
                wait(act, s_tx, 2 * t + hf + 1)
                wait(act, s_used["U"], 4 * t - 2 + 2 * hf)
                nc.scalar.activation(xgT_h[:, 4 * hf:4 * hf + 4, :], psum[4 + hf][:].rearrange("p (c n) -> p c n", c=4),
                                     ACT.Copy).then_inc(s_xh, 1)

            def silu(t):
                wait(act, s_used["G"], 4 * t + 4)
                wait(act, s_hid, t)
                nc.scalar.activation(gsil[:], psum[0][:], ACT.Silu).then_inc(s_silu, 1)

            def h_high(t):
                wait(act, s_ht, t + 1)
                wait(act, s_used["D"], used0["D"] + 4 * t)
                nc.scalar.activation(hT_h[:], psum[6][:], ACT.Copy).then_inc(s_hh, 1)

            def rows(t):
                wait(act, s_used["D"], used0["D"] + 4 * t + 4)
                wait(act, s_gcol, t + 1)
                wait(act, s_scatter, 16 * t)
                nc.scalar.activation(yg[:, 0:FF], psum[2][:], ACT.Copy, scale=gate_col[:])
                nc.scalar.activation(yg[:, FF:D], psum[3][:], ACT.Copy, scale=gate_col[:]).then_inc(s_yg, 1)

            def iteration(t, last):
                x_high(t, 1)
                if not first_iteration(t):
                    high("D", t - 1, (2, 3))
                h_high(t - 1)
                high("U", t)
                silu(t)
                if not last:
                    high("G", t + 1)
                rows(t - 1)
                high("D", t, (0, 1))
                if not last:
                    x_high(t + 1, 0)

            x_high(0, 0)
            x_high(0, 1)
            silu(0)
            high("G", 1)
            x_high(1, 0)
            count = iterate(act, iteration)
            high("D", count - 1, (2, 3))
            h_high(count - 1)
            rows(count - 1)

        @block.vector
        def _(dve):
            def low_part(X, t, units=range(4)):
                for i in units:
                    wait(dve, s_hi[X], 4 * t + i + 1)
                    nc.vector.tensor_tensor(wl_[X][i][:], raw_of(X, t, i)[:], f32(wh_[X][i][:]), ALU.subtract).then_inc(s_lo[X], 1)

            def x_low(t, hf):
                wait(dve, s_xh, 2 * t + hf + 1)
                hs = slice(4 * hf, 4 * hf + 4)
                nc.vector.tensor_tensor(xgT_l[:, hs, :], psum[4 + hf][:].rearrange("p (c n) -> p c n", c=4),
                                        f32(xgT_h[:, hs, :]), ALU.subtract).then_inc(s_xl, 1)

            def hidden(t):
                wait(dve, s_silu, t + 1)
                wait(dve, s_used["U"], 4 * t + 4)
                wait(dve, s_ht, t)
                nc.vector.tensor_tensor(hid[:], gsil[:], psum[1][:], ALU.mult).then_inc(s_hid, 1)

            def h_low(t):
                wait(dve, s_hh, t + 1)
                nc.vector.tensor_tensor(hT_l[:], psum[6][:], f32(hT_h[:]), ALU.subtract).then_inc(s_hl, 1)

            def iteration(t, last):
                x_low(t, 1)
                hidden(t - 1)
                if not first_iteration(t):
                    low_part("D", t - 1, (2, 3))
                h_low(t - 1)
                low_part("U", t)
                if not last:
                    low_part("G", t + 1)
                low_part("D", t, (0, 1))
                if not last:
                    x_low(t + 1, 0)

            x_low(0, 0)
            x_low(0, 1)
            low_part("G", 1)
            x_low(1, 0)
            count = iterate(dve, iteration)
            hidden(count - 1)
            low_part("D", count - 1, (2, 3))
            h_low(count - 1)

        @block.gpsimd
        def _(pool):
            def gather(t):
                wait(pool, s_gather, 16 * t)
                nc.gpsimd.tensor_copy(idx_g[:], idx_tab[:, bass.ds(t, 1)]).then_inc(s_idxg, 1)
                wait(pool, s_idxg, t + 1)
                wait(pool, s_tx, 2 * t)
                gather_rows()

            def add_rows(t):
                wait(pool, s_yg, t)
                nc.gpsimd.tensor_copy(gate_col[:], gate_tab[:, bass.ds(t, 1)]).then_inc(s_gcol, 1)
                wait(pool, s_scatter, 16 * t)
                nc.gpsimd.tensor_copy(idx_s[:], idx_tab[:, bass.ds(t, 1)]).then_inc(s_idxs, 1)
                wait(pool, s_idxs, t + 1)
                wait(pool, s_yg, t + 1)
                pool.indirect_dma_start(out=acc_rows, out_offset=bass.IndirectOffsetOnAxis(ap=idx_s[:, 0:1], axis=0),
                                        in_=yg[:], in_offset=None, bounds_check=TOK + P - 1, oob_is_err=True,
                                        compute_op=ALU.add).then_inc(s_scatter, 16)

            def iteration(t, last):
                if not last:
                    gather(t + 1)
                add_rows(t - 1)

            gather(1)
            count = iterate(pool, iteration)
            add_rows(count - 1)
            pool.wait_ge(s_scatter, 16 * count)

    s_var2, s_rstd2, s_y = sem("ln2_variance"), sem("ln2_rstd"), sem("y_ready")
    s_acc = s_x
    s_out = sem("y_stored")
    shift = small("shift", [P, NT])
    s_shift2, s_norm2, s_gain2 = sem("ln2_shift"), sem("ln2_normed"), sem("ln2_scaled")

    with nc.Block() as block:

        @block.sync
        def _(sp):
            for t in range(NT):
                sp.dma_start(res[:, t, :], acc_rows[t * P:(t + 1) * P, :]).then_inc(s_acc[t], 16)
            for t in range(NT):
                sp.wait_ge(s_y, t + 1)
                dst = y_prompt[0, t * P:(t + 1) * P, :] if t < NT_P else y_sample[0, (t - NT_P) * P:(t - NT_P + 1) * P, :]
                sp.dma_start(dst, res[:, t, :]).then_inc(s_out, 16)
            sp.wait_ge(s_out, 16 * NT)

        @block.scalar
        def _(act):
            for t in range(NT):
                act.wait_ge(s_shift2, t + 1)
                nc.scalar.activation(res[:, t, :], res[:, t, :], ACT.Identity, scale=rstd[:, t:t + 1],
                                     bias=shift[:, t:t + 1]).then_inc(s_norm2, 1)

        @block.gpsimd
        def _(pool):
            def gains(t):
                pool.wait_ge(s_norm2, t + 1)
                if t == 0:
                    pool.wait_ge(s_ln2w, 32)
                nc.gpsimd.tensor_tensor(res[:, t, :], res[:, t, :], ln2g_sb[:], ALU.mult).then_inc(s_gain2, 1)

            for t in range(NT):
                pool.wait_ge(s_var2, t + 1)
                nc.gpsimd.tensor_tensor(rstd[:, t:t + 1], mv[:, t, 1:2], minus_half[:, 0:1], ALU.pow).then_inc(s_rstd2, 1)
                pool.wait_ge(s_rstd2, t + 1)
                nc.gpsimd.tensor_scalar(shift[:, t:t + 1], mv[:, t, 0:1], rstd[:, t:t + 1], -1.0, ALU.mult,
                                        ALU.mult).then_inc(s_shift2, 1)
                if t:
                    gains(t - 1)

        @block.vector
        def _(dve):
            def biases(t):
                if t < NT - 1:
                    dve.wait_ge(s_gain2, t + 1)
                else:
                    dve.wait_ge(s_norm2, t + 1)
                    dve.wait_ge(s_ln2w, 32)
                    then(nc.vector.tensor_tensor(res[:, t, :], res[:, t, :], ln2g_sb[:], ALU.mult))
                nc.vector.tensor_tensor(res[:, t, :], res[:, t, :], ln2b_sb[:], ALU.add).then_inc(s_y, 1)

            for t in range(NT):
                dve.wait_ge(s_acc[t], 32)
                nc.vector.bn_stats(stats[:, t % 2, 0, :], res[:, t, 0:HW])
                then(nc.vector.bn_stats(stats[:, t % 2, 1, :], res[:, t, HW:D]))
                then(nc.vector.bn_aggr(mv[:, t, :], stats[:, t % 2, :, :].rearrange("p a b -> p (a b)")))
                nc.vector.tensor_scalar_add(mv[:, t, 1:2], mv[:, t, 1:2], LN_EPS).then_inc(s_var2, 1)
                if t >= 2:
                    biases(t - 2)
            biases(NT - 2)
            biases(NT - 1)


def tables():
    import numpy as np

    pos = np.concatenate([np.arange(SEQ_P), np.arange(SEQ_S)]).astype(np.float32)
    inv = (1.0 / (np.float32(10000.0) ** (np.arange(0, ROPE, 2, dtype=np.float32) / np.float32(ROPE)))).astype(np.float32)
    ang = pos[:, None] * inv[None, :]
    by_tile = lambda a: np.ascontiguousarray(a.astype(np.float32).reshape(NT, P, HALF).transpose(1, 0, 2))
    dist = -np.abs(np.arange(P)[:, None] - (np.arange(ALIBI_W)[None, :] - (SEQ_P - P))).astype(np.float32)
    return {"rope_cos": by_tile(np.cos(ang)), "rope_sin": by_tile(np.sin(ang)), "alibi": dist}


_INS = ["x_prompt", "x_sample", "ln0_g", "ln0_b", "w_in", "g_q", "g_kv", "w_uq", "w_ukv", "lam_q1", "lam_k1",
        "lam_q2", "lam_k2", "g_sub", "w_o", "ln1_g", "ln1_b", "w_router", "b_router", "w_gate", "w_up",
        "w_down", "ln2_g", "ln2_b"]


def kernel(**inputs):
    import numpy as np
    import concourse.bacc as bacc
    from concourse.bass_utils import run_bass_kernel_spmd

    nc = bacc.Bacc("TRN2", target_bir_lowering=False, num_devices=1)
    arrays, args = {}, {}
    for name, a in [(n, inputs[n]) for n in _INS] + list(tables().items()):
        arrays[f"in_{name}"] = np.ascontiguousarray(a)
        args[name] = nc.dram_tensor(f"in_{name}", arrays[f"in_{name}"].shape, F, kind="ExternalInput").ap()
    for name, n in (("y_prompt", SEQ_P), ("y_sample", SEQ_S)):
        args[name] = nc.dram_tensor(name, (1, n, D), F, kind="ExternalOutput").ap()
    encoder_trunk(nc, **args)
    r = run_bass_kernel_spmd(nc, [arrays], core_ids=[0])
    return tuple(r.results[0][name] for name in ("y_prompt", "y_sample"))
```
